# Optimizing a Trainium2 kernel written in Bass

```python
import numpy as np
import jax
import jax.numpy as jnp
from jax import lax
import jax, jax.numpy as jnp

D_MODEL = 1024
BATCH = 1
SEQ = 512
DEPTH = 1

POOL_WINDOWS = (2, 4, 8, 16)
POOL_GROUPS = len(POOL_WINDOWS)
POOL_GROUP_W = 128
POOL_W = POOL_GROUPS * POOL_GROUP_W
N_HEADS = 8
HEAD_DIM = 64
N_KV_GROUPS = 2
HEADS_PER_GROUP = N_HEADS // N_KV_GROUPS
ATTN_W = N_HEADS * HEAD_DIM
KV_W = N_KV_GROUPS * HEAD_DIM
N_KV_SLOTS = 6
N_NSA_BRANCHES = 3
CMP_BLOCK = 32
CMP_STRIDE = 16
CMP_HIDDEN = 128
SEL_BLOCK = 64
N_SELECT = 16
WINDOW = 512
QUERY_CHUNK = 16
ROPE_THETA = 500000.0
ROT_DIM = HEAD_DIM // 4
N_MERGE = 2
D_FF = 2816
CONV_WIDTH = 3
IN_W = POOL_W + ATTN_W + N_KV_SLOTS * KV_W + N_HEADS * N_NSA_BRANCHES + N_MERGE * D_MODEL
RMS_EPS = 1e-6
NEG_INF = -1e30
SEL_FORCE = 1e9


def rms_norm(x, g):
    xf = x.astype(jnp.float32)
    y = xf * lax.rsqrt(jnp.mean(xf * xf, axis=-1, keepdims=True) + RMS_EPS)
    return (y * g.astype(jnp.float32)).astype(x.dtype)

def partial_rope(x, pos):
    half = ROT_DIM // 2
    inv = ROPE_THETA ** (-(jnp.arange(half, dtype=jnp.float32) * 2.0 / ROT_DIM))
    ang = pos.astype(jnp.float32)[:, :, None, None] * inv
    cos, sin = jnp.cos(ang), jnp.sin(ang)
    xf = x.astype(jnp.float32)
    x1, x2 = xf[..., :half], xf[..., half:ROT_DIM]
    rot = jnp.concatenate([x1 * cos - x2 * sin, x2 * cos + x1 * sin], axis=-1).astype(x.dtype)
    return jnp.concatenate([rot, x[..., ROT_DIM:]], axis=-1)

def masked_softmax(s, mask, axis):
    s = jnp.where(mask, s.astype(jnp.float32), NEG_INF)
    p = jax.nn.softmax(s, axis=axis)
    return jnp.where(mask, p, 0.0)

def pooling_mixer(u, pool_w, pool_scale):
    S = u.shape[1]
    uf = u.astype(jnp.float32)
    cs = jnp.cumsum(uf, axis=1)
    count = jnp.arange(S, dtype=jnp.float32) + 1.0
    outs = []
    for gi, w in enumerate(POOL_WINDOWS):
        sl = slice(gi * POOL_GROUP_W, (gi + 1) * POOL_GROUP_W)
        c = cs[..., sl]
        lag = jnp.pad(c[:, :S - w], ((0, 0), (w, 0), (0, 0)))
        mean = (c - lag) / jnp.minimum(count, float(w))[None, :, None]
        pooled = (mean - uf[..., sl]).astype(u.dtype)
        outs.append(pooled @ pool_w[gi])
    return jnp.concatenate(outs, axis=-1) * pool_scale

def compress_blocks(kv, pe, w1, w2, idx):
    blk = kv[:, idx] + pe[None, None, :, None, :]
    hid = jax.nn.silu(jnp.einsum('bnlgd,ldh->bngh', blk, w1))
    return jnp.einsum('bngh,hd->bngd', hid, w2)

def nsa_mixer(q, k_cmp, v_cmp, k_sel, v_sel, k_win, v_win, gates, positions,
              q_norm_g, k_norm_g, cmp_pe, cmp_w1, cmp_w2):
    B, S = q.shape[0], q.shape[1]
    G, R, dh = N_KV_GROUPS, HEADS_PER_GROUP, HEAD_DIM
    scale = HEAD_DIM ** -0.5
    q = partial_rope(rms_norm(q, q_norm_g), positions)

    n_cmp = (S - CMP_BLOCK) // CMP_STRIDE + 1
    cmp_idx = np.arange(n_cmp)[:, None] * CMP_STRIDE + np.arange(CMP_BLOCK)[None, :]
    cmp_end = jnp.asarray(cmp_idx[:, -1], dtype=jnp.int32)
    kc = compress_blocks(k_cmp, cmp_pe[0], cmp_w1[0], cmp_w2[0], cmp_idx)
    vc = compress_blocks(v_cmp, cmp_pe[1], cmp_w1[1], cmp_w2[1], cmp_idx)
    kc = partial_rope(rms_norm(kc, k_norm_g[0]), positions[:, cmp_idx[:, -1]])

    n_sel = S // SEL_BLOCK
    k_top = min(N_SELECT, n_sel)
    ks = partial_rope(rms_norm(k_sel, k_norm_g[1]), positions)
    ks_blocks = ks.reshape(B, n_sel, SEL_BLOCK, G, dh).transpose(0, 3, 1, 2, 4)
    vs_blocks = v_sel.reshape(B, n_sel, SEL_BLOCK, G, dh).transpose(0, 3, 1, 2, 4)
    sel_start = np.arange(n_sel)[:, None] * SEL_BLOCK
    cmp_start = np.arange(n_cmp)[None, :] * CMP_STRIDE
    ov = np.clip(np.minimum(sel_start + SEL_BLOCK, cmp_start + CMP_BLOCK)
                 - np.maximum(sel_start, cmp_start), 0, None) / CMP_BLOCK
    overlap = jnp.asarray(ov, dtype=jnp.float32)
    gather_blocks = jax.vmap(jax.vmap(lambda blocks, i: blocks[i]))

    kw = partial_rope(rms_norm(k_win, k_norm_g[2]), positions)
    kw_pad = jnp.pad(kw, ((0, 0), (WINDOW, 0), (0, 0), (0, 0)))
    vw_pad = jnp.pad(v_win, ((0, 0), (WINDOW, 0), (0, 0), (0, 0)))

    n_chunks = S // QUERY_CHUNK
    q_ch = q.reshape(B, n_chunks, QUERY_CHUNK, G, R, dh).swapaxes(0, 1)
    g_ch = gates.reshape(B, n_chunks, QUERY_CHUNK, G, R, N_NSA_BRANCHES).swapaxes(0, 1)
    j_blk = jnp.arange(n_sel)
    tok_off = jnp.arange(SEL_BLOCK)
    win_off = jnp.arange(WINDOW + QUERY_CHUNK)

    def chunk(args):
        c, qc, gc = args
        t = c * QUERY_CHUNK + jnp.arange(QUERY_CHUNK)
        s = jnp.einsum('bqgrd,bngd->bgrqn', qc, kc) * scale
        p_cmp = masked_softmax(s, cmp_end[None, :] <= t[:, None], -1)
        o_cmp = jnp.einsum('bgrqn,bngd->bqgrd', p_cmp.astype(vc.dtype), vc)
        imp = jnp.einsum('bgrqn,jn->bgqj', p_cmp, overlap)
        cur = t // SEL_BLOCK
        forced = (j_blk[None, :] == 0) | (j_blk[None, :] == cur[:, None]) | (j_blk[None, :] == cur[:, None] - 1)
        future = j_blk[None, :] * SEL_BLOCK > t[:, None]
        imp = jnp.where(forced, SEL_FORCE, jnp.where(future, NEG_INF, imp))
        _, top = lax.top_k(imp, k_top)
        ksel = gather_blocks(ks_blocks, top)
        vsel = gather_blocks(vs_blocks, top)
        tok = top[..., None] * SEL_BLOCK + tok_off
        m_sel = (tok <= t[None, None, :, None, None])[:, :, None]
        s = jnp.einsum('bqgrd,bgqkld->bgrqkl', qc, ksel) * scale
        p = masked_softmax(s, m_sel, (-2, -1))
        o_sel = jnp.einsum('bgrqkl,bgqkld->bqgrd', p.astype(vsel.dtype), vsel)
        kwc = lax.dynamic_slice_in_dim(kw_pad, c * QUERY_CHUNK, WINDOW + QUERY_CHUNK, axis=1)
        vwc = lax.dynamic_slice_in_dim(vw_pad, c * QUERY_CHUNK, WINDOW + QUERY_CHUNK, axis=1)
        kpos = c * QUERY_CHUNK - WINDOW + win_off
        m_win = (kpos[None, :] >= 0) & (kpos[None, :] <= t[:, None]) & (t[:, None] - kpos[None, :] < WINDOW)
        s = jnp.einsum('bqgrd,bkgd->bgrqk', qc, kwc) * scale
        p = masked_softmax(s, m_win, -1)
        o_win = jnp.einsum('bgrqk,bkgd->bqgrd', p.astype(vwc.dtype), vwc)
        return gc[..., 0:1] * o_cmp + gc[..., 1:2] * o_sel + gc[..., 2:3] * o_win

    out = lax.map(chunk, (jnp.arange(n_chunks), q_ch, g_ch))
    return out.swapaxes(0, 1).reshape(B, S, ATTN_W)

def causal_dwconv(x, w, b):
    C = x.shape[-1]
    y = lax.conv_general_dilated(x, w[:, None, :].astype(x.dtype), window_strides=(1,),
                                 padding=[(CONV_WIDTH - 1, 0)],
                                 dimension_numbers=('NWC', 'WIO', 'NWC'),
                                 feature_group_count=C)
    return y + b

def first_inputs(seed: int = 0) -> dict:
    key = jax.random.key(seed)
    ks = jax.random.split(key, 20)
    f32 = jnp.float32

    def nrm(k, shape, s):
        return jax.random.normal(k, shape, f32) * s

    x = jax.random.normal(ks[0], (BATCH, SEQ, D_MODEL), f32)
    offsets = jax.random.randint(ks[1], (BATCH, 1), 0, 4096, dtype=jnp.int32)
    positions = (jnp.arange(SEQ, dtype=jnp.int32)[None, :] + offsets).astype(jnp.int32)
    return {
        "x": x,
        "positions": positions,
        "mix_norm_g": 1.0 + nrm(ks[2], (DEPTH, D_MODEL), 0.05),
        "w_in": nrm(ks[3], (DEPTH, D_MODEL, IN_W), D_MODEL ** -0.5),
        "q_norm_g": 1.0 + nrm(ks[4], (DEPTH, HEAD_DIM), 0.05),
        "k_norm_g": 1.0 + nrm(ks[5], (DEPTH, 3, HEAD_DIM), 0.05),
        "cmp_pe": nrm(ks[6], (DEPTH, 2, CMP_BLOCK, HEAD_DIM), 0.1),
        "cmp_w1": nrm(ks[7], (DEPTH, 2, CMP_BLOCK, HEAD_DIM, CMP_HIDDEN), (CMP_BLOCK * HEAD_DIM) ** -0.5),
        "cmp_w2": nrm(ks[8], (DEPTH, 2, CMP_HIDDEN, HEAD_DIM), CMP_HIDDEN ** -0.5),
        "pool_w": nrm(ks[9], (DEPTH, POOL_GROUPS, POOL_GROUP_W, POOL_GROUP_W), POOL_GROUP_W ** -0.5),
        "pool_scale": 1.0 + nrm(ks[10], (DEPTH, POOL_W), 0.1),
        "w_pool_out": nrm(ks[11], (DEPTH, POOL_W, D_MODEL), POOL_W ** -0.5),
        "w_nsa_out": nrm(ks[12], (DEPTH, ATTN_W, D_MODEL), ATTN_W ** -0.5),
        "w_out": nrm(ks[13], (DEPTH, D_MODEL, D_MODEL), D_MODEL ** -0.5),
        "ffn_norm_g": 1.0 + nrm(ks[14], (DEPTH, D_MODEL), 0.05),
        "w_up": nrm(ks[15], (DEPTH, D_MODEL, 2 * D_FF), D_MODEL ** -0.5),
        "conv_w": nrm(ks[16], (DEPTH, CONV_WIDTH, D_FF), CONV_WIDTH ** -0.5),
        "conv_b": nrm(ks[17], (DEPTH, D_FF), 0.01),
        "w_down": nrm(ks[18], (DEPTH, D_FF, D_MODEL), D_FF ** -0.5),
    }

def first_block(x, positions, mix_norm_g, w_in, q_norm_g, k_norm_g, cmp_pe, cmp_w1, cmp_w2,
              pool_w, pool_scale, w_pool_out, w_nsa_out, w_out, ffn_norm_g, w_up, conv_w,
              conv_b, w_down):
    B, S = x.shape[0], x.shape[1]
    split_at = [POOL_W, POOL_W + ATTN_W, POOL_W + ATTN_W + N_KV_SLOTS * KV_W,
                POOL_W + ATTN_W + N_KV_SLOTS * KV_W + N_HEADS * N_NSA_BRANCHES]
    for l in range(DEPTH):
        h = rms_norm(x, mix_norm_g[l])
        proj = h @ w_in[l]
        u, q, kv, nsa_g, merge_g = jnp.split(proj, split_at, axis=-1)
        q = q.reshape(B, S, N_HEADS, HEAD_DIM)
        kv = kv.reshape(B, S, N_KV_SLOTS, N_KV_GROUPS, HEAD_DIM)
        nsa_gates = jax.nn.sigmoid(nsa_g.reshape(B, S, N_HEADS, N_NSA_BRANCHES))
        gate_pool, gate_nsa = jnp.split(jax.nn.sigmoid(merge_g), N_MERGE, axis=-1)
        y_pool = pooling_mixer(u, pool_w[l], pool_scale[l]) @ w_pool_out[l]
        y_nsa = nsa_mixer(q, kv[:, :, 0], kv[:, :, 1], kv[:, :, 2], kv[:, :, 3], kv[:, :, 4], kv[:, :, 5],
                          nsa_gates, positions, q_norm_g[l], k_norm_g[l], cmp_pe[l], cmp_w1[l],
                          cmp_w2[l]) @ w_nsa_out[l]
        x = x + (gate_pool * y_pool + gate_nsa * y_nsa) @ w_out[l]
        h = rms_norm(x, ffn_norm_g[l])
        gate_pre, val = jnp.split(h @ w_up[l], 2, axis=-1)
        gate_c = causal_dwconv(gate_pre, conv_w[l], conv_b[l])
        x = x + (jax.nn.silu(gate_c) * val) @ w_down[l]
    return x


CHUNK = 64
EPS = 1e-6
GDN_HEADS = 4
GDN_DK = 128
GDN_DV = 128
GDN_CONV = 4
ATT_HEADS = 8
ATT_DH = 64
ATT_BAND = 9
REL_CLIP = 128
FFN_CONV = 3

KEY_A = GDN_HEADS * GDN_DK
VAL_A = GDN_HEADS * GDN_DV
WIDTH_B = ATT_HEADS * ATT_DH
IN_SIZES = (KEY_A, KEY_A, VAL_A, VAL_A, GDN_HEADS, GDN_HEADS,
            WIDTH_B, WIDTH_B, WIDTH_B, D_MODEL, D_MODEL)
IN_SPLITS = tuple(sum(IN_SIZES[:i + 1]) for i in range(len(IN_SIZES) - 1))
D_IN = sum(IN_SIZES)
CONV_A = 2 * KEY_A + VAL_A


def rmsnorm(x, w):
    xf = x.astype(jnp.float32)
    y = xf * lax.rsqrt(jnp.mean(xf * xf, axis=-1, keepdims=True) + EPS)
    return (y * w.astype(jnp.float32)).astype(x.dtype)

def l2norm(x):
    xf = x.astype(jnp.float32)
    return xf * lax.rsqrt(jnp.sum(xf * xf, axis=-1, keepdims=True) + EPS)

def causal_dwconv_2(x, w):
    width = w.shape[0]
    return lax.conv_general_dilated(
        x, w[:, None, :].astype(x.dtype), window_strides=(1,), padding=[(width - 1, 0)],
        dimension_numbers=('NWC', 'WIO', 'NWC'), feature_group_count=x.shape[-1])

def gated_delta_rule(q, k, v, g, beta):
    b_, t_, h_, dk = q.shape
    dv = v.shape[-1]
    n = t_ // CHUNK

    def to_chunks(a):
        return a.astype(jnp.float32).reshape(b_, n, CHUNK, h_, -1).transpose(1, 0, 3, 2, 4)

    q = to_chunks(q) * (dk ** -0.5)
    k = to_chunks(k)
    v = to_chunks(v)
    g = g.astype(jnp.float32).reshape(b_, n, CHUNK, h_).transpose(1, 0, 3, 2)
    beta = beta.astype(jnp.float32).reshape(b_, n, CHUNK, h_).transpose(1, 0, 3, 2)

    G = jnp.cumsum(g, axis=-1)
    idx = jnp.arange(CHUNK)
    strict = idx[:, None] > idx[None, :]
    incl = idx[:, None] >= idx[None, :]
    diff = G[..., :, None] - G[..., None, :]
    dec_strict = jnp.exp(jnp.where(strict, diff, -jnp.inf))
    dec_incl = jnp.exp(jnp.where(incl, diff, -jnp.inf))
    gam = jnp.exp(G)

    a_mat = beta[..., :, None] * jnp.einsum('nbhid,nbhjd->nbhij', k, k) * dec_strict
    eye = jnp.eye(CHUNK, dtype=jnp.float32)
    rhs = jnp.concatenate([(beta * gam)[..., None] * k, beta[..., None] * v], axis=-1)
    sol = lax.linalg.triangular_solve(a_mat + eye, rhs, left_side=True, lower=True)
    w_c = sol[..., :dk]
    uv_c = sol[..., dk:]
    p_c = jnp.einsum('nbhid,nbhjd->nbhij', q, k) * dec_incl
    qg_c = q * gam[..., None]
    kd_c = k * jnp.exp(G[..., -1:] - G)[..., None]
    gl_c = gam[..., -1]

    def step(s, xs):
        w_i, uv_i, p_i, qg_i, kd_i, gl_i = xs
        u = uv_i - jnp.einsum('bhid,bhde->bhie', w_i, s)
        o = jnp.einsum('bhid,bhde->bhie', qg_i, s) + jnp.einsum('bhij,bhje->bhie', p_i, u)
        s = gl_i[..., None, None] * s + jnp.einsum('bhid,bhie->bhde', kd_i, u)
        return s, o

    s0 = jnp.zeros((b_, h_, dk, dv), jnp.float32)
    _, o = lax.scan(step, s0, (w_c, uv_c, p_c, qg_c, kd_c, gl_c))
    return o.transpose(1, 0, 3, 2, 4).reshape(b_, t_, h_, dv)

def chunk_band_attention(q, k, v, rel_table):
    b_, t_, h_, dh = q.shape
    n = t_ // CHUNK
    band = ATT_BAND * CHUNK
    lead = (ATT_BAND - 1) * CHUNK
    kp = jnp.pad(k, ((0, 0), (lead, 0), (0, 0), (0, 0)))
    vp = jnp.pad(v, ((0, 0), (lead, 0), (0, 0), (0, 0)))
    r = jnp.arange(CHUNK)
    j = jnp.arange(band)
    dist = lead + r[:, None] - j[None, :]
    bias = rel_table.astype(jnp.float32)[:, jnp.clip(dist, -REL_CLIP, REL_CLIP) + REL_CLIP]
    scale = dh ** -0.5

    def one_chunk(c):
        start = c * CHUNK
        qc = lax.dynamic_slice_in_dim(q, start, CHUNK, axis=1)
        kc = lax.dynamic_slice_in_dim(kp, start, band, axis=1)
        vc = lax.dynamic_slice_in_dim(vp, start, band, axis=1)
        s = jnp.einsum('bqhd,bkhd->bhqk', qc, kc).astype(jnp.float32) * scale + bias
        valid = j >= lead - start
        s = jnp.where(valid[None, None, None, :], s, -jnp.inf)
        p = jax.nn.softmax(s, axis=-1).astype(v.dtype)
        return jnp.einsum('bhqk,bkhd->bqhd', p, vc)

    out = lax.map(one_chunk, jnp.arange(n))
    return out.transpose(1, 0, 2, 3, 4).reshape(b_, t_, h_ * dh)

def second_inputs(seed: int = 0) -> dict:
    key = jax.random.key(seed)
    ks = jax.random.split(key, 20)
    f32 = jnp.float32
    nrm = lambda k, shape, s: jax.random.normal(k, shape, f32) * s
    gain = lambda k, shape: 1.0 + 0.02 * jax.random.normal(k, shape, f32)
    dt = jnp.exp(jax.random.uniform(ks[4], (DEPTH, GDN_HEADS), f32, np.log(1e-3), np.log(1e-1)))
    return {
        "x": nrm(ks[0], (BATCH, SEQ, D_MODEL), 1.0),
        "norm_mix_w": gain(ks[1], (DEPTH, D_MODEL)),
        "w_in": nrm(ks[2], (DEPTH, D_MODEL, D_IN), D_MODEL ** -0.5),
        "conv_qkv_w": nrm(ks[3], (DEPTH, GDN_CONV, CONV_A), GDN_CONV ** -0.5),
        "a_log": jnp.log(jax.random.uniform(ks[5], (DEPTH, GDN_HEADS), f32, 1.0, 16.0)),
        "dt_bias": dt + jnp.log(-jnp.expm1(-dt)),
        "gdn_norm_w": gain(ks[6], (DEPTH, GDN_DV)),
        "w_branch_a": nrm(ks[7], (DEPTH, VAL_A, D_MODEL), VAL_A ** -0.5),
        "w_branch_b": nrm(ks[8], (DEPTH, WIDTH_B, D_MODEL), WIDTH_B ** -0.5),
        "rel_bias": nrm(ks[9], (DEPTH, ATT_HEADS, 2 * REL_CLIP + 1), 0.5),
        "w_out": nrm(ks[10], (DEPTH, D_MODEL, D_MODEL), D_MODEL ** -0.5),
        "norm_ffn_w": gain(ks[11], (DEPTH, D_MODEL)),
        "w_up": nrm(ks[12], (DEPTH, D_MODEL, 2 * D_FF), D_MODEL ** -0.5),
        "conv_ffn_w": nrm(ks[13], (DEPTH, FFN_CONV, 2 * D_FF), FFN_CONV ** -0.5),
        "conv_ffn_b": nrm(ks[14], (DEPTH, 2 * D_FF), 0.02),
        "w_down": nrm(ks[15], (DEPTH, D_FF, D_MODEL), D_FF ** -0.5),
        "norm_final_w": gain(ks[16], (D_MODEL,)),
    }

def second_block(x, norm_mix_w, w_in, conv_qkv_w, a_log, dt_bias, gdn_norm_w, w_branch_a, w_branch_b,
              rel_bias, w_out, norm_ffn_w, w_up, conv_ffn_w, conv_ffn_b, w_down, norm_final_w):
    b_, t_, _ = x.shape
    for l in range(DEPTH):
        h = rmsnorm(x, norm_mix_w[l])
        proj = h @ w_in[l]
        qa, ka, va, za, ba, aa, qb, kb, vb, ga, gb = jnp.split(proj, IN_SPLITS, axis=-1)

        qkv = jax.nn.silu(causal_dwconv_2(jnp.concatenate([qa, ka, va], axis=-1), conv_qkv_w[l]))
        qa, ka, va = jnp.split(qkv, (KEY_A, 2 * KEY_A), axis=-1)
        qa = l2norm(qa.reshape(b_, t_, GDN_HEADS, GDN_DK))
        ka = l2norm(ka.reshape(b_, t_, GDN_HEADS, GDN_DK))
        va = va.reshape(b_, t_, GDN_HEADS, GDN_DV)
        beta = jax.nn.sigmoid(ba.astype(jnp.float32))
        g = -jnp.exp(a_log[l].astype(jnp.float32)) * jax.nn.softplus(
            aa.astype(jnp.float32) + dt_bias[l].astype(jnp.float32))
        oa = gated_delta_rule(qa, ka, va, g, beta)
        za = za.reshape(b_, t_, GDN_HEADS, GDN_DV).astype(jnp.float32)
        oa = (rmsnorm(oa, gdn_norm_w[l]) * jax.nn.silu(za)).astype(x.dtype).reshape(b_, t_, VAL_A)

        ob = chunk_band_attention(qb.reshape(b_, t_, ATT_HEADS, ATT_DH),
                                  kb.reshape(b_, t_, ATT_HEADS, ATT_DH),
                                  vb.reshape(b_, t_, ATT_HEADS, ATT_DH), rel_bias[l])

        mix = jax.nn.sigmoid(ga) * (oa @ w_branch_a[l]) + jax.nn.sigmoid(gb) * (ob @ w_branch_b[l])
        x = x + mix @ w_out[l]

        h = rmsnorm(x, norm_ffn_w[l])
        u = causal_dwconv_2(h @ w_up[l], conv_ffn_w[l]) + conv_ffn_b[l]
        gate, up = jnp.split(u, 2, axis=-1)
        x = x + (jax.nn.silu(gate) * up) @ w_down[l]
    return rmsnorm(x, norm_final_w)


def setup_inputs(seed=0):
    out = dict(first_inputs(seed))
    for name, value in second_inputs(seed + 1).items():
        if name != "x":
            out[name + "_2"] = value
    return out


def reference(
    x, positions, mix_norm_g, w_in, q_norm_g, k_norm_g, cmp_pe, cmp_w1, cmp_w2, pool_w,
    pool_scale, w_pool_out, w_nsa_out, w_out, ffn_norm_g, w_up, conv_w, conv_b, w_down,
    norm_mix_w_2, w_in_2, conv_qkv_w_2, a_log_2, dt_bias_2, gdn_norm_w_2, w_branch_a_2,
    w_branch_b_2, rel_bias_2, w_out_2, norm_ffn_w_2, w_up_2, conv_ffn_w_2, conv_ffn_b_2,
    w_down_2, norm_final_w_2,
):
    x = first_block(
        x, positions, mix_norm_g, w_in, q_norm_g, k_norm_g, cmp_pe, cmp_w1, cmp_w2, pool_w,
        pool_scale, w_pool_out, w_nsa_out, w_out, ffn_norm_g, w_up, conv_w, conv_b, w_down,
    )
    return second_block(
        x, norm_mix_w_2, w_in_2, conv_qkv_w_2, a_log_2, dt_bias_2, gdn_norm_w_2, w_branch_a_2,
        w_branch_b_2, rel_bias_2, w_out_2, norm_ffn_w_2, w_up_2, conv_ffn_w_2, conv_ffn_b_2,
        w_down_2, norm_final_w_2,
    )


_drawn_inputs = setup_inputs


def setup_inputs(seed=0):
    import zlib

    import numpy as np

    out = dict(_drawn_inputs(seed))
    spreads = {}
    factors = {'q_norm_g': 8.0,
     'k_norm_g': 8.0,
     'cmp_pe': 3.353,
     'conv_b': 8.0,
     'norm_mix_w_2': 6.161,
     'gdn_norm_w_2': 8.0,
     'norm_ffn_w_2': 15.711,
     'conv_ffn_b_2': 16.729,
     'norm_final_w_2': 7.487,
     'rel_bias_2': 4.087}
    for name, (base, spread) in spreads.items():
        noise = np.random.default_rng([zlib.crc32(name.encode()), seed]).standard_normal(out[name].shape)
        drawn = base * np.exp(spread * noise) if base else spread * noise
        out[name] = jnp.asarray(drawn.astype(out[name].dtype))
    for name, factor in factors.items():
        out[name] = (out[name] * factor).astype(out[name].dtype)
    return out
```

```python
from contextlib import ExitStack

import numpy as np

import concourse.bass as bass
from concourse import mybir

F32 = mybir.dt.float32
F32R = mybir.dt.float32r
I32 = mybir.dt.int32
ALU = mybir.AluOpType
ACT = mybir.ActivationFunctionType
AXX = mybir.AxisListType.X

P = 128
T = 512
D = 1024
DK = D // P
FF = 2816
FK = FF // P
NT = T // P
NH = 8
DH = 64
GH = 4
CH = 64
NCH = T // CH
NCMP = (T - 32) // 16 + 1
NEG = -1.0e30
EPS = 1e-6
SLOT = 11 * P

STAGES = [
    ("in1", 15, 1, DK), ("mix1", DK, 3, DK), ("out1", DK, 1, DK), ("up1", FK, 2, DK), ("down1", DK, 2, FK // 2),
    ("in2c", 12, 1, DK), ("in2z", 5, 1, DK), ("in2b", 12, 1, DK), ("mix2", DK, 3, DK), ("out2", DK, 1, DK), ("up2", FK, 2, DK),
    ("down2", DK, 2, FK // 2),
]

CONST = {}
_at = 0
for _name, _n in (("ident", P), ("ones", P), ("halves", P), ("rot", P), ("causal", T), ("level", 6 * P),
                  ("decay", P), ("strict", P), ("pick", 2 * GH * P), ("cmp", NT * NCMP), ("reset", T),
                  ("count", 4 * 16), ("cmp_any", 1), ("inv", 1)):
    CONST[_name] = (_at, _n)
    _at += _n
N_CONST = _at

PARAM = {}
_at = 0
for _name, _n in (("gain", 5 * DK), ("q_gain", 1), ("k_gain", 3), ("pe", 2 * 32), ("pool_scale", 4),
                  ("conv1", FK * 4), ("conv2", 2 * FK * 4), ("conv_qkv", 12 * 4), ("gdn_gain", 1),
                  ("a_log", 1), ("dt_bias", 1)):
    PARAM[_name] = (_at, _n)
    _at += _n
N_PARAM = _at


def constants():
    c = np.zeros((P, N_CONST), np.float32)
    p = np.arange(P)[:, None]
    m = np.arange(P)[None, :]

    def put(name, value):
        at, n = CONST[name]
        c[:, at:at + n] = value

    put("ident", p == m)
    put("ones", 1.0)
    put("halves", p // DH == m // DH)
    rot = np.zeros((P, P), np.float32)
    for half in (0, DH):
        for d in range(8):
            rot[half + d + 8, half + d] = -1.0
            rot[half + d, half + d + 8] = 1.0
    put("rot", rot)
    put("causal", np.where(np.arange(T)[None, :] - (T - P) <= p, 0.0, NEG))
    lev = np.zeros((P, 6, P), np.float32)
    for s in range(6):
        w = 2 ** s
        lev[:, s] = (p // (2 * w) == m // (2 * w)) & (p // w % 2 == 0) & (m // w % 2 == 1)
    put("level", lev.reshape(P, -1))
    put("decay", np.where((p // CH == m // CH) & (m >= p), 0.0, NEG))
    put("strict", m > p)
    pick = np.zeros((P, 2 * GH, P), np.float32)
    for h in range(GH):
        pick[h, h] = 1.0
        pick[32 + h, GH + h] = 1.0
    put("pick", pick.reshape(P, -1))
    tok = (np.arange(NT)[None, :, None] * P + np.arange(P)[:, None, None])
    put("cmp", np.where(np.arange(NCMP)[None, None, :] * 16 + 31 <= tok, 0.0, NEG).reshape(P, -1))
    put("reset", np.arange(T)[None, :] % CH != 0)
    t = np.arange(16)
    put("count", np.stack([1.0 / np.minimum(t + 1, w) for w in (2, 4, 8, 16)]).reshape(1, -1))
    put("cmp_any", p >= 31)
    inv = np.zeros((P, 1), np.float32)
    freq = np.float32(500000.0) ** (-(np.arange(8, dtype=np.float32) * np.float32(2.0) / np.float32(16)))
    for half in (0, DH):
        inv[half:half + 8, 0] = freq
        inv[half + 8:half + 16, 0] = freq
    put("inv", inv)
    return c


def lin(a, b, i):
    return a + b * i if isinstance(i, int) else i * b + a


class Chunk:

    def __init__(self, first, half, i, index, loop):
        self.first, self.half, self.i, self.index, self.loop = first, half, i, index, loop
        self.slot = first % 2

    def count(self, more=0):
        return lin(self.first + more, 2 * self.half, self.i)

    def loads(self):
        return lin(16 * (self.first // 2 + 1), 16 * self.half, self.i)


def units(eng, n):
    full = n // 2
    for j in range(2):
        yield 0, j
    if full > 2:
        with eng.Fori(1, full - 1) as i:
            for j in range(2):
                yield i, j
    for u in range(2 * (full - 1), n):
        yield u // 2, u % 2


def chunk_table():
    base, at, sizes = {}, 0, []
    for name, n, per, kt in STAGES:
        base[name] = at
        sizes += [kt] * (n * per)
        at += n * per
    return base, sizes


def two_blocks(nc, t_in, out):
    BASE, SIZES = chunk_table()
    INFO = {name: (n, per, kt) for name, n, per, kt in STAGES}
    NCHUNK = len(SIZES)

    def chunk(name, i, j, q=0):
        n, per, kt = INFO[name]
        local = per * j + q
        return Chunk(BASE[name] + local, per, i, lin(local, 2 * per, i), not isinstance(i, int))

    ctx = ExitStack()
    with ctx:
        kb = 1024
        base = -(-nc.sbuf_base // 64) * 64

        def sb(name, shape, dt, at):
            return nc.alloc_sbuf_tensor_at(name, shape, dt, offset=base + int(at))

        def sem(name):
            return ctx.enter_context(nc.semaphore(name))

        at = 0
        w_raw = sb("w_raw", [P, 2, SLOT], F32, at); at += 2 * SLOT * 4
        w_hi = sb("w_hi", [P, 2, SLOT], F32R, at); at += 2 * SLOT * 4
        w_lo = sb("w_lo", [P, 2, SLOT], F32R, at); at += 2 * SLOT * 4
        X = sb("X", [P, DK, T], F32, at); at += DK * T * 4
        h_hi = sb("h_hi", [P, DK, T], F32R, at); at += DK * T * 4
        h_lo = sb("h_lo", [P, DK, T], F32R, at); at += DK * T * 4
        consts = sb("consts", [P, N_CONST], F32, at); at += -(-N_CONST * 4 // 64) * 64
        params = sb("params", [P, N_PARAM], F32, at); at += -(-N_PARAM * 4 // 64) * 64
        sq_sum = sb("sq_sum", [P, T], F32, at); at += T * 4
        rms_inv = sb("rms_inv", [P, T], F32, at); at += T * 4
        arena = at
        arena_size = (nc.sbuf_usable_end - base - arena) // 64 * 64

        def area(name, shape, dt, at_kb):
            n = 4 * int(np.prod(shape[1:]))
            assert at_kb * kb + n <= arena_size, (name, at_kb, n, arena_size)
            return sb(name, shape, dt, arena + at_kb * kb)

        def const(name, *shape):
            a, n = CONST[name]
            v = consts[:, a:a + n]
            if len(shape) == 2:
                v = v.rearrange("p (a b) -> p a b", a=shape[0])
            return v

        def param(name, a=0, n=None):
            at, size = PARAM[name]
            return params[:, at + a:at + a + (size - a if n is None else n)]

        ident, ones, halves = const("ident"), const("ones"), const("halves")

        sq_ring = area("sq_ring", [P, 2, T], F32, 97)
        hn = area("hn", [P, 2, T], F32, 101)
        rope = area("rope", [P, 2, T], F32, 84)
        angle = area("angle", [P, 3, T], F32, 62)
        pos_i = area("pos_i", [P, T], I32, 68)
        rel_row = area("rel_row", [NH, 257], F32, 70)
        rel_ext = area("rel_ext", [NH, 640], F32, 72)
        p1 = area("p1", [P, 15, T], F32, 0)
        KC, VC, VS, VW, KS, KW, GT = range(8, 15)
        cmp_w1 = area("cmp_w1", [P, 2, 32 * P], F32, 30)
        cmp_blk = area("cmp_blk", [P, 2, 32, 2, NCMP], F32, 62)
        nr_sq = area("nr_sq", [P, 2, T], F32, 62)
        nr_r = area("nr_r", [P, 2, T], F32, 66)
        nr_c = area("nr_c", [P, 2, T], F32, 70)
        nr_s = area("nr_s", [P, 2, T], F32, 74)
        v1_nat = area("v1_nat", [P, 2, NT, P], F32, 78)
        pool_w = area("pool_w", [P, 4, P], F32, 82)
        pool_pad = area("pool_pad", [P, 2, 16 + T], F32, 88)
        cmp_w2 = area("cmp_w2", [P, 2, DH], F32, 92.25)
        gate_t = area("gate_t", [P, NT, 24], F32, 92.75)
        hid = area("hid", [2 * NCMP, 2, P], F32, 93.25)
        hid_t = area("hid_t", [P, 2, 2 * NCMP], F32, 94.25)
        kc_t = area("kc_t", [P, NCMP], F32, 94.75)
        vc_nat = area("vc_nat", [NCMP, 2, DH], F32, 95)
        cmp_red = area("cmp_red", [P, 3, 4 * NT * 2], F32, 95.5)
        cmp_s = area("cmp_s", [P, 2, NT, 4, NCMP], F32, 96)
        kc_tmp = area("kc_tmp", [P, 4, NCMP], F32, 100)
        cols1 = area("cols1", [P, 12], F32, 100.5)
        pc_t = area("pc_t", [NCMP, NT * NH, P], F32, 30)
        at1_sm = area("at1_sm", [P, 2, T], F32, 62)
        at1_p = area("at1_p", [P, 3, T], F32, 66)
        at1_pt = area("at1_pt", [P, 2, T], F32, 72)
        o1_hi = area("o1_hi", [P, 4, T], F32R, 46)
        o1_lo = area("o1_lo", [P, 4, T], F32R, 54)
        yp_hi = area("yp_hi", [P, 4, T], F32R, 0)
        yp_lo = area("yp_lo", [P, 4, T], F32R, 16)
        sg1 = area("sg1", [P, 2, T], F32, 62)
        mt1 = area("mt1", [P, 3, T], F32, 66)
        mix1_hi = area("mix1_hi", [P, DK, T], F32R, 24)
        mix1_lo = area("mix1_lo", [P, DK, T], F32R, 72)
        act_hi = area("act_hi", [P, FK, T], F32R, 0)
        act_lo = area("act_lo", [P, FK, T], F32R, 44)
        t_gate = area("t_gate", [P, 2, T], F32, 88)
        t_val = area("t_val", [P, 2, T], F32, 92)
        p2a = area("p2a", [P, 17, T], F32, 0)
        cv = area("cv", [P, 2, T], F32, 74)
        l2_sq = area("l2_sq", [P, 2, T], F32, 78)
        l2_r = area("l2_r", [P, 2, T], F32, 82)
        a_t = area("a_t", [P, GH, NT, P], F32, 34)
        x_inv = area("x_inv", [P, GH, NT, P], F32, 42)
        y_inv = area("y_inv", [P, GH, NT, P], F32, 50)
        p_t = area("p_t", [P, GH, NT, P], F32, 58)
        k_dec = area("k_dec", [P, GH, NT, P], F32, 66)
        gam_row = area("gam_row", [P, T], F32, 74)
        dec = area("dec", [P, NT, P], F32, 76)
        beta_strict = area("beta_strict", [P, NT, P], F32, 78)
        b_t = area("b_t", [P, 2, NT, P], F32, 80)
        bx = area("bx", [P, 2, NT, P], F32, 84)
        state = area("state", [P, 2, GH, P], F32, 88)
        u_new = area("u_new", [P, 2, GH, P], F32, 92)
        gd_cols = area("gd_cols", [P, NT, 64], F32, 96)
        gd_neg = area("gd_neg", [P, NT, GH], F32, 97)
        gd_bg = area("gd_bg", [P, NT, GH], F32, 97.25)
        gd_kd = area("gd_kd", [P, GH, NT], F32, 97.5)
        gd_last = area("gd_last", [P, GH, NCH], F32, 97.75)
        o_red = area("o_red", [P, NT * GH], F32, 98)
        gb_rows = area("gb_rows", [64, T], F32, 99)
        gz = area("gz", [64, T], F32, 101)
        gz2 = area("gz2", [64, T], F32, 103)
        ea = area("ea", [64, 2], F32, 105)
        k_bg = p2a[:, 4:8, :].rearrange("p h (c d) -> p h c d", c=NT)
        v_b = p2a[:, 8:12, :].rearrange("p h (c d) -> p h c d", c=NT)
        w_t, uv = x_inv, a_t
        o_nat = p2a[:, 4:8, :].rearrange("p c (h d) -> p c h d", h=GH)
        o_sq = p2a[:, 8:12, :].rearrange("p c (h d) -> p c h d", h=GH)
        oa = area("oa", [P, 2, T], F32, 34)
        oa_hi = area("oa_hi", [P, 4, T], F32R, 58)
        oa_lo = area("oa_lo", [P, 4, T], F32R, 66)
        p2b = area("p2b", [P, 12, T], F32, 0)
        rel = area("rel", [P, NH, T], F32, 24)
        v2_nat = area("v2_nat", [P, NT, T], F32, 40)
        at2_sm = area("at2_sm", [P, 2, T], F32, 74)
        at2_p = area("at2_p", [P, 3, T], F32, 78)
        at2_pt = area("at2_pt", [P, 2, T], F32, 84)
        cols2 = area("cols2", [P, 12], F32, 56)
        ob_hi = area("ob_hi", [P, 4, T], F32R, 48)
        ob_lo = area("ob_lo", [P, 4, T], F32R, 88)
        sg2 = area("sg2", [P, 2, T], F32, 0)
        mt2 = area("mt2", [P, 3, T], F32, 4)
        mix2_hi = area("mix2_hi", [P, DK, T], F32R, 10)
        mix2_lo = area("mix2_lo", [P, DK, T], F32R, 26)

        banks = ctx.enter_context(nc.psum_tensor("banks", [P, 8, T], F32))
        ACC, BS, BT, BO = 0, 2, 4, 6

        def bank(n, shape=None):
            v = banks[:, n, :]
            return v.rearrange("p (a b) -> p a b", a=shape) if shape else v

        rel_dram = nc.dram_tensor("rel_scratch", (NH, 640), F32, kind="Internal").ap()

        w_loaded = [sem(f"w_loaded{s}") for s in range(2)]
        hi_ready = sem("hi_ready")
        lo_ready = sem("lo_ready")
        chunk_done = sem("chunk_done")
        first_half = [sem(f"first_half{b}") for b in (1, 2)]
        consts_in = sem("consts_in")
        x_in = [sem(f"x_in{q}") for q in range(4)]
        pos_in, rel_in, cmp_in = sem("pos_in"), sem("rel_in"), sem("cmp_in")
        rel_stored, rel_loaded = sem("rel_stored"), sem("rel_loaded")
        start_step = sem("start_step")
        sin_done = sem("sin_done")
        copied = {n: sem("copied_" + n) for n in ("in1", "in2z", "in2b")}
        x_done = sem("x_done")
        sq_done = sem("sq_done")
        sum_done = sem("sum_done")
        mean_done = sem("mean_done")
        ln_done = sem("ln_done")
        inv_done = sem("inv_done")
        hn_done = sem("hn_done")
        hh_done = sem("hh_done")
        hl_done = sem("hl_done")
        out_stored = [sem("out_stored0"), sem("out_stored1")]
        gate_sig = [sem(f"gate_sig{b}") for b in (1, 2)]
        y_pool_done = [sem(f"y_first{b}") for b in (1, 2)]
        y_nsa_done = [sem(f"y_second{b}") for b in (1, 2)]
        mixed = [sem(f"mixed{b}") for b in (1, 2)]
        mix_hh = [sem(f"mix_hh{b}") for b in (1, 2)]
        mix_hl = [sem(f"mix_hl{b}") for b in (1, 2)]
        conv_done = [sem(f"conv_done{b}") for b in (1, 2)]
        silu_done = [sem(f"silu_done{b}") for b in (1, 2)]
        gated = [sem(f"gated{b}") for b in (1, 2)]
        act_hh = [sem(f"act_hh{b}") for b in (1, 2)]
        act_hl = [sem(f"act_hl{b}") for b in (1, 2)]
        cv_done, cv_silu = sem("cv_done"), sem("cv_silu")
        n_sq, n_ms, n_ln, n_inv, n_gain = (sem("n_" + x) for x in ("sq", "ms", "ln", "inv", "gain"))
        n_rot, n_cos, n_sin, n_sum = (sem("n_" + x) for x in ("rot", "cos", "sin", "sum"))
        l_sq, l_ms, l_ln, l_inv, l_out = (sem("l_" + x) for x in ("sq", "ms", "ln", "inv", "out"))
        turned = [sem(f"turned{b}") for b in (1, 2)]
        v_copied = [sem(f"v_copied{b}") for b in (1, 2)]
        gates_ready = sem("gates_ready")
        pad_zero, blk_zero = sem("pad_zero"), sem("blk_zero")
        pooled = sem("pooled")
        pool_mul = sem("pool_mul")
        yp_h, yp_l = sem("yp_h"), sem("yp_l")
        blk_done = sem("blk_done")
        c_pe, c_act, c_dve = sem("c_pe"), sem("c_act"), sem("c_dve")
        s_pe, s_act, s_dve = sem("s_pe"), sem("s_act"), sem("s_dve")

        class Attention:

            def __init__(self, b, units_, per_tile, sm, p, pt, cols, o_hi, o_lo):
                self.units, self.per_tile = units_, per_tile
                self.sm, self.p, self.pt, self.o_hi, self.o_lo = sm, p, pt, o_hi, o_lo
                self.nbias, self.sums, self.inv = cols[:, 0:4], cols[:, 4:8], cols[:, 8:12]
                self.scored = sem(f"scored{b}")
                self.masked = sem(f"masked{b}")
                self.shifted = sem(f"shifted{b}")
                self.exped = sem(f"exped{b}")
                self.inverted = sem(f"inverted{b}")
                self.weighted = sem(f"weighted{b}")
                self.flipped = sem(f"flipped{b}")
                self.fetched = sem(f"fetched{b}")
                self.summed = sem(f"summed{b}")
                self.high = sem(f"o_high{b}")
                self.low = sem(f"o_low{b}")

        att1 = Attention(1, [(j, i, b, half) for j in range(4) for i in range(NT) for b in range(2)
                             for half in range(2)], 4 * NT, at1_sm, at1_p, at1_pt, cols1, o1_hi, o1_lo)
        att2 = Attention(2, [(j, i, 0, half) for j in range(4) for i in range(NT) for half in range(2)],
                         2 * NT, at2_sm, at2_p, at2_pt, cols2, ob_hi, ob_lo)
        d_pe, d_dve, d_act = sem("d_pe"), sem("d_dve"), sem("d_act")
        g_pe, g_dve, g_act = sem("g_pe"), sem("g_dve"), sem("g_act")
        i_mask, i_bx, i_cp, i_pe, i_x, i_y = (sem("i_" + x) for x in ("mask", "bx", "cp", "pe", "x", "y"))
        r_w, r_cp, r_ws, r_u, r_ds, r_s, r_o, r_ocp = (
            sem("r_" + x) for x in ("w", "cp", "ws", "u", "ds", "s", "o", "ocp"))
        f_dve, f_act, f_pe = sem("f_dve"), sem("f_act"), sem("f_pe")
        oa_h, oa_l = sem("oa_h"), sem("oa_l")

        block = ctx.enter_context(nc.Block())

        def rows(half):
            return slice(half * DH, (half + 1) * DH)

        def ahead(c, q_kt):
            if c.loop:
                return Chunk(c.first + 2, c.half, c.i, None, True), q_kt
            n = c.count() + 2
            return (Chunk(n, 0, 0, None, False), SIZES[n]) if n < NCHUNK else (None, 0)

        def wait(eng, s, value):
            if not isinstance(value, int) or value > 0:
                eng.wait_ge(s, value)

        @block.sync
        def _(sp):
            for q in range(4):
                sp.dma_start(X[:, 2 * q:2 * q + 2, :], t_in["x"][:, 2 * q:2 * q + 2, :]).then_inc(x_in[q], 16)
            for name, n, per, kt in STAGES:
                for i, j in units(sp, n):
                    for q in range(per):
                        c = chunk(name, i, j, q)
                        wait(sp, lo_ready, c.count(-1))
                        sp.dma_start(w_raw[:, c.slot, 0:kt * P], t_in["w_" + name][c.index])\
                            .then_inc(w_loaded[c.slot], 16)
            for m in range(DK):
                sp.wait_ge(hn_done, 4 * DK + m + 1)
                sp.dma_start(out[:, m, :], hn[:, m % 2, :]).then_inc(out_stored[m % 2], 16)
            sp.wait_ge(out_stored[0], 16 * DK // 2)
            sp.wait_ge(out_stored[1], 16 * DK // 2)

        @block.gpsimd
        def _(pool):
            def low(c, kt):
                pool.wait_ge(hi_ready, c.count(1))
                pool.tensor_tensor(w_lo[:, c.slot, 0:kt * P], w_raw[:, c.slot, 0:kt * P],
                                   w_hi[:, c.slot, 0:kt * P], ALU.subtract).then_inc(lo_ready, 1)

            def split(name):
                n, per, kt = INFO[name]
                for i, j in units(pool, n):
                    for q in range(per):
                        c2, kt2 = ahead(chunk(name, i, j, q), kt)
                        if c2:
                            low(c2, kt2)

            step = [0]

            def pool_step(ins):
                step[0] += 1
                ins.then_inc(pooled, 1)
                pool.wait_ge(pooled, step[0])

            def pooling(gi):
                w, cur, u = 2 ** (gi + 1), 0, p1[:, gi, :]
                pool_step(pool.tensor_copy(pool_pad[:, 0, 16:], u))
                d = 1
                while d < w:
                    pool_step(pool.tensor_tensor(pool_pad[:, 1 - cur, 16:], pool_pad[:, cur, 16:],
                                                 pool_pad[:, cur, 16 - d:16 + T - d], ALU.add))
                    cur, d = 1 - cur, 2 * d
                s, m = pool_pad[:, cur, :], pool_pad[:, 1 - cur, :]
                pool_step(pool.tensor_scalar(m[:, 32:], s[:, 32:], 1.0 / w, None, ALU.mult))
                pool_step(pool.tensor_tensor(m[:, 16:32], s[:, 16:32], const("count", 4, 16)[:, gi, :], ALU.mult))
                pool_step(pool.tensor_tensor(u, m[:, 16:], u, ALU.subtract))

            def weights(a, gated_):
                for u, (j, i, b, half) in enumerate(a.units):
                    w = (i + 1) * P
                    pr = a.p[:, u % 3, 0:w]
                    pool.wait_ge(a.inverted, u + 1)
                    if gated_:
                        g = (j + 4 * half) * 3 + 1 + b
                        ins = pool.tensor_scalar(pr, pr, a.inv[:, u % 4:u % 4 + 1], gate_t[:, i, g:g + 1],
                                                 ALU.mult, ALU.mult)
                    else:
                        ins = pool.tensor_scalar(pr, pr, a.inv[:, u % 4:u % 4 + 1], None, ALU.mult)
                    ins.then_inc(a.weighted, 1)

            low(Chunk(0, 0, 0, None, False), DK)
            low(Chunk(1, 0, 0, None, False), DK)
            split("in1")
            pool.wait_ge(copied["in1"], 15)
            pool.wait_ge(consts_in, 32)
            pool.memset(pool_pad[:, :, 0:16], 0.0).then_inc(pad_zero, 1)
            pool.wait_ge(pad_zero, 1)
            pooling(0)
            pooling(1)
            pool.wait_ge(n_sum, 6)
            pool.memset(cmp_blk[:, :, :, :, :], 0.0).then_inc(blk_zero, 1)
            pooling(2)
            pooling(3)
            weights(att1, True)
            for name in ("mix1", "out1", "up1", "down1", "in2c", "in2z"):
                split(name)
            pool.wait_ge(copied["in2z"], 5)
            pool.memset(gb_rows[:, :], 0.0).then_inc(blk_zero, 1)
            split("in2b")
            pool.wait_ge(rel_loaded, 16 * NH)
            pool.memset(rel[0:CH, :, 0:CH], NEG).then_inc(blk_zero, 1)
            weights(att2, False)
            for name in ("mix2", "out2", "up2", "down2"):
                split(name)

        @block.scalar
        def _(act):
            def high(c, kt):
                act.wait_ge(w_loaded[c.slot], c.loads())
                wait(act, chunk_done, c.count(-1))
                act.activation(w_hi[:, c.slot, 0:kt * P], w_raw[:, c.slot, 0:kt * P], ACT.Copy)\
                    .then_inc(hi_ready, 1)

            def next_high(name, i, j, q=0):
                c2, kt2 = ahead(chunk(name, i, j, q), INFO[name][2])
                if c2:
                    high(c2, kt2)

            def plain(name):
                for i, j in units(act, INFO[name][0]):
                    next_high(name, i, j)

            def norm(n):
                act.wait_ge(mean_done, n + 1)
                act.activation(rms_inv[:, :], bank(BS), ACT.Ln, bias=EPS, scale=1.0 / D).then_inc(ln_done, 1)
                act.wait_ge(ln_done, n + 1)
                act.activation(rms_inv[:, :], rms_inv[:, :], ACT.Exp, scale=-0.5).then_inc(inv_done, 1)
                if n < 4:
                    for m in range(DK):
                        act.wait_ge(hn_done, DK * n + m + 1)
                        act.activation(h_hi[:, m, :], hn[:, m % 2, :], ACT.Copy).then_inc(hh_done, 1)

            def residual(name, n):
                for i, j in units(act, DK):
                    for q in range(INFO[name][1]):
                        next_high(name, i, j, q)
                    act.wait_ge(x_done, lin(DK * (n - 1) + j + 1, 2, i))
                    wait(act, sum_done, lin(DK * n + j - 1, 2, i))
                    act.activation(sq_ring[:, j, :], X[:, lin(j, 2, i), :], ACT.Square).then_inc(sq_done, 1)

            def merge(name, b, sg, mt, mix_hi):
                for i, j in units(act, DK):
                    m = lin(j, 2, i)
                    for q, used in ((0, y_pool_done), (1, y_nsa_done)):
                        next_high(name, i, j, q)
                        act.wait_ge(chunk_done, chunk(name, i, j, q).count(1))
                        wait(act, used[b], m)
                        act.activation(sg[:, q, :], bank(ACC + q), ACT.Sigmoid).then_inc(gate_sig[b], 1)
                    next_high(name, i, j, 2)
                    act.wait_ge(mixed[b], lin(j + 1, 2, i))
                    act.activation(mix_hi[:, m, :], mt[:, 2, :], ACT.Copy).then_inc(mix_hh[b], 1)

            def ffn(name, b, steps):
                for i, j in units(act, FK):
                    next_high(name, i, j, 0)
                    act.wait_ge(conv_done[b], lin(steps * j + 3, 2 * steps, i))
                    act.activation(t_gate[:, j, :], t_gate[:, j, :], ACT.Silu).then_inc(silu_done[b], 1)
                    next_high(name, i, j, 1)
                    act.wait_ge(gated[b], lin(j + 1, 2, i))
                    act.activation(act_hi[:, lin(j, 2, i), :], t_gate[:, j, :], ACT.Copy).then_inc(act_hh[b], 1)

            def inverse_roots(tiles, sq, rt, s_sq, s_ms, s_ln, s_inv, s_used, scale):
                def square(n):
                    wait(act, s_ms, n - 1)
                    act.activation(sq[:, n % 2, :], tiles[n], ACT.Square).then_inc(s_sq, 1)
                square(0)
                square(1)
                for n in range(len(tiles)):
                    act.wait_ge(s_ms, n + 1)
                    wait(act, s_used, n - 1)
                    act.activation(rt[:, n % 2, :], bank(BS + n % 2), ACT.Ln, bias=EPS, scale=scale)\
                        .then_inc(s_ln, 1)
                    act.wait_ge(s_ln, n + 1)
                    act.activation(rt[:, n % 2, :], rt[:, n % 2, :], ACT.Exp, scale=-0.5).then_inc(s_inv, 1)
                    if n + 2 < len(tiles):
                        square(n + 2)

            def attention(a):
                n = len(a.units)
                for s in range(n + 5):
                    if s < n:
                        w = (a.units[s][1] + 1) * P
                        act.wait_ge(a.shifted, s + 1)
                        wait(act, a.flipped, s - 2)
                        act.activation(a.p[:, s % 3, 0:w], a.sm[:, s % 2, 0:w], ACT.Exp,
                                       bias=a.nbias[:, s % 4:s % 4 + 1], scale=DH ** -0.5,
                                       accum_out=a.sums[:, s % 4:s % 4 + 1]).then_inc(a.exped, 1)
                    u = s - 2
                    if 0 <= u < n:
                        w = (a.units[u][1] + 1) * P
                        act.wait_ge(a.flipped, u + 1)
                        wait(act, a.summed, u - 1)
                        act.activation(a.pt[:, u % 2, 0:w], banks[:, BT + u % 2, 0:w], ACT.Copy)\
                            .then_inc(a.fetched, 1)
                    u = s - 4
                    if 0 <= u < n and u % a.per_tile == a.per_tile - 1:
                        j = u // a.per_tile
                        act.wait_ge(a.summed, u + 1)
                        act.activation(a.o_hi[:, j, :], bank(BO + j % 2), ACT.Copy).then_inc(a.high, 1)

            act.dma_start(consts[:, :], t_in["consts"]).then_inc(consts_in, 16)
            act.dma_start(params[:, :], t_in["params"]).then_inc(consts_in, 16)
            act.dma_start(pos_i[:, :], t_in["positions"].partition_broadcast(P)).then_inc(pos_in, 16)
            act.dma_start(rel_row[:, :], t_in["rel"]).then_inc(rel_in, 16)
            act.dma_start(cmp_w2[:, :, :], t_in["cmp_w2"]).then_inc(cmp_in, 16)
            act.dma_start(pool_w[:, :, :], t_in["pool_w"]).then_inc(cmp_in, 16)
            for half in range(2):
                act.dma_start(cmp_w1[rows(half), :, :], t_in["cmp_w1"]).then_inc(cmp_in, 16)
            act.wait_ge(start_step, 9)
            act.activation(rope[:, 1, :], angle[:, 1, :], ACT.Sin).then_inc(sin_done, 1)
            act.activation(rope[:, 0, :], angle[:, 2, :], ACT.Sin).then_inc(sin_done, 1)
            act.wait_ge(start_step, 11)
            act.dma_start(rel_dram, rel_ext[:, :]).then_inc(rel_stored, 16)
            for m in range(DK):
                act.wait_ge(x_in[m // 2], 16)
                wait(act, sum_done, m - 1)
                act.activation(sq_ring[:, m % 2, :], X[:, m, :], ACT.Square).then_inc(sq_done, 1)
            high(Chunk(0, 0, 0, None, False), DK)
            high(Chunk(1, 0, 0, None, False), DK)
            norm(0)
            plain("in1")

            act.wait_ge(copied["in1"], 15)
            act.activation(p1[0:24, GT, :], p1[0:24, GT, :], ACT.Sigmoid).then_inc(gates_ready, 1)
            inverse_roots([p1[:, t, :] for t in (4, 5, 6, 7, KS, KW)], nr_sq, nr_r, n_sq, n_ms, n_ln, n_inv,
                          n_gain, 1.0 / DH)
            for v in range(2):
                act.wait_ge(turned[0], v + 1)
                act.activation(v1_nat[:, v, :, :], bank(BO + v, NT), ACT.Copy).then_inc(v_copied[0], 1)
            act.wait_ge(turned[0], 3)
            act.activation(gate_t[:, :, :], banks[:, ACC, 0:NT * 24].rearrange("p (a b) -> p a b", a=NT),
                           ACT.Copy).then_inc(v_copied[0], 1)
            for c in range(2):
                act.wait_ge(c_pe, c + 1)
                act.activation(hid[:, c, :], banks[0:2 * NCMP, BS + c, 0:P], ACT.Silu).then_inc(c_act, 1)
            for c in range(2):
                act.wait_ge(c_pe, c + 3)
                act.activation(hid_t[:, c, :], banks[:, BT + c, 0:2 * NCMP], ACT.Copy).then_inc(c_act, 1)
            act.wait_ge(c_pe, 5)
            act.activation(kc_tmp[:, 0, :], banks[:, BO, 0:NCMP], ACT.Square).then_inc(c_act, 1)
            act.wait_ge(c_pe, 6)
            act.activation(vc_nat[:, :, :], banks[0:NCMP, BO + 1, 0:2 * DH].rearrange("p (a b) -> p a b", a=2),
                           ACT.Copy).then_inc(c_act, 1)
            act.wait_ge(c_pe, 7)
            act.activation(kc_tmp[:, 1, :], banks[:, BS, 0:NCMP], ACT.Ln, bias=EPS, scale=1.0 / DH)\
                .then_inc(c_act, 1)
            act.wait_ge(c_act, 7)
            act.activation(kc_tmp[:, 1, :], kc_tmp[:, 1, :], ACT.Exp, scale=-0.5).then_inc(c_act, 1)
            for gi in range(4):
                act.wait_ge(pool_mul, gi + 1)
                act.activation(yp_hi[:, gi, :], bank(ACC + gi % 2), ACT.Copy, scale=param("pool_scale", gi, 1))\
                    .then_inc(yp_h, 1)
            act.wait_ge(s_dve, 4)
            act.activation(cmp_s[:, :, :, :, :], cmp_s[:, :, :, :, :], ACT.Exp, scale=DH ** -0.5).then_inc(s_act, 1)
            for r in range(8):
                act.wait_ge(s_pe, 3 + r)
                act.activation(pc_t[:, 4 * r:4 * r + 4, :], banks[0:NCMP, BT + r % 2, :].rearrange(
                    "p (a b) -> p a b", a=4), ACT.Copy).then_inc(s_act, 1)
            attention(att1)
            merge("mix1", 0, sg1, mt1, mix1_hi)
            residual("out1", 1)
            norm(1)
            ffn("up1", 0, 3)
            residual("down1", 2)

            norm(2)
            for i, j in units(act, 12):
                next_high("in2c", i, j)
                act.wait_ge(cv_done, lin(4 * j + 4, 8, i))
                act.activation(p2a[:, lin(j, 2, i), :], cv[:, j, :], ACT.Silu).then_inc(cv_silu, 1)
            plain("in2z")
            inverse_roots([p2a[:, t, :] for t in range(8)], l2_sq, l2_r, l_sq, l_ms, l_ln, l_inv, l_out, 1.0)
            g = slice(32, 32 + GH)
            act.wait_ge(g_dve, 2)
            act.activation(gz2[g, :], gz2[g, :], ACT.Exp, scale=-1.0).then_inc(g_act, 1)
            act.wait_ge(g_act, 1)
            act.activation(gz2[g, :], gz2[g, :], ACT.Ln, bias=1.0).then_inc(g_act, 1)
            act.activation(ea[g, 0:1], params[g, PARAM["a_log"][0]:PARAM["a_log"][0] + 1], ACT.Exp)\
                .then_inc(g_act, 1)
            act.wait_ge(blk_zero, 2)
            act.activation(gb_rows[0:GH, :], p2a[0:GH, 16, :], ACT.Sigmoid).then_inc(g_act, 1)
            act.wait_ge(g_pe, 1)
            act.activation(gd_cols[:, :, :], banks[:, BO, 0:NT * 64].rearrange("p (a b) -> p a b", a=NT),
                           ACT.Copy).then_inc(g_act, 1)
            act.wait_ge(g_act, 5)
            act.activation(gd_bg[:, :, :], gd_cols[:, :, 32:32 + GH], ACT.Exp).then_inc(g_act, 1)
            act.wait_ge(g_dve, 7)
            for h in range(GH):
                act.wait_ge(d_pe, 6 * h + 1)
                wait(act, d_dve, 11 * (h - 1) + 5 if h else 0)
                wait(act, d_act, 7 * h)
                act.activation(gam_row[:, :], bank(BS), ACT.Exp).then_inc(d_act, 1)
                act.wait_ge(d_dve, 11 * h + 1)
                for p in range(NT):
                    act.activation(dec[:, p, :], dec[:, p, :], ACT.Exp, bias=gd_neg[:, p, h:h + 1])\
                        .then_inc(d_act, 1)
                act.wait_ge(d_dve, 11 * h + 3)
                act.activation(gd_kd[:, h, :], gd_kd[:, h, :], ACT.Exp).then_inc(d_act, 1)
                act.wait_ge(d_act, 7 * h + 1)
                act.activation(gd_last[:, h, :], gam_row[:, CH - 1:T:CH], ACT.Copy).then_inc(d_act, 1)
            for k in range(5 * GH):
                act.wait_ge(i_bx, GH + k + 1)
                wait(act, i_pe, 2 * (k - 1))
                act.activation(bx[:, k % 2, :, :], bank(BT + k % 2, NT), ACT.Copy).then_inc(i_cp, 1)
            for h in range(GH):
                act.wait_ge(r_w, 2 * h + 1)
                act.activation(w_t[:, h, :, :], bank(BT + h % 2, NT), ACT.Copy).then_inc(r_cp, 1)
                act.wait_ge(r_w, 2 * h + 2)
                act.activation(uv[:, h, :, :], bank(BO + h % 2, NT), ACT.Copy).then_inc(r_cp, 1)
            act.activation(p2a[:, 12:16, :], p2a[:, 12:16, :], ACT.Silu).then_inc(f_act, 1)
            for p in range(NT):
                act.wait_ge(r_o, 2 * p + 2)
                act.activation(o_nat[:, p, :, :], bank(BO + p % 2, GH), ACT.Copy).then_inc(r_ocp, 1)
            act.wait_ge(r_ocp, NT)
            act.activation(o_sq, o_nat, ACT.Square).then_inc(f_act, 1)
            act.wait_ge(f_dve, 1)
            act.activation(o_red[:, :], o_red[:, :], ACT.Ln, bias=EPS, scale=1.0 / P).then_inc(f_act, 1)
            act.wait_ge(f_act, 3)
            act.activation(o_red[:, :], o_red[:, :], ACT.Exp, scale=-0.5).then_inc(f_act, 1)
            for h in range(GH):
                act.wait_ge(f_dve, 3 + h)
                act.activation(oa_hi[:, h, :], oa[:, h % 2, :], ACT.Copy).then_inc(oa_h, 1)
            act.wait_ge(rel_stored, 16)
            act.wait_ge(oa_l, GH)
            for h in range(NH):
                act.dma_start(rel[:, h, :], diagonals(rel_dram, h)).then_inc(rel_loaded, 16)
            plain("in2b")
            for v in range(4):
                act.wait_ge(turned[1], v + 1)
                act.activation(v2_nat[:, :, v * P:(v + 1) * P], bank(BO + v % 2, NT), ACT.Copy)\
                    .then_inc(v_copied[1], 1)
            attention(att2)
            merge("mix2", 1, sg2, mt2, mix2_hi)
            residual("out2", 3)
            norm(3)
            ffn("up2", 1, 6)
            residual("down2", 4)
            norm(4)

        @block.vector
        def _(dve):
            def sub(out_, a, b):
                return dve.tensor_tensor(out_, a, b, ALU.subtract)

            def norm(n):
                dve.wait_ge(inv_done, n + 1)

                def low(m):
                    dve.wait_ge(hh_done, DK * n + m + 1)
                    sub(h_lo[:, m, :], hn[:, m % 2, :], h_hi[:, m, :]).then_inc(hl_done, 1)

                for m in range(DK):
                    if n < 4:
                        wait(dve, hl_done, DK * n + m - 1)
                    elif m >= 2:
                        dve.wait_ge(out_stored[m % 2], 16 * (m // 2))
                    dve.scalar_tensor_tensor(hn[:, m % 2, :], X[:, m, :], param("gain", DK * n + m, 1),
                                             rms_inv[:, :], ALU.mult, ALU.mult).then_inc(hn_done, 1)
                    if n < 4 and m:
                        low(m - 1)
                if n < 4:
                    low(DK - 1)

            def add_square(n, m, first):
                dve.wait_ge(sq_done, lin(DK * n + 1, 1, m) if isinstance(m, int) else m + (DK * n + 1))
                if first:
                    dve.tensor_copy(sq_sum[:, :], sq_ring[:, 0, :]).then_inc(sum_done, 1)

            def residual(name, n):
                per = INFO[name][1]
                for i, j in units(dve, DK):
                    m = lin(j, 2, i)
                    dve.wait_ge(chunk_done, chunk(name, i, j, per - 1).count(1))
                    dve.tensor_tensor(X[:, m, :], X[:, m, :], bank(ACC + j), ALU.add).then_inc(x_done, 1)
                    dve.wait_ge(sq_done, lin(DK * n + j + 1, 2, i))
                    if isinstance(i, int) and m == 0:
                        dve.tensor_copy(sq_sum[:, :], sq_ring[:, j, :]).then_inc(sum_done, 1)
                    else:
                        dve.wait_ge(sum_done, lin(DK * n + j, 2, i))
                        dve.tensor_tensor(sq_sum[:, :], sq_sum[:, :], sq_ring[:, j, :], ALU.add)\
                            .then_inc(sum_done, 1)

            def copy_tiles(name, dst):
                for i, j in units(dve, INFO[name][0]):
                    dve.wait_ge(chunk_done, chunk(name, i, j).count(1))
                    dve.tensor_copy(dst[:, lin(j, 2, i), :], bank(ACC + j)).then_inc(copied[name], 1)

            def merge(name, b, sg, mt, mix_hi, mix_lo):
                for i, j in units(dve, DK):
                    m = lin(j, 2, i)
                    dve.wait_ge(gate_sig[b], lin(2 * j + 1, 4, i))
                    dve.wait_ge(first_half[b], lin(j + 1, 2, i))
                    wait(dve, mixed[b], m)
                    dve.tensor_tensor(mt[:, 0, :], bank(BS), sg[:, 0, :], ALU.mult).then_inc(y_pool_done[b], 1)
                    dve.wait_ge(gate_sig[b], lin(2 * j + 2, 4, i))
                    dve.wait_ge(chunk_done, chunk(name, i, j, 2).count(1))
                    dve.tensor_tensor(mt[:, 1, :], bank(BS + 1), sg[:, 1, :], ALU.mult).then_inc(y_nsa_done[b], 1)
                    dve.wait_ge(y_pool_done[b], lin(j + 1, 2, i))
                    dve.wait_ge(y_nsa_done[b], lin(j + 1, 2, i))
                    wait(dve, mix_hl[b], m)
                    dve.tensor_tensor(mt[:, 2, :], mt[:, 0, :], mt[:, 1, :], ALU.add).then_inc(mixed[b], 1)
                    dve.wait_ge(mix_hh[b], lin(j + 1, 2, i))
                    sub(mix_lo[:, m, :], mt[:, 2, :], mix_hi[:, m, :]).then_inc(mix_hl[b], 1)

            def ffn(name, b, steps):
                prm = param("conv1" if b == 0 else "conv2").rearrange("p (f w) -> p f w", w=4)

                def conv(dst, src, f, done, i):
                    def w(k):
                        return prm[:, f, k:k + 1]
                    dve.tensor_scalar(dst, src, w(2), w(3), ALU.mult, ALU.add).then_inc(conv_done[b], 1)
                    dve.wait_ge(conv_done[b], lin(done + 1, 2 * steps, i))
                    dve.scalar_tensor_tensor(dst[:, 1:], src[:, 0:T - 1], w(1), dst[:, 1:], ALU.mult, ALU.add)\
                        .then_inc(conv_done[b], 1)
                    dve.wait_ge(conv_done[b], lin(done + 2, 2 * steps, i))
                    dve.scalar_tensor_tensor(dst[:, 2:], src[:, 0:T - 2], w(0), dst[:, 2:], ALU.mult, ALU.add)\
                        .then_inc(conv_done[b], 1)

                for i, j in units(dve, FK):
                    f = lin(j, 2, i)
                    dve.wait_ge(chunk_done, chunk(name, i, j, 0).count(1))
                    wait(dve, act_hl[b], lin(j - 1, 2, i))
                    conv(t_gate[:, j, :], bank(ACC), f, steps * j, i)
                    dve.wait_ge(chunk_done, chunk(name, i, j, 1).count(1))
                    if b == 0:
                        val = bank(ACC + 1)
                    else:
                        val = t_val[:, j, :]
                        conv(val, bank(ACC + 1), lin(FK + j, 2, i), steps * j + 3, i)
                        dve.wait_ge(conv_done[b], lin(steps * j + 6, 2 * steps, i))
                    dve.wait_ge(silu_done[b], lin(j + 1, 2, i))
                    dve.tensor_tensor(t_gate[:, j, :], t_gate[:, j, :], val, ALU.mult).then_inc(gated[b], 1)
                    dve.wait_ge(act_hh[b], lin(j + 1, 2, i))
                    sub(act_lo[:, f, :], t_gate[:, j, :], act_hi[:, f, :]).then_inc(act_hl[b], 1)

            def attention(a, mask):
                n = len(a.units)
                for s in range(n + 5):
                    if s < n:
                        w = (a.units[s][1] + 1) * P
                        dve.wait_ge(a.scored, s + 1)
                        wait(dve, a.exped, s - 1)
                        col = slice(s % 4, s % 4 + 1)
                        dve.tensor_tensor_reduce(a.sm[:, s % 2, 0:w], banks[:, BS + s % 2, 0:w],
                                                 mask(a.units[s], w), 1.0, NEG, ALU.add, ALU.max,
                                                 a.nbias[:, col]).then_inc(a.masked, 1)
                        dve.wait_ge(a.masked, s + 1)
                        dve.tensor_scalar(a.nbias[:, col], a.nbias[:, col], -DH ** -0.5, None, ALU.mult)\
                            .then_inc(a.shifted, 1)
                    u = s - 1
                    if 0 <= u < n:
                        col = slice(u % 4, u % 4 + 1)
                        dve.wait_ge(a.exped, u + 1)
                        wait(dve, a.weighted, u - 3)
                        dve.reciprocal(a.inv[:, col], a.sums[:, col]).then_inc(a.inverted, 1)
                    u = s - 4
                    if 0 <= u < n and u % a.per_tile == a.per_tile - 1:
                        j = u // a.per_tile
                        dve.wait_ge(a.high, j + 1)
                        sub(a.o_lo[:, j, :], bank(BO + j % 2), a.o_hi[:, j, :]).then_inc(a.low, 1)

            step = [0]

            def start(ins):
                step[0] += 1
                ins.then_inc(start_step, 1)
                dve.wait_ge(start_step, step[0])

            TURN = (6.28125, 0.0019350051879882812, 3.019915981956753e-07)
            MAGIC = 12582912.0
            ang, turns, tmp = angle[:, 1, :], angle[:, 0, :], angle[:, 2, :]
            dve.wait_ge(consts_in, 32)
            dve.wait_ge(pos_in, 16)
            start(dve.tensor_copy(tmp, pos_i[:, :]))
            start(dve.tensor_scalar(ang, tmp, const("inv"), None, ALU.mult))
            start(dve.tensor_scalar(tmp, ang, 1.0 / (2.0 * np.pi), MAGIC, ALU.mult, ALU.add))
            start(dve.tensor_scalar(turns, tmp, MAGIC, None, ALU.subtract))
            for part in TURN:
                start(dve.scalar_tensor_tensor(ang, turns, -part, ang, ALU.mult, ALU.add))
            start(dve.scalar_tensor_tensor(tmp, ang, -1.0, ang, ALU.mult, ALU.max))
            start(dve.tensor_scalar(tmp, tmp, -1.0, float(np.pi / 2), ALU.mult, ALU.add))
            dve.wait_ge(rel_in, 16)
            start(dve.tensor_scalar(rel_ext[:, 0:256], rel_row[:, 1:257], DH ** 0.5, None, ALU.mult))
            start(dve.tensor_scalar(rel_ext[:, 256:640], rel_row[:, 256:257].to_broadcast([NH, 384]), DH ** 0.5,
                                    None, ALU.mult))
            for m in range(DK):
                dve.wait_ge(sq_done, m + 1)
                if m == 0:
                    dve.tensor_copy(sq_sum[:, :], sq_ring[:, 0, :]).then_inc(sum_done, 1)
                else:
                    dve.wait_ge(sum_done, m)
                    dve.tensor_tensor(sq_sum[:, :], sq_sum[:, :], sq_ring[:, m % 2, :], ALU.add)\
                        .then_inc(sum_done, 1)
            norm(0)
            copy_tiles("in1", p1)

            tiles = [(t, param("q_gain")) for t in (4, 5, 6, 7)] + [(KS, param("k_gain", 1, 1)),
                                                                   (KW, param("k_gain", 2, 1))]
            dve.wait_ge(sin_done, 2)
            dve.wait_ge(rel_stored, 16)

            def rotate(n):
                x = p1[:, tiles[n][0], :]
                dve.wait_ge(n_gain, n + 1)
                wait(dve, n_sum, n - 1)
                dve.tensor_tensor(nr_c[:, n % 2, :], x, rope[:, 0, :], ALU.mult).then_inc(n_cos, 1)
                dve.wait_ge(n_rot, n + 1)
                dve.tensor_tensor(nr_s[:, n % 2, :], bank(BT + n % 2), rope[:, 1, :], ALU.mult).then_inc(n_sin, 1)
                dve.wait_ge(n_cos, n + 1)
                dve.wait_ge(n_sin, n + 1)
                dve.tensor_tensor(x, nr_c[:, n % 2, :], nr_s[:, n % 2, :], ALU.add).then_inc(n_sum, 1)

            for n, (t, gain) in enumerate(tiles):
                dve.wait_ge(n_inv, n + 1)
                dve.scalar_tensor_tensor(p1[:, t, :], p1[:, t, :], gain, nr_r[:, n % 2, :], ALU.mult, ALU.mult)\
                    .then_inc(n_gain, 1)
                if n:
                    rotate(n - 1)
            rotate(5)
            dve.wait_ge(blk_zero, 1)
            pe_ = param("pe").rearrange("p (c l) -> p c l", c=2)
            for c in range(2):
                for g in range(2):
                    src = p1[rows(g), KC + c, :].rearrange("p (a b) -> p b a", b=16)
                    for l2 in range(2):
                        dve.tensor_tensor(cmp_blk[rows(g), c, 16 * l2:16 * l2 + 16, g, :], src[:, :, l2:l2 + NCMP],
                                          pe_[rows(g), c, 16 * l2:16 * l2 + 16].unsqueeze(2).to_broadcast(
                                              [DH, 16, NCMP]), ALU.add).then_inc(blk_done, 1)
            dve.wait_ge(c_act, 8)
            dve.scalar_tensor_tensor(kc_t[:, :], banks[:, BO, 0:NCMP], param("k_gain", 0, 1), kc_tmp[:, 1, :],
                                     ALU.mult, ALU.mult).then_inc(c_dve, 1)
            dve.wait_ge(c_dve, 1)
            dve.tensor_tensor(kc_tmp[:, 2, :], kc_t[:, :], rope[:, 0, 31:T:16], ALU.mult).then_inc(c_dve, 1)
            dve.wait_ge(c_pe, 8)
            dve.tensor_tensor(kc_tmp[:, 3, :], banks[:, BT, 0:NCMP], rope[:, 1, 31:T:16], ALU.mult)\
                .then_inc(c_dve, 1)
            dve.wait_ge(c_dve, 3)
            dve.tensor_tensor(kc_t[:, :], kc_tmp[:, 2, :], kc_tmp[:, 3, :], ALU.add).then_inc(c_dve, 1)
            for gi in range(4):
                dve.wait_ge(yp_h, gi + 1)
                dve.scalar_tensor_tensor(yp_lo[:, gi, :], bank(ACC + gi % 2), param("pool_scale", gi, 1),
                                         yp_hi[:, gi, :], ALU.mult, ALU.subtract).then_inc(yp_l, 1)
            flat = cmp_s[:, :, :, :, :].rearrange("p a b c n -> p (a b c) n")
            wide = [P, 32, NCMP]
            for half in range(2):
                dve.wait_ge(s_pe, half + 1)
                dve.tensor_tensor(cmp_s[:, half, :, :, :],
                                  banks[:, BS + half, 0:16 * NCMP].rearrange("p (a b n) -> p a b n", a=4, b=4),
                                  const("cmp", NT, NCMP).unsqueeze(2).to_broadcast([P, NT, 4, NCMP]), ALU.add)\
                    .then_inc(s_dve, 1)
            dve.wait_ge(s_dve, 2)
            dve.tensor_reduce(cmp_red[:, 0, :], flat, AXX, ALU.max).then_inc(s_dve, 1)
            dve.wait_ge(s_dve, 3)
            sub(flat, flat, cmp_red[:, 0, :].unsqueeze(2).to_broadcast(wide)).then_inc(s_dve, 1)
            dve.wait_ge(s_act, 1)
            dve.tensor_reduce(cmp_red[:, 1, :], flat, AXX, ALU.add).then_inc(s_dve, 1)
            dve.wait_ge(s_dve, 5)
            dve.reciprocal(cmp_red[:, 2, :], cmp_red[:, 1, :]).then_inc(s_dve, 1)
            dve.wait_ge(v_copied[0], 3)
            dve.wait_ge(s_dve, 6)
            fac = cmp_red[:, 2, :].rearrange("p (h a b) -> p h a b", h=2, a=NT)
            gts = gate_t[:, :, :].rearrange("p a (h n) -> p a h n", n=3)
            for half in range(2):
                dve.tensor_tensor(fac[:, half, :, :], fac[:, half, :, :], gts[:, :, 4 * half:4 * half + 4, 0],
                                  ALU.mult).then_inc(s_dve, 1)
            dve.wait_ge(s_dve, 8)
            dve.tensor_scalar(fac[:, :, 0, :], fac[:, :, 0, :], const("cmp_any"), None, ALU.mult).then_inc(s_dve, 1)
            dve.wait_ge(s_dve, 9)
            dve.tensor_tensor(flat, flat, cmp_red[:, 2, :].unsqueeze(2).to_broadcast(wide), ALU.mult)\
                .then_inc(s_dve, 1)
            attention(att1, lambda u, w: const("causal")[:, T - w:T])
            merge("mix1", 0, sg1, mt1, mix1_hi, mix1_lo)
            residual("out1", 1)
            norm(1)
            ffn("up1", 0, 3)
            residual("down1", 2)

            norm(2)
            taps = param("conv_qkv").rearrange("p (f w) -> p f w", w=4)
            for i, j in units(dve, 12):
                t = lin(j, 2, i)
                src, dst = bank(ACC + j), cv[:, j, :]
                dve.wait_ge(chunk_done, chunk("in2c", i, j).count(1))
                wait(dve, cv_silu, lin(j - 1, 2, i))
                dve.tensor_scalar(dst, src, taps[:, t, 3:4], None, ALU.mult).then_inc(cv_done, 1)
                for k in range(1, 4):
                    dve.wait_ge(cv_done, lin(4 * j + k, 8, i))
                    dve.scalar_tensor_tensor(dst[:, k:], src[:, 0:T - k], taps[:, t, 3 - k:4 - k], dst[:, k:],
                                             ALU.mult, ALU.add).then_inc(cv_done, 1)
            copy_tiles("in2z", p2a[:, 12:17, :])
            g = slice(32, 32 + GH)
            col = {n: params[g, PARAM[n][0]:PARAM[n][0] + 1] for n in ("a_log", "dt_bias")}
            dve.wait_ge(copied["in2z"], 5)
            dve.tensor_scalar(gz[g, :], p2a[g, 16, :], col["dt_bias"], None, ALU.add).then_inc(g_dve, 1)
            dve.wait_ge(g_dve, 1)
            dve.scalar_tensor_tensor(gz2[g, :], gz[g, :], -1.0, gz[g, :], ALU.mult, ALU.max).then_inc(g_dve, 1)
            for n in range(8):
                dve.wait_ge(l_inv, n + 1)
                dve.scalar_tensor_tensor(p2a[:, n, :], p2a[:, n, :], float(P) ** -0.5 if n < GH else 1.0,
                                         l2_r[:, n % 2, :], ALU.mult, ALU.mult).then_inc(l_out, 1)
            dve.wait_ge(g_act, 3)
            dve.scalar_tensor_tensor(gz[g, :], gz[g, :], 0.0, gz2[g, :], ALU.max, ALU.add).then_inc(g_dve, 1)
            dve.tensor_scalar(ea[g, 1:2], ea[g, 0:1], -1.0, None, ALU.mult).then_inc(g_dve, 1)
            dve.wait_ge(g_dve, 4)
            dve.tensor_scalar(gz2[g, :], gz[g, :], ea[g, 1:2], None, ALU.mult).then_inc(g_dve, 1)
            dve.wait_ge(g_dve, 5)
            dve.wait_ge(blk_zero, 2)
            dve.tensor_tensor_scan(gb_rows[g, :], const("reset")[g, :], gz2[g, :], 0.0, ALU.mult, ALU.add)\
                .then_inc(g_dve, 1)
            dve.wait_ge(g_act, 6)
            dve.tensor_scalar(gd_neg[:, :, :], gd_cols[:, :, 32:32 + GH], -1.0, None, ALU.mult).then_inc(g_dve, 1)
            dve.tensor_tensor(gd_bg[:, :, :], gd_bg[:, :, :], gd_cols[:, :, 0:GH], ALU.mult).then_inc(g_dve, 1)
            dve.wait_ge(g_dve, 8)
            sq3 = [P, NT, P]

            def every(mask):
                return mask.unsqueeze(1).to_broadcast(sq3)

            def per_token(c_):
                return c_.unsqueeze(2).to_broadcast(sq3)

            dve.wait_ge(l_out, 8)
            for h in range(GH):
                b = 11 * h
                dve.wait_ge(d_pe, 6 * h + 1)
                dve.wait_ge(d_act, 7 * h + 1)
                wait(dve, d_dve, b)
                dve.tensor_tensor(dec[:, :, :], bank(BS, NT), every(const("decay")), ALU.add).then_inc(d_dve, 1)
                for half in range(2):
                    e = CH - 1 if half == 0 else P - 1
                    sub(gd_kd[rows(half), h, :], banks[rows(half), BS, e:T:P],
                        gd_cols[rows(half), :, 32 + h]).then_inc(d_dve, 1)
                dve.wait_ge(d_pe, 6 * h + 2)
                dve.tensor_tensor(beta_strict[:, :, :], bank(BS + 1, NT), every(const("strict")), ALU.mult)\
                    .then_inc(d_dve, 1)
                dve.wait_ge(d_pe, 6 * h + 4)
                dve.wait_ge(d_act, 7 * h + 1)
                dve.tensor_tensor(p2a[:, h, :], p2a[:, h, :], gam_row[:, :], ALU.mult).then_inc(d_dve, 1)
                dve.wait_ge(d_act, 7 * h + 5)
                dve.tensor_tensor(p_t[:, h, :, :], bank(BT + 1, NT), dec[:, :, :], ALU.mult).then_inc(d_dve, 1)
                dve.wait_ge(d_dve, b + 6)
                dve.tensor_tensor(dec[:, :, :], bank(BT, NT), dec[:, :, :], ALU.mult).then_inc(d_dve, 1)
                dve.wait_ge(d_dve, b + 7)
                dve.tensor_tensor(a_t[:, h, :, :], dec[:, :, :], beta_strict[:, :, :], ALU.mult).then_inc(d_dve, 1)
                dve.wait_ge(d_pe, 6 * h + 5)
                dve.tensor_tensor(k_bg[:, h, :, :], bank(BO, NT), per_token(gd_bg[:, :, h]), ALU.mult)\
                    .then_inc(d_dve, 1)
                dve.wait_ge(d_act, 7 * h + 6)
                dve.tensor_tensor(k_dec[:, h, :, :], bank(BO, NT), per_token(gd_kd[:, h, :]), ALU.mult)\
                    .then_inc(d_dve, 1)
                dve.wait_ge(d_pe, 6 * h + 6)
                dve.tensor_tensor(v_b[:, h, :, :], bank(BO + 1, NT), per_token(gd_cols[:, :, h]), ALU.mult)\
                    .then_inc(d_dve, 1)
            dve.wait_ge(d_dve, 11 * GH)
            lev = const("level", 6, P)
            for h in range(GH):
                wait(dve, i_bx, h - 1)
                dve.tensor_tensor(b_t[:, h % 2, :, :], a_t[:, h, :, :], every(lev[:, 0, :]), ALU.mult)\
                    .then_inc(i_mask, 1)
                dve.wait_ge(i_mask, h + 1)
                sub(y_inv[:, h, :, :], every(ident), b_t[:, h % 2, :, :]).then_inc(i_y, 1)
                dve.wait_ge(i_bx, h + 1)
                sub(x_inv[:, h, :, :], every(ident), bank(BT + h % 2, NT)).then_inc(i_x, 1)

            def update(k):
                h = k % GH
                dve.wait_ge(i_pe, 2 * k + 1)
                sub(x_inv[:, h, :, :], x_inv[:, h, :, :], bank(BS + k % 2, NT)).then_inc(i_x, 1)
                dve.wait_ge(i_pe, 2 * k + 2)
                sub(y_inv[:, h, :, :], y_inv[:, h, :, :], bank(BO + k % 2, NT)).then_inc(i_y, 1)

            for k in range(5 * GH):
                dve.wait_ge(i_y, GH)
                dve.wait_ge(i_bx, GH + k - 1)
                dve.tensor_tensor(b_t[:, k % 2, :, :], a_t[:, k % GH, :, :], every(lev[:, 1 + k // GH, :]), ALU.mult)\
                    .then_inc(i_mask, 1)
                if k:
                    update(k - 1)
            update(5 * GH - 1)
            for c in range(NCH):
                p, half, slot = c // 2, c % 2, c // 2 % 2
                rs = rows(half)
                if c == 0:
                    dve.wait_ge(r_cp, 2 * GH)
                    dve.tensor_copy(u_new[rs, slot, :, :], uv[rs, :, p, :]).then_inc(r_u, 1)
                else:
                    dve.wait_ge(r_ws, c)
                    sub(u_new[rs, slot, :, :], uv[rs, :, p, :], bank(BS + c % 2, GH)[rs]).then_inc(r_u, 1)
                if c == NCH - 1:
                    break
                dve.wait_ge(r_ds, c + 1)
                wait(dve, r_o, c)
                wait(dve, r_s, GH * c)
                for h in range(GH):
                    new = bank(BT + c % 2, GH)[:, h, :]
                    if c == 0:
                        dve.tensor_copy(state[:, 0, h, :], new).then_inc(r_s, 1)
                    else:
                        dve.scalar_tensor_tensor(state[:, c % 2, h, :], state[:, (c - 1) % 2, h, :],
                                                 gd_last[:, h, c:c + 1], new, ALU.mult, ALU.add).then_inc(r_s, 1)
            dve.wait_ge(f_act, 2)
            dve.tensor_reduce(o_red[:, :], o_sq.rearrange("p c h d -> p (c h) d"), AXX, ALU.add).then_inc(f_dve, 1)
            dve.wait_ge(f_act, 4)
            on = o_nat.rearrange("p c h d -> p (c h) d")
            dve.tensor_tensor(on, on, o_red[:, :].unsqueeze(2).to_broadcast([P, NT * GH, P]), ALU.mult)\
                .then_inc(f_dve, 1)
            for h in range(GH):
                dve.wait_ge(f_pe, h + 1)
                wait(dve, oa_l, h - 1)
                dve.scalar_tensor_tensor(oa[:, h % 2, :], bank(BT + h % 2), param("gdn_gain"), p2a[:, 12 + h, :],
                                         ALU.mult, ALU.mult).then_inc(f_dve, 1)
                dve.wait_ge(oa_h, h + 1)
                sub(oa_lo[:, h, :], oa[:, h % 2, :], oa_hi[:, h, :]).then_inc(oa_l, 1)
            copy_tiles("in2b", p2b)
            dve.wait_ge(blk_zero, 3)
            attention(att2, lambda u, w: rel[:, 2 * u[0] + u[3], w - 1::-1])
            merge("mix2", 1, sg2, mt2, mix2_hi, mix2_lo)
            residual("out2", 3)
            norm(3)
            ffn("up2", 1, 6)
            residual("down2", 4)
            norm(4)

        @block.tensor
        def _(pe):
            def product(c, dst, hi, lo, ks, first, last, done, ready=None):
                for n, (ks_, kr) in enumerate(ks):
                    w_h = w_hi[:, c.slot, ks_ * P:(ks_ + 1) * P]
                    w_l = w_lo[:, c.slot, ks_ * P:(ks_ + 1) * P]
                    if ready:
                        pe.wait_ge(ready[0], ready[1] + kr + 1)
                    pe.matmul(dst, w_h, hi[:, kr, :], start=first and n == 0, stop=False)
                    pe.matmul(dst, w_h, lo[:, kr, :], start=False, stop=False)
                    mm = pe.matmul(dst, w_l, hi[:, kr, :], start=False, stop=last and n == len(ks) - 1)
                mm.then_inc(done, 1)

            def whole(n, off=0):
                return [(k, off + k) for k in range(n)]

            def norm(n):
                pe.wait_ge(sum_done, DK * (n + 1))
                pe.matmul(bank(BS), ones, sq_sum[:, :], start=True, stop=True).then_inc(mean_done, 1)

            def linear(name, n, used, per=1):
                for i, j in units(pe, INFO[name][0]):
                    c = chunk(name, i, j)
                    pe.wait_ge(lo_ready, c.count(1))
                    wait(pe, used, lin(per * (j - 1), 2 * per, i))
                    first = isinstance(i, int) and i == 0 and j == 0
                    product(c, bank(ACC + j), h_hi, h_lo, whole(DK), True, True, chunk_done,
                            (hl_done, DK * n) if first else None)

            def residual(name, n, hi, lo, split_):
                nchunk, kt = INFO[name][1], INFO[name][2]
                for i, j in units(pe, DK):
                    wait(pe, x_done, lin(DK * (n - 1) + j - 1, 2, i) if not (isinstance(i, int) and i == 0) else 0)
                    for q in range(nchunk):
                        c = chunk(name, i, j, q)
                        pe.wait_ge(lo_ready, c.count(1))
                        first = isinstance(i, int) and i == 0 and j == 0
                        product(c, bank(ACC + j), hi, lo, whole(kt, kt * q), q == 0, q == nchunk - 1, chunk_done,
                                (split_, 0) if first else None)

            def merge(name, b, y1, y2):
                for i, j in units(pe, DK):
                    m = lin(j, 2, i)
                    for q in range(2):
                        c = chunk(name, i, j, q)
                        pe.wait_ge(lo_ready, c.count(1))
                        wait(pe, gate_sig[b], lin(2 * j - 1 + q, 4, i))
                        product(c, bank(ACC + q), h_hi, h_lo, whole(DK), True, True, chunk_done)
                    c = chunk(name, i, j, 2)
                    pe.wait_ge(lo_ready, c.count(1))
                    wait(pe, y_pool_done[b], m)
                    product(c, bank(BS), *y1, [(k, k) for k in range(4)], True, True, first_half[b])
                    wait(pe, y_nsa_done[b], m)
                    product(c, bank(BS + 1), *y2, [(4 + k, k) for k in range(4)], True, True, chunk_done)

            def ffn(name, b, n, steps):
                for i, j in units(pe, FK):
                    first = isinstance(i, int) and i == 0 and j == 0
                    for q in range(2):
                        c = chunk(name, i, j, q)
                        pe.wait_ge(lo_ready, c.count(1))
                        if q == 0 and not first:
                            pe.wait_ge(conv_done[b], lin(steps * (j - 1) + 3, 2 * steps, i))
                        elif q == 1 and b == 0:
                            wait(pe, gated[b], lin(j, 2, i))
                        elif q == 1:
                            wait(pe, conv_done[b], lin(steps * j, 2 * steps, i))
                        product(c, bank(ACC + q), h_hi, h_lo, whole(DK), True, True, chunk_done,
                                (hl_done, DK * n) if first and q == 0 else None)
                pe.wait_ge(conv_done[b], steps * (FK - 1) + 3)

            def turn(dst, src, n=P, last=None):
                return pe.transpose(dst, src, ident[0:n, 0:n])

            def attention(a, q_tile, k_tile, v_tile, first_values=None):
                n = len(a.units)
                for s in range(n + 3):
                    if s < n:
                        j, i, b, half = a.units[s]
                        wait(pe, a.masked, s - 1)
                        pe.matmul(banks[:, BS + half, 0:(i + 1) * P], q_tile(j)[rows(half), i * P:(i + 1) * P],
                                  k_tile(j, b)[rows(half), 0:(i + 1) * P], start=True, stop=True)\
                            .then_inc(a.scored, 1)
                    u = s - 2
                    if 0 <= u < n:
                        j, i, b, half = a.units[u]
                        pe.wait_ge(a.weighted, u + 1)
                        wait(pe, a.fetched, u - 1)
                        for k in range(i + 1):
                            mm = turn(banks[:, BT + u % 2, k * P:(k + 1) * P], a.p[:, u % 3, k * P:(k + 1) * P])
                        mm.then_inc(a.flipped, 1)
                    u = s - 3
                    if 0 <= u < n:
                        j, i, b, half = a.units[u]
                        pe.wait_ge(a.fetched, u + 1)
                        if u % a.per_tile == 0:
                            wait(pe, a.low, j - 1)
                        dst = banks[rows(half), BO + j % 2, i * P:(i + 1) * P]
                        begin = b == 0
                        if begin and first_values:
                            pe.matmul(dst, *first_values(j, i, half), start=True, stop=False)
                            begin = False
                        end = b == max(x[2] for x in a.units)
                        for k in range(i + 1):
                            mm = pe.matmul(dst, v_tile(j, b, half, k), a.pt[:, u % 2, k * P:(k + 1) * P],
                                           start=begin and k == 0, stop=end and k == i)
                        mm.then_inc(a.summed, 1)

            pe.wait_ge(consts_in, 32)
            norm(0)
            linear("in1", 0, copied["in1"])

            pe.wait_ge(copied["in1"], 15)
            tiles = (4, 5, 6, 7, KS, KW)

            def rotate(n):
                pe.wait_ge(n_gain, n + 1)
                wait(pe, n_sin, n - 1)
                pe.matmul(bank(BT + n % 2), const("rot"), p1[:, tiles[n], :], start=True, stop=True)\
                    .then_inc(n_rot, 1)

            for n in range(6):
                pe.wait_ge(n_sq, n + 1)
                wait(pe, n_ln, n - 1)
                pe.matmul(bank(BS + n % 2), halves, nr_sq[:, n % 2, :], start=True, stop=True).then_inc(n_ms, 1)
                if n:
                    rotate(n - 1)
            rotate(5)
            for v in range(2):
                for k in range(NT):
                    mm = turn(banks[:, BO + v, k * P:(k + 1) * P], p1[:, VS + v, k * P:(k + 1) * P])
                mm.then_inc(turned[0], 1)
            pe.wait_ge(gates_ready, 1)
            for k in range(NT):
                mm = turn(banks[:, ACC, 24 * k:24 * k + 24], p1[0:24, GT, k * P:(k + 1) * P], 24)
            mm.then_inc(turned[0], 1)
            pe.wait_ge(blk_done, 8)
            pe.wait_ge(cmp_in, 64)
            pe.wait_ge(n_ln, 6)
            pe.wait_ge(n_sin, 6)
            for c in range(2):
                for l in range(32):
                    mm = pe.matmul(banks[0:2 * NCMP, BS + c, 0:P],
                                   cmp_blk[:, c, l, :, :].rearrange("p a b -> p (a b)"),
                                   cmp_w1[:, c, l * P:(l + 1) * P], start=l == 0, stop=l == 31)
                mm.then_inc(c_pe, 1)
            for c in range(2):
                pe.wait_ge(c_act, c + 1)
                turn(banks[:, BT + c, 0:2 * NCMP], hid[:, c, :], 2 * NCMP).then_inc(c_pe, 1)
            pe.wait_ge(v_copied[0], 3)
            pe.wait_ge(c_act, 3)
            for g in range(2):
                mm = pe.matmul(banks[rows(g), BO, 0:NCMP], cmp_w2[:, 0, :], hid_t[:, 0, g * NCMP:(g + 1) * NCMP],
                               start=True, stop=True)
            mm.then_inc(c_pe, 1)
            pe.wait_ge(c_act, 4)
            for g in range(2):
                mm = pe.matmul(banks[0:NCMP, BO + 1, g * DH:(g + 1) * DH], hid_t[:, 1, g * NCMP:(g + 1) * NCMP],
                               cmp_w2[:, 1, :], start=True, stop=True)
            mm.then_inc(c_pe, 1)
            pe.wait_ge(c_act, 5)
            pe.matmul(banks[:, BS, 0:NCMP], halves, kc_tmp[:, 0, :], start=True, stop=True).then_inc(c_pe, 1)
            for gi in range(2):
                pe.wait_ge(pooled, sum(1 + g_ + 1 + 3 for g_ in range(gi + 1)))
                pe.matmul(bank(ACC + gi % 2), pool_w[:, gi, :], p1[:, gi, :], start=True, stop=True)\
                    .then_inc(pool_mul, 1)
            pe.wait_ge(c_dve, 1)
            pe.matmul(banks[:, BT, 0:NCMP], const("rot"), kc_t[:, :], start=True, stop=True).then_inc(c_pe, 1)
            for gi in range(2, 4):
                pe.wait_ge(pooled, sum(1 + g_ + 1 + 3 for g_ in range(gi + 1)))
                pe.wait_ge(yp_l, gi - 1)
                pe.matmul(bank(ACC + gi % 2), pool_w[:, gi, :], p1[:, gi, :], start=True, stop=True)\
                    .then_inc(pool_mul, 1)
            pe.wait_ge(c_dve, 4)
            pe.wait_ge(n_sum, 6)
            for half in range(2):
                for i in range(NT):
                    for j in range(4):
                        at_ = (4 * i + j) * NCMP
                        mm = pe.matmul(banks[:, BS + half, at_:at_ + NCMP],
                                       p1[rows(half), 4 + j, i * P:(i + 1) * P], kc_t[rows(half), :],
                                       start=True, stop=True)
                mm.then_inc(s_pe, 1)
            pe.wait_ge(s_dve, 10)
            for r in range(8):
                wait(pe, s_act, r)
                for k in range(4):
                    half, i, j = r // 4, r % 4, k
                    mm = turn(banks[0:NCMP, BT + r % 2, k * P:(k + 1) * P], cmp_s[:, half, i, j, :])
                mm.then_inc(s_pe, 1)
            pe.wait_ge(s_act, 9)
            attention(att1, lambda j: p1[:, 4 + j, :], lambda j, b: p1[:, KS + b, :],
                      lambda j, b, half, k: v1_nat[:, b, k, rows(half)],
                      lambda j, i, half: (vc_nat[:, half, :], pc_t[:, 16 * half + 4 * i + j, :]))
            pe.wait_ge(yp_l, 4)
            pe.wait_ge(att1.low, 4)
            merge("mix1", 0, (yp_hi, yp_lo), (o1_hi, o1_lo))
            residual("out1", 1, mix1_hi, mix1_lo, mix_hl[0])
            norm(1)
            ffn("up1", 0, 1, 3)
            residual("down1", 2, act_hi, act_lo, act_hl[0])

            norm(2)
            linear("in2c", 2, cv_done, 4)
            pe.wait_ge(cv_done, 48)
            linear("in2z", 2, copied["in2z"])
            for n in range(8):
                pe.wait_ge(l_sq, n + 1)
                wait(pe, l_ln, n - 1)
                pe.matmul(bank(BS + n % 2), ones, l2_sq[:, n % 2, :], start=True, stop=True).then_inc(l_ms, 1)
            pe.wait_ge(g_dve, 6)
            pe.wait_ge(g_act, 4)
            for p in range(NT):
                mm = turn(banks[:, BO, 64 * p:64 * p + 64], gb_rows[:, p * P:(p + 1) * P], 64)
            mm.then_inc(g_pe, 1)
            pe.wait_ge(g_act, 5)
            pe.wait_ge(l_out, 8)
            pick = const("pick", 2 * GH, P)
            for h in range(GH):
                q_, k_, v_ = p2a[:, h, :], p2a[:, GH + h, :], p2a[:, 2 * GH + h, :]
                b = 11 * (h - 1)

                def free(n):
                    if h:
                        pe.wait_ge(d_dve, b + n)

                free(3)
                if h:
                    pe.wait_ge(d_act, 7 * (h - 1) + 1)
                pe.matmul(bank(BS), pick[0:64, GH + h, :], gb_rows[:, :], start=True, stop=True).then_inc(d_pe, 1)
                free(4)
                pe.matmul(bank(BS + 1), pick[0:64, h, :], gb_rows[:, :], start=True, stop=True).then_inc(d_pe, 1)
                for n, (dst, lhs, rhs) in enumerate(((BT, k_, k_), (BT + 1, k_, q_), (BO, k_, None), (BO + 1, v_, None))):
                    free((7, 6, 10, 11)[n])
                    for p in range(NT):
                        cols = slice(p * P, (p + 1) * P)
                        if rhs is None:
                            mm = turn(banks[:, dst, cols], lhs[:, cols])
                        else:
                            mm = pe.matmul(banks[:, dst, cols], lhs[:, cols], rhs[:, cols], start=True, stop=True)
                    mm.then_inc(d_pe, 1)
            pe.wait_ge(d_dve, 11 * GH)
            for h in range(GH):
                pe.wait_ge(i_mask, h + 1)
                wait(pe, i_x, h - 1)
                for p in range(NT):
                    mm = turn(banks[:, BT + h % 2, p * P:(p + 1) * P], b_t[:, h % 2, p, :])
                mm.then_inc(i_bx, 1)
            pe.wait_ge(i_x, GH)

            def corrections(k):
                h, r = k % GH, k % 2
                pe.wait_ge(i_cp, k + 1)
                wait(pe, i_x, GH + k - 1)
                for p in range(NT):
                    mm = pe.matmul(banks[:, BS + r, p * P:(p + 1) * P], y_inv[:, h, p, :], bx[:, r, p, :],
                                   start=True, stop=True)
                mm.then_inc(i_pe, 1)
                wait(pe, i_y, GH + k - 1)
                for p in range(NT):
                    mm = pe.matmul(banks[:, BO + r, p * P:(p + 1) * P], bx[:, r, p, :], y_inv[:, h, p, :],
                                   start=True, stop=True)
                mm.then_inc(i_pe, 1)

            for k in range(5 * GH):
                h, r = k % GH, k % 2
                pe.wait_ge(i_mask, GH + k + 1)
                pe.wait_ge(i_x, k + 1)
                pe.wait_ge(i_y, k + 1)
                wait(pe, i_cp, k - 1)
                for p in range(NT):
                    mm = pe.matmul(banks[:, BT + r, p * P:(p + 1) * P], b_t[:, r, p, :], x_inv[:, h, p, :],
                                   start=True, stop=True)
                mm.then_inc(i_bx, 1)
                if k:
                    corrections(k - 1)
            corrections(5 * GH - 1)
            pe.wait_ge(i_y, 6 * GH)
            pe.wait_ge(i_x, 6 * GH)
            for h in range(GH):
                for m, dst in ((0, BT), (1, BO)):
                    wait(pe, r_cp, 2 * (h - 2) + 1 + m)
                    for p in range(NT):
                        lhs, rhs = (k_bg[:, h, p, :], y_inv[:, h, p, :]) if m == 0 else \
                            (y_inv[:, h, p, :], v_b[:, h, p, :])
                        mm = pe.matmul(banks[:, dst + h % 2, p * P:(p + 1) * P], lhs, rhs, start=True, stop=True)
                    mm.then_inc(r_w, 1)
            pe.wait_ge(r_cp, 2 * GH)
            for c in range(NCH):
                p, half, slot = c // 2, c % 2, c // 2 % 2
                rs, tok = rows(half), slice(c * CH, (c + 1) * CH)
                if c:
                    pe.wait_ge(r_s, GH * c)
                    for h in range(GH):
                        w = w_t[:, h, :, :].rearrange("p a b -> p (a b)")
                        mm = pe.matmul(banks[rs, BS + c % 2, h * P:(h + 1) * P], w[:, tok],
                                       state[:, (c - 1) % 2, h, :], start=True, stop=True)
                    mm.then_inc(r_ws, 1)
                pe.wait_ge(r_u, c + 1)
                if c < NCH - 1:
                    for h in range(GH):
                        mm = pe.matmul(banks[:, BT + c % 2, h * P:(h + 1) * P], k_dec[rs, h, p, :],
                                       u_new[rs, slot, h, :], start=True, stop=True)
                    mm.then_inc(r_ds, 1)
                if half == 0:
                    wait(pe, r_ocp, p - 1)
                for h in range(GH):
                    dst = banks[rs, BO + p % 2, h * P:(h + 1) * P]
                    if c:
                        pe.matmul(dst, p2a[:, h, tok], state[:, (c - 1) % 2, h, :], start=True, stop=False)
                    mm = pe.matmul(dst, p_t[rs, h, p, rs], u_new[rs, slot, h, :], start=c == 0, stop=True)
                mm.then_inc(r_o, 1)
            pe.wait_ge(f_dve, 2)
            for h in range(GH):
                wait(pe, f_dve, h + 1 if h >= 2 else 0)
                for p in range(NT):
                    mm = turn(banks[:, BT + h % 2, p * P:(p + 1) * P], o_nat[:, p, h, :])
                mm.then_inc(f_pe, 1)
            linear("in2b", 2, copied["in2b"])
            pe.wait_ge(copied["in2b"], 12)
            for v in range(4):
                wait(pe, v_copied[1], v - 1)
                for k in range(NT):
                    mm = turn(banks[:, BO + v % 2, k * P:(k + 1) * P], p2b[:, 8 + v, k * P:(k + 1) * P])
                mm.then_inc(turned[1], 1)
            pe.wait_ge(v_copied[1], 4)
            attention(att2, lambda j: p2b[:, j, :], lambda j, b: p2b[:, 4 + j, :],
                      lambda j, b, half, k: v2_nat[:, k, j * P + half * DH:j * P + (half + 1) * DH])
            pe.wait_ge(att2.low, 4)
            pe.wait_ge(oa_l, 4)
            merge("mix2", 1, (oa_hi, oa_lo), (ob_hi, ob_lo))
            residual("out2", 3, mix2_hi, mix2_lo, mix_hl[1])
            norm(3)
            ffn("up2", 1, 3, 6)
            residual("down2", 4, act_hi, act_lo, act_hl[1])
            norm(4)


def diagonals(rows_dram, h):
    view = rows_dram[h:h + 1, 0:T]
    return bass.AP(tensor=view.tensor, offset=view.offset, ap=[[1, P], [1, T]])


def by_tiles(w, columns=None):
    k, m = w.shape
    if columns is None:
        t = w.reshape(k // P, P, m // P, P)
    else:
        t = np.zeros((k, len(columns), P), w.dtype)
        for n, cols in enumerate(columns):
            for at, a, b in cols:
                t[:, n, at:at + b - a] = w[:, a:b]
        t = t.reshape(k // P, P, len(columns), P)
    return np.ascontiguousarray(t.transpose(2, 1, 0, 3)).reshape(t.shape[2], P, -1)


def by_columns(v):
    return v.reshape(-1, P).T


def kernel(**inputs):
    from concourse import bacc
    from concourse.bass_utils import run_bass_kernel_spmd

    a = {k: np.asarray(v) for k, v in inputs.items()}
    a = {k: v[0] if k not in ("norm_final_w_2",) else v for k, v in a.items()}

    def straight(first, n):
        return [[(0, first + P * t, first + P * (t + 1))] for t in range(n)]

    q_pairs = [[(0, 512 + DH * j, 512 + DH * (j + 1)), (DH, 512 + DH * (j + 4), 512 + DH * (j + 5))]
               for j in range(4)]
    kv = 1024
    in1 = straight(0, 4) + q_pairs + straight(kv, 2) + straight(kv + 3 * P, 1) + straight(kv + 5 * P, 1) + \
        straight(kv + 2 * P, 1) + straight(kv + 4 * P, 1) + [[(0, 1792, 1816)]]
    branch = np.concatenate([a["w_pool_out"]] + [a["w_nsa_out"][DH * h:DH * (h + 1)] for h in
                                                 (0, 4, 1, 5, 2, 6, 3, 7)])

    def merged(gates, first, branches):
        t = [by_tiles(gates, straight(first, DK)), by_tiles(gates, straight(first + D, DK)), by_tiles(branches)]
        return np.stack(t, 1).reshape(3 * DK, P, -1)

    def gate_and_value(w):
        t = by_tiles(w)
        return np.stack([t[:FK], t[FK:]], 1).reshape(2 * FK, P, -1)

    def in_halves(w):
        t = by_tiles(w)
        return np.ascontiguousarray(t.reshape(DK, P, 2, -1).transpose(0, 2, 1, 3)).reshape(2 * DK, P, -1)

    w2 = a["w_in_2"]
    small = [[(0, 2048, 2052), (32, 2052, 2056)]]
    feeds = {
        "w_in1": by_tiles(a["w_in"], in1),
        "w_mix1": merged(a["w_in"], 1816, branch),
        "w_out1": by_tiles(a["w_out"]),
        "w_up1": gate_and_value(a["w_up"]),
        "w_down1": in_halves(a["w_down"]),
        "w_in2c": by_tiles(w2, straight(0, 12)),
        "w_in2z": by_tiles(w2, straight(1536, 4) + small),
        "w_in2b": by_tiles(w2, straight(2056, 12)),
        "w_mix2": merged(w2, 2056 + 1536, np.concatenate([a["w_branch_a_2"], a["w_branch_b_2"]])),
        "w_out2": by_tiles(a["w_out_2"]),
        "w_up2": gate_and_value(a["w_up_2"]),
        "w_down2": in_halves(a["w_down_2"]),
        "x": np.ascontiguousarray(a["x"].T.reshape(DK, P, T).transpose(1, 0, 2)),
        "positions": a["positions"][None, :],
        "rel": a["rel_bias_2"],
        "cmp_w1": np.ascontiguousarray(a["cmp_w1"].transpose(2, 0, 1, 3)).reshape(DH, 2, 32 * P),
        "cmp_w2": np.ascontiguousarray(a["cmp_w2"].transpose(1, 0, 2)),
        "pool_w": np.ascontiguousarray(a["pool_w"].transpose(1, 0, 2)),
        "consts": constants(),
    }
    prm = np.zeros((P, N_PARAM), np.float32)

    def put(name, value, rows_=slice(0, P)):
        at, n = PARAM[name]
        prm[rows_, at:at + n] = value

    put("gain", np.concatenate([by_columns(a[n]) for n in (
        "mix_norm_g", "ffn_norm_g", "norm_mix_w_2", "norm_ffn_w_2", "norm_final_w_2")], 1))
    twice = (slice(0, DH), slice(DH, P))
    for r in twice:
        put("q_gain", a["q_norm_g"][:, None], r)
        put("k_gain", a["k_norm_g"].T, r)
        put("pe", a["cmp_pe"].transpose(2, 0, 1).reshape(DH, 64), r)
    put("pool_scale", by_columns(a["pool_scale"]))

    def taps(w, b=None):
        rows_ = [by_columns(x) for x in w] + ([by_columns(b)] if b is not None else [])
        return np.stack(rows_, 2).reshape(P, -1)

    put("conv1", taps(a["conv_w"], a["conv_b"]))
    put("conv2", taps(a["conv_ffn_w_2"], a["conv_ffn_b_2"]))
    put("conv_qkv", taps(a["conv_qkv_w_2"]))
    put("gdn_gain", a["gdn_norm_w_2"][:, None])
    put("a_log", a["a_log_2"][:, None], slice(32, 32 + GH))
    put("dt_bias", a["dt_bias_2"][:, None], slice(32, 32 + GH))
    feeds["params"] = prm

    nc = bacc.Bacc("TRN2", target_bir_lowering=False, num_devices=1)
    t_in = {name: nc.dram_tensor("in_" + name, v.shape, mybir.dt.from_np(v.dtype), kind="ExternalInput").ap()
            for name, v in feeds.items()}
    out = nc.dram_tensor("out_t", (P, DK, T), F32, kind="ExternalOutput").ap()
    two_blocks(nc, t_in, out)
    r = run_bass_kernel_spmd(nc, [{"in_" + k: v for k, v in feeds.items()}], core_ids=[0])
    got = np.asarray(r.results[0]["out_t"]).reshape(P, DK, T)
    return got.transpose(2, 1, 0).reshape(1, T, D)
```

```python
from contextlib import ExitStack

import numpy as np

import concourse.bass as bass
from concourse import mybir

F32 = mybir.dt.float32
F32R = mybir.dt.float32r
I32 = mybir.dt.int32
ALU = mybir.AluOpType
ACT = mybir.ActivationFunctionType
AXX = mybir.AxisListType.X

P = 128
T = 512
D = 1024
DK = D // P
FF = 2816
FK = FF // P
NT = T // P
NH = 8
DH = 64
GH = 4
CH = 64
NCH = T // CH
NCMP = (T - 32) // 16 + 1
NEG = -1.0e30
EPS = 1e-6
SLOT = 11 * P

STAGES = [
    ("in1", 15, 1, DK), ("fill1", 2 * DK, 1, DK), ("mix1", DK, 1, DK), ("out1", DK, 1, DK), ("up1", FK, 2, DK), ("down1", DK, 2, FK // 2),
    ("in2c", 12, 1, DK), ("in2z", 5, 1, DK), ("fill2", 12 + 2 * DK, 1, DK), ("mix2", DK, 1, DK), ("out2", DK, 1, DK), ("up2", FK, 2, DK),
    ("down2", DK, 2, FK // 2),
]

PIECES = 4


def fill_plan(steps):
    plan, total = {}, 0
    for name, n, num, den in steps:
        start = total
        for i in range(n):
            behind = start + num * (i + 1) // den
            plan[name, i] = (total, behind)
            total = behind
    return plan, total


FILL2, FILLED2 = fill_plan([("norm", 8, 2, 1), ("gates", 2, 3, 1), ("rows", 4, 2, 1), ("first", 4, 1, 1),
                            ("level", 20, 1, 1), ("chunk", 8, 1, 1), ("out", 2, 3, 1), ("turn", 4, 2, 1),
                            ("unit", 32, 9, 8)])
FILL1, FILLED1 = fill_plan([("norm", 6, 2, 1), ("turn", 3, 2, 1), ("compress", 5, 1, 1), ("scores", 2, 3, 1),
                            ("unit", 64, 35, 64)])
assert FILLED1 == PIECES * 2 * DK
assert FILLED2 == PIECES * (12 + 2 * DK)

CONST = {}
_at = 0
for _name, _n in (("ident", P), ("ones", P), ("halves", P), ("rot", P), ("causal", T), ("level", 6 * P),
                  ("decay", P), ("strict", P), ("pick", 2 * GH * P), ("cmp", NT * NCMP), ("reset", T),
                  ("count", 4 * 16), ("cmp_any", 1), ("inv", 1)):
    CONST[_name] = (_at, _n)
    _at += _n
N_CONST = _at

PARAM = {}
_at = 0
for _name, _n in (("gain", 5 * DK), ("q_gain", 1), ("k_gain", 3), ("pe", 2 * 32), ("pool_scale", 4),
                  ("conv1", FK * 4), ("conv2", 2 * FK * 4), ("conv_qkv", 12 * 4), ("gdn_gain", 1),
                  ("a_log", 1), ("dt_bias", 1)):
    PARAM[_name] = (_at, _n)
    _at += _n
N_PARAM = _at


def constants():
    c = np.zeros((P, N_CONST), np.float32)
    p = np.arange(P)[:, None]
    m = np.arange(P)[None, :]

    def put(name, value):
        at, n = CONST[name]
        c[:, at:at + n] = value

    put("ident", p == m)
    put("ones", 1.0)
    put("halves", p // DH == m // DH)
    rot = np.zeros((P, P), np.float32)
    for half in (0, DH):
        for d in range(8):
            rot[half + d + 8, half + d] = -1.0
            rot[half + d, half + d + 8] = 1.0
    put("rot", rot)
    put("causal", np.where(np.arange(T)[None, :] - (T - P) <= p, 0.0, NEG))
    lev = np.zeros((P, 6, P), np.float32)
    for s in range(6):
        w = 2 ** s
        lev[:, s] = (p // (2 * w) == m // (2 * w)) & (p // w % 2 == 0) & (m // w % 2 == 1)
    put("level", lev.reshape(P, -1))
    put("decay", np.where((p // CH == m // CH) & (m >= p), 0.0, NEG))
    put("strict", m > p)
    pick = np.zeros((P, 2 * GH, P), np.float32)
    for h in range(GH):
        pick[h, h] = 1.0
        pick[32 + h, GH + h] = 1.0
    put("pick", pick.reshape(P, -1))
    tok = (np.arange(NT)[None, :, None] * P + np.arange(P)[:, None, None])
    put("cmp", np.where(np.arange(NCMP)[None, None, :] * 16 + 31 <= tok, 0.0, NEG).reshape(P, -1))
    put("reset", np.arange(T)[None, :] % CH != 0)
    t = np.arange(16)
    put("count", np.stack([1.0 / np.minimum(t + 1, w) for w in (2, 4, 8, 16)]).reshape(1, -1))
    put("cmp_any", p >= 31)
    inv = np.zeros((P, 1), np.float32)
    freq = np.float32(500000.0) ** (-(np.arange(8, dtype=np.float32) * np.float32(2.0) / np.float32(16)))
    for half in (0, DH):
        inv[half:half + 8, 0] = freq
        inv[half + 8:half + 16, 0] = freq
    put("inv", inv)
    return c


def lin(a, b, i):
    return a + b * i if isinstance(i, int) else i * b + a


class Chunk:

    def __init__(self, first, half, i, index, loop):
        self.first, self.half, self.i, self.index, self.loop = first, half, i, index, loop
        self.slot = first % 2

    def count(self, more=0):
        return lin(self.first + more, 2 * self.half, self.i)

    def loads(self):
        return lin(16 * (self.first // 2 + 1), 16 * self.half, self.i)


def units(eng, n):
    full = n // 2
    for j in range(2):
        yield 0, j
    if full > 2:
        with eng.Fori(1, full - 1) as i:
            for j in range(2):
                yield i, j
    for u in range(2 * (full - 1), n):
        yield u // 2, u % 2


def chunk_table():
    base, at, sizes = {}, 0, []
    for name, n, per, kt in STAGES:
        base[name] = at
        sizes += [kt] * (n * per)
        at += n * per
    return base, sizes


def two_blocks(nc, t_in, out):
    BASE, SIZES = chunk_table()
    INFO = {name: (n, per, kt) for name, n, per, kt in STAGES}
    NCHUNK = len(SIZES)

    def chunk(name, i, j, q=0):
        n, per, kt = INFO[name]
        local = per * j + q
        return Chunk(BASE[name] + local, per, i, lin(local, 2 * per, i), not isinstance(i, int))

    ctx = ExitStack()
    with ctx:
        kb = 1024
        base = -(-nc.sbuf_base // 64) * 64

        def sb(name, shape, dt, at):
            return nc.alloc_sbuf_tensor_at(name, shape, dt, offset=base + int(at))

        def sem(name):
            return ctx.enter_context(nc.semaphore(name))

        at = 0
        w_raw = sb("w_raw", [P, 2, SLOT], F32, at); at += 2 * SLOT * 4
        w_hi = sb("w_hi", [P, 2, SLOT], F32R, at); at += 2 * SLOT * 4
        w_lo = sb("w_lo", [P, 2, SLOT], F32R, at); at += 2 * SLOT * 4
        X = sb("X", [P, DK, T], F32, at); at += DK * T * 4
        h_hi = sb("h_hi", [P, DK, T], F32R, at); at += DK * T * 4
        h_lo = sb("h_lo", [P, DK, T], F32R, at); at += DK * T * 4
        consts = sb("consts", [P, N_CONST], F32, at); at += -(-N_CONST * 4 // 64) * 64
        params = sb("params", [P, N_PARAM], F32, at); at += -(-N_PARAM * 4 // 64) * 64
        sq_sum = sb("sq_sum", [P, T], F32, at); at += T * 4
        rms_inv = sb("rms_inv", [P, T], F32, at); at += T * 4
        arena = at
        arena_size = (nc.sbuf_usable_end - base - arena) // 64 * 64

        def area(name, shape, dt, at_kb):
            n = 4 * int(np.prod(shape[1:]))
            assert at_kb * kb + n <= arena_size, (name, at_kb, n, arena_size)
            return sb(name, shape, dt, arena + at_kb * kb)

        def const(name, *shape):
            a, n = CONST[name]
            v = consts[:, a:a + n]
            if len(shape) == 2:
                v = v.rearrange("p (a b) -> p a b", a=shape[0])
            return v

        def param(name, a=0, n=None):
            at, size = PARAM[name]
            return params[:, at + a:at + a + (size - a if n is None else n)]

        ident, ones, halves = const("ident"), const("ones"), const("halves")

        sq_ring = area("sq_ring", [P, 2, T], F32, 97)
        hn = area("hn", [P, 2, T], F32, 101)
        rope = area("rope", [P, 2, T], F32, 84)
        angle = area("angle", [P, 3, T], F32, 62)
        pos_i = area("pos_i", [P, T], I32, 68)
        rel_row = area("rel_row", [NH, 257], F32, 70)
        rel_ext = area("rel_ext", [NH, 640], F32, 72)
        p1 = area("p1", [P, 15, T], F32, 0)
        KC, VC, VS, VW, KS, KW, GT = range(8, 15)
        cmp_w1 = area("cmp_w1", [P, 2, 32 * P], F32, 30)
        cmp_blk = area("cmp_blk", [P, 2, 32, 2, NCMP], F32, 62)
        nr_sq = area("nr_sq", [P, 2, T], F32, 62)
        nr_r = area("nr_r", [P, 2, T], F32, 66)
        nr_c = area("nr_c", [P, 2, T], F32, 70)
        nr_s = area("nr_s", [P, 2, T], F32, 74)
        v1_nat = area("v1_nat", [P, 2, NT, P], F32, 78)
        pool_w = area("pool_w", [P, 4, P], F32, 82)
        pool_pad = area("pool_pad", [P, 2, 16 + T], F32, 88)
        cmp_w2 = area("cmp_w2", [P, 2, DH], F32, 92.25)
        gate_t = area("gate_t", [P, NT, 24], F32, 92.75)
        hid = area("hid", [2 * NCMP, 2, P], F32, 93.25)
        hid_t = area("hid_t", [P, 2, 2 * NCMP], F32, 94.25)
        kc_t = area("kc_t", [P, NCMP], F32, 94.75)
        vc_nat = area("vc_nat", [NCMP, 2, DH], F32, 95)
        cmp_red = area("cmp_red", [P, 3, 4 * NT * 2], F32, 95.5)
        cmp_s = area("cmp_s", [P, 2, NT, 4, NCMP], F32, 96)
        kc_tmp = area("kc_tmp", [P, 4, NCMP], F32, 100)
        cols1 = area("cols1", [P, 12], F32, 100.5)
        pc_t = area("pc_t", [NCMP, NT * NH, P], F32, 30)
        at1_sm = area("at1_sm", [P, 2, T], F32, 62)
        at1_p = area("at1_p", [P, 3, T], F32, 66)
        at1_pt = area("at1_pt", [P, 2, T], F32, 72)
        o1_hi = area("o1_hi", [P, 4, T], F32R, 46)
        o1_lo = area("o1_lo", [P, 4, T], F32R, 54)
        yp_hi = area("yp_hi", [P, 4, T], F32R, 0)
        yp_lo = area("yp_lo", [P, 4, T], F32R, 16)
        sg1 = area("sg1", [P, 2, 2, T], F32, 82)
        mt1 = area("mt1", [P, 3, T], F32, 8)
        stage1 = area("stage1", [P, 2, T], F32, 101)
        mix1_hi = area("mix1_hi", [P, DK, T], F32R, 24)
        mix1_lo = area("mix1_lo", [P, DK, T], F32R, 62)
        act_hi = area("act_hi", [P, FK, T], F32R, 0)
        act_lo = area("act_lo", [P, FK, T], F32R, 44)
        t_gate = area("t_gate", [P, 2, T], F32, 88)
        t_val = area("t_val", [P, 2, T], F32, 92)
        p2a = area("p2a", [P, 17, T], F32, 0)
        cv = area("cv", [P, 2, T], F32, 74)
        l2_sq = area("l2_sq", [P, 2, T], F32, 78)
        l2_r = area("l2_r", [P, 2, T], F32, 82)
        a_t = area("a_t", [P, GH, NT, P], F32, 34)
        x_inv = area("x_inv", [P, GH, NT, P], F32, 42)
        y_inv = area("y_inv", [P, GH, NT, P], F32, 50)
        p_t = area("p_t", [P, GH, NT, P], F32, 58)
        k_dec = area("k_dec", [P, GH, NT, P], F32, 66)
        gam_row = area("gam_row", [P, T], F32, 74)
        dec = area("dec", [P, NT, P], F32, 76)
        beta_strict = area("beta_strict", [P, NT, P], F32, 78)
        b_t = area("b_t", [P, 2, NT, P], F32, 80)
        bx = area("bx", [P, 2, NT, P], F32, 84)
        state = area("state", [P, 2, GH, P], F32, 88)
        u_new = area("u_new", [P, 2, GH, P], F32, 92)
        gd_cols = area("gd_cols", [P, NT, 64], F32, 96)
        gd_neg = area("gd_neg", [P, NT, GH], F32, 97)
        gd_bg = area("gd_bg", [P, NT, GH], F32, 97.25)
        gd_kd = area("gd_kd", [P, GH, NT], F32, 97.5)
        gd_last = area("gd_last", [P, GH, NCH], F32, 97.75)
        o_red = area("o_red", [P, NT * GH], F32, 98)
        gb_rows = area("gb_rows", [64, T], F32, 99)
        gz = area("gz", [64, T], F32, 42)
        gz2 = area("gz2", [64, T], F32, 44)
        stage2 = area("stage2", [P, 2, T], F32, 101)
        ea = area("ea", [64, 2], F32, 105)
        k_bg = p2a[:, 4:8, :].rearrange("p h (c d) -> p h c d", c=NT)
        v_b = p2a[:, 8:12, :].rearrange("p h (c d) -> p h c d", c=NT)
        w_t, uv = x_inv, a_t
        o_nat = p2a[:, 4:8, :].rearrange("p c (h d) -> p c h d", h=GH)
        o_sq = p2a[:, 8:12, :].rearrange("p c (h d) -> p c h d", h=GH)
        oa = area("oa", [P, 2, T], F32, 34)
        oa_hi = area("oa_hi", [P, 4, T], F32R, 58)
        oa_lo = area("oa_lo", [P, 4, T], F32R, 66)
        p2b = area("p2b", [P, 12, T], F32, 0)
        rel = area("rel", [P, NH, T], F32, 24)
        v2_nat = area("v2_nat", [P, NT, T], F32, 40)
        at2_sm = area("at2_sm", [P, 2, T], F32, 74)
        at2_p = area("at2_p", [P, 3, T], F32, 78)
        at2_pt = area("at2_pt", [P, 2, T], F32, 84)
        cols2 = area("cols2", [P, 12], F32, 56)
        ob_hi = area("ob_hi", [P, 4, T], F32R, 48)
        ob_lo = area("ob_lo", [P, 4, T], F32R, 88)
        sg2 = area("sg2", [P, 2, 2, T], F32, 16)
        mt2 = area("mt2", [P, 3, T], F32, 40)
        mix2_hi = area("mix2_hi", [P, DK, T], F32R, 0)
        mix2_lo = area("mix2_lo", [P, DK, T], F32R, 24)

        banks = ctx.enter_context(nc.psum_tensor("banks", [P, 8, T], F32))
        ACC, BS, BT, BO = 0, 2, 4, 6
        POOLED = (BS + 1, BT + 1)

        def bank(n, shape=None):
            v = banks[:, n, :]
            return v.rearrange("p (a b) -> p a b", a=shape) if shape else v

        late1 = nc.dram_tensor("late1_scratch", (DK, 2, P, T), F32, kind="Internal").ap()
        late2 = nc.dram_tensor("late2_scratch", (6 + DK, 2, P, T), F32, kind="Internal").ap()
        rel_dram = nc.dram_tensor("rel_scratch", (NH, 640), F32, kind="Internal").ap()

        w_loaded = [sem(f"w_loaded{s}") for s in range(2)]
        hi_ready = sem("hi_ready")
        lo_ready = sem("lo_ready")
        chunk_done = sem("chunk_done")
        first_half = [sem(f"first_half{b}") for b in (1, 2)]
        consts_in = sem("consts_in")
        x_in = [sem(f"x_in{q}") for q in range(4)]
        pos_in, rel_in, cmp_in = sem("pos_in"), sem("rel_in"), sem("cmp_in")
        rel_stored, rel_loaded = sem("rel_stored"), sem("rel_loaded")
        start_step = sem("start_step")
        sin_done = sem("sin_done")
        copied = {n: sem("copied_" + n) for n in ("in1", "in2z")}
        filled = [sem("filled1"), sem("filled2")]
        late_stored = [[sem(f"late_stored{b}{s}") for s in range(2)] for b in (1, 2)]
        gate_in = [[sem(f"gate_in{b}{s}") for s in range(2)] for b in (1, 2)]
        qkv_in = {n: sem(n + "2_in") for n in "qkv"}
        x_done = sem("x_done")
        sq_done = sem("sq_done")
        sum_done = sem("sum_done")
        mean_done = sem("mean_done")
        ln_done = sem("ln_done")
        inv_done = sem("inv_done")
        hn_done = sem("hn_done")
        hh_done = sem("hh_done")
        hl_done = sem("hl_done")
        out_stored = [sem("out_stored0"), sem("out_stored1")]
        gate_sig = [sem(f"gate_sig{b}") for b in (1, 2)]
        y_pool_done = [sem(f"y_first{b}") for b in (1, 2)]
        y_nsa_done = [sem(f"y_second{b}") for b in (1, 2)]
        mixed = [sem(f"mixed{b}") for b in (1, 2)]
        mix_hh = [sem(f"mix_hh{b}") for b in (1, 2)]
        mix_hl = [sem(f"mix_hl{b}") for b in (1, 2)]
        conv_done = [sem(f"conv_done{b}") for b in (1, 2)]
        silu_done = [sem(f"silu_done{b}") for b in (1, 2)]
        gated = [sem(f"gated{b}") for b in (1, 2)]
        act_hh = [sem(f"act_hh{b}") for b in (1, 2)]
        act_hl = [sem(f"act_hl{b}") for b in (1, 2)]
        cv_done, cv_silu = sem("cv_done"), sem("cv_silu")
        n_sq, n_ms, n_ln, n_inv, n_gain = (sem("n_" + x) for x in ("sq", "ms", "ln", "inv", "gain"))
        n_rot, n_cos, n_sin, n_sum = (sem("n_" + x) for x in ("rot", "cos", "sin", "sum"))
        l_sq, l_ms, l_ln, l_inv, l_out = (sem("l_" + x) for x in ("sq", "ms", "ln", "inv", "out"))
        turned = [sem(f"turned{b}") for b in (1, 2)]
        v_copied = [sem(f"v_copied{b}") for b in (1, 2)]
        gates_ready = sem("gates_ready")
        pad_zero, blk_zero = sem("pad_zero"), sem("blk_zero")
        pooled = sem("pooled")
        pool_mul = sem("pool_mul")
        yp_h, yp_l = sem("yp_h"), sem("yp_l")
        blk_done = sem("blk_done")
        c_pe, c_act, c_dve = sem("c_pe"), sem("c_act"), sem("c_dve")
        s_pe, s_act, s_dve = sem("s_pe"), sem("s_act"), sem("s_dve")

        class Attention:

            def __init__(self, b, units_, per_tile, sm, p, pt, cols, o_hi, o_lo):
                self.units, self.per_tile = units_, per_tile
                self.sm, self.p, self.pt, self.o_hi, self.o_lo = sm, p, pt, o_hi, o_lo
                self.nbias, self.sums, self.inv = cols[:, 0:4], cols[:, 4:8], cols[:, 8:12]
                self.scored = sem(f"scored{b}")
                self.masked = sem(f"masked{b}")
                self.shifted = sem(f"shifted{b}")
                self.exped = sem(f"exped{b}")
                self.inverted = sem(f"inverted{b}")
                self.weighted = sem(f"weighted{b}")
                self.flipped = sem(f"flipped{b}")
                self.fetched = sem(f"fetched{b}")
                self.summed = sem(f"summed{b}")
                self.high = sem(f"o_high{b}")
                self.low = sem(f"o_low{b}")

        att1 = Attention(1, [(j, i, b, half) for j in range(4) for i in range(NT) for b in range(2)
                             for half in range(2)], 4 * NT, at1_sm, at1_p, at1_pt, cols1, o1_hi, o1_lo)
        att2 = Attention(2, [(j, i, 0, half) for j in range(4) for i in range(NT) for half in range(2)],
                         2 * NT, at2_sm, at2_p, at2_pt, cols2, ob_hi, ob_lo)
        d_pe, d_dve, d_act = sem("d_pe"), sem("d_dve"), sem("d_act")
        g_pe, g_dve, g_act = sem("g_pe"), sem("g_dve"), sem("g_act")
        i_mask, i_bx, i_cp, i_pe, i_x, i_y = (sem("i_" + x) for x in ("mask", "bx", "cp", "pe", "x", "y"))
        r_w, r_cp, r_ws, r_u, r_ds, r_s, r_o, r_ocp = (
            sem("r_" + x) for x in ("w", "cp", "ws", "u", "ds", "s", "o", "ocp"))
        f_dve, f_act, f_pe = sem("f_dve"), sem("f_act"), sem("f_pe")
        oa_h, oa_l = sem("oa_h"), sem("oa_l")

        LATE_BANK = (1, 1)

        block = ctx.enter_context(nc.Block())

        def level(n):
            return const("level", 6, P)[:, n, :].unsqueeze(1).to_broadcast([P, NT, P])

        def rows(half):
            return slice(half * DH, (half + 1) * DH)

        def ahead(c, q_kt):
            if c.loop:
                return Chunk(c.first + 2, c.half, c.i, None, True), q_kt
            n = c.count() + 2
            return (Chunk(n, 0, 0, None, False), SIZES[n]) if n < NCHUNK else (None, 0)

        def wait(eng, s, value):
            if not isinstance(value, int) or value > 0:
                eng.wait_ge(s, value)

        @block.sync
        def _(sp):
            for q in range(4):
                sp.dma_start(X[:, 2 * q:2 * q + 2, :], t_in["x"][:, 2 * q:2 * q + 2, :]).then_inc(x_in[q], 16)
            def load(c, name, kt):
                wait(sp, lo_ready, c.count(-1))
                sp.dma_start(w_raw[:, c.slot, 0:kt * P], t_in["w_" + name][c.index]).then_inc(w_loaded[c.slot], 16)

            def store_late(b, late, stage, n):
                sp.wait_ge(filled[b], n + 1)
                sp.dma_start(late[n // 2, n % 2], stage[:, n % 2, :]).then_inc(late_stored[b][n % 2], 16)

            def late(name, b, scratch, stage):
                n = INFO[name][0]
                for c in range(n):
                    load(chunk(name, c // 2, c % 2), name, DK)
                    if c >= 3:
                        store_late(b, scratch, stage, c - 3)

            def merge(name, b, last, late_, scratch, stage, first_gate, sg):
                n = INFO[late_][0]

                def gates(m, j):
                    sp.dma_start(sg[:, j, :, :], scratch.rearrange("n a p t -> n p a t")[m + first_gate])\
                        .then_inc(gate_in[b][j], 16)

                for i, j in units(sp, DK):
                    load(chunk(name, i, j), name, DK)
                    m = lin(j, 2, i)
                    if isinstance(m, int) and m == 0:
                        store_late(b, scratch, stage, n - 3)
                    elif isinstance(m, int) and m == 1:
                        store_late(b, scratch, stage, n - 2)
                        store_late(b, scratch, stage, n - 1)
                        sp.wait_ge(late_stored[b][0], 16 * ((n + 1) // 2))
                        sp.wait_ge(late_stored[b][1], 16 * (n // 2))
                        last()
                        gates(0, 0)
                        gates(1, 1)
                    else:
                        sp.wait_ge(y_nsa_done[b], m - 1)
                        gates(m, j)

            for name, n, per, kt in STAGES:
                if name == "fill1":
                    late(name, 0, late1, stage1)
                elif name == "mix1":
                    merge(name, 0, lambda: sp.wait_ge(pool_mul, 4), "fill1", late1, stage1, 0, sg1)
                elif name == "fill2":
                    late(name, 1, late2, stage2)
                elif name == "mix2":
                    merge(name, 1, lambda: sp.wait_ge(turned[1], 4), "fill2", late2, stage2, 6, sg2)
                else:
                    for i, j in units(sp, n):
                        for q in range(per):
                            load(chunk(name, i, j, q), name, kt)
            for m in range(DK):
                sp.wait_ge(hn_done, 4 * DK + m + 1)
                sp.dma_start(out[:, m, :], hn[:, m % 2, :]).then_inc(out_stored[m % 2], 16)
            sp.wait_ge(out_stored[0], 16 * DK // 2)
            sp.wait_ge(out_stored[1], 16 * DK // 2)

        @block.gpsimd
        def _(pool):
            def low(c, kt):
                pool.wait_ge(hi_ready, c.count(1))
                pool.tensor_tensor(w_lo[:, c.slot, 0:kt * P], w_raw[:, c.slot, 0:kt * P],
                                   w_hi[:, c.slot, 0:kt * P], ALU.subtract).then_inc(lo_ready, 1)

            def split(name):
                n, per, kt = INFO[name]
                for i, j in units(pool, n):
                    for q in range(per):
                        c2, kt2 = ahead(chunk(name, i, j, q), kt)
                        if c2:
                            low(c2, kt2)

            step = [0]

            def pool_step(ins):
                step[0] += 1
                ins.then_inc(pooled, 1)
                pool.wait_ge(pooled, step[0])

            def pooling(gi):
                w, cur, u = 2 ** (gi + 1), 0, p1[:, gi, :]
                pool_step(pool.tensor_copy(pool_pad[:, 0, 16:], u))
                d = 1
                while d < w:
                    pool_step(pool.tensor_tensor(pool_pad[:, 1 - cur, 16:], pool_pad[:, cur, 16:],
                                                 pool_pad[:, cur, 16 - d:16 + T - d], ALU.add))
                    cur, d = 1 - cur, 2 * d
                s, m = pool_pad[:, cur, :], pool_pad[:, 1 - cur, :]
                pool_step(pool.tensor_scalar(m[:, 32:], s[:, 32:], 1.0 / w, None, ALU.mult))
                pool_step(pool.tensor_tensor(m[:, 16:32], s[:, 16:32], const("count", 4, 16)[:, gi, :], ALU.mult))
                pool_step(pool.tensor_tensor(u, m[:, 16:], u, ALU.subtract))

            def lows(name, plan, total):
                state = [0]

                def serve(*at):
                    upto = (plan[at][0] if at else total) // PIECES
                    while state[0] < upto:
                        low(*ahead(chunk(name, state[0] // 2, state[0] % 2), DK))
                        state[0] += 1
                return serve

            def weights(a, gated_, serve=None):
                for u, (j, i, b, half) in enumerate(a.units):
                    w = (i + 1) * P
                    pr = a.p[:, u % 3, 0:w]
                    pool.wait_ge(a.inverted, u + 1)
                    if gated_:
                        g = (j + 4 * half) * 3 + 1 + b
                        ins = pool.tensor_scalar(pr, pr, a.inv[:, u % 4:u % 4 + 1], gate_t[:, i, g:g + 1],
                                                 ALU.mult, ALU.mult)
                    else:
                        ins = pool.tensor_scalar(pr, pr, a.inv[:, u % 4:u % 4 + 1], None, ALU.mult)
                    ins.then_inc(a.weighted, 1)
                    if serve:
                        serve("unit", u)

            low(Chunk(0, 0, 0, None, False), DK)
            low(Chunk(1, 0, 0, None, False), DK)
            split("in1")
            pool.wait_ge(copied["in1"], 15)
            pool.wait_ge(consts_in, 32)
            pool.memset(pool_pad[:, :, 0:16], 0.0).then_inc(pad_zero, 1)
            pool.wait_ge(pad_zero, 1)
            serve = lows("fill1", FILL1, FILLED1)
            serve("norm", 2)
            pooling(0)
            serve("norm", 4)
            pooling(1)
            serve("norm", 5)
            pool.wait_ge(n_sum, 6)
            pool.memset(cmp_blk[:, :, :, :, :], 0.0).then_inc(blk_zero, 1)
            serve("turn", 2)
            pooling(2)
            pooling(3)
            serve("compress", 4)
            serve("scores", 0)
            serve("scores", 1)
            weights(att1, True, serve)
            serve()
            for name in ("mix1", "out1", "up1", "down1", "in2c", "in2z"):
                split(name)
            pool.wait_ge(copied["in2z"], 5)
            pool.memset(gb_rows[:, :], 0.0).then_inc(blk_zero, 1)
            serve = lows("fill2", FILL2, FILLED2)
            for h in range(GH):
                serve("first", h)
                if h == 0:
                    pool.wait_ge(d_dve, 11 * GH)
                wait(pool, i_bx, h - 1)
                wait(pool, i_y, h - 1)
                pool.tensor_tensor(b_t[:, h % 2, :, :], a_t[:, h, :, :], level(0), ALU.mult).then_inc(i_mask, 1)
            pool.wait_ge(i_y, GH)
            for k in range(5 * GH):
                pool.wait_ge(i_bx, GH + k - 1)
                pool.tensor_tensor(b_t[:, k % 2, :, :], a_t[:, k % GH, :, :], level(1 + k // GH), ALU.mult)\
                    .then_inc(i_mask, 1)
                serve("level", k)
            for c in range(NCH):
                serve("chunk", c)
            for n in range(2):
                serve("out", n)
            for v in range(4):
                serve("turn", v)
            pool.wait_ge(rel_loaded, 16 * NH)
            pool.memset(rel[0:CH, :, 0:CH], NEG).then_inc(blk_zero, 1)
            weights(att2, False, serve)
            serve()
            for name in ("mix2", "out2", "up2", "down2"):
                split(name)

        @block.scalar
        def _(act):
            def high(c, kt):
                act.wait_ge(w_loaded[c.slot], c.loads())
                wait(act, chunk_done, c.count(-1))
                act.activation(w_hi[:, c.slot, 0:kt * P], w_raw[:, c.slot, 0:kt * P], ACT.Copy)\
                    .then_inc(hi_ready, 1)

            def next_high(name, i, j, q=0):
                c2, kt2 = ahead(chunk(name, i, j, q), INFO[name][2])
                if c2:
                    high(c2, kt2)

            def plain(name):
                for i, j in units(act, INFO[name][0]):
                    next_high(name, i, j)

            def late(name, b, plan, total, stage):
                state = [0]

                def serve(*at):
                    upto = (plan[at][0] if at else total) // PIECES
                    while state[0] < upto:
                        n = state[0]
                        next_high(name, n // 2, n % 2)
                        act.wait_ge(chunk_done, chunk(name, n // 2, n % 2).count(1))
                        wait(act, late_stored[b][n % 2], 16 * (n // 2))
                        act.activation(stage[:, n % 2, :], bank(ACC + (n + LATE_BANK[b]) % 2), ACT.Copy)\
                            .then_inc(filled[b], 1)
                        state[0] += 1
                return serve

            def logs_and_exps():
                act.preload_act_table_set("natural_log_exp_and_others")

            def norm(n):
                logs_and_exps()
                act.wait_ge(mean_done, n + 1)
                act.activation(rms_inv[:, :], bank(BS), ACT.Ln, bias=EPS, scale=1.0 / D).then_inc(ln_done, 1)
                act.wait_ge(ln_done, n + 1)
                act.activation(rms_inv[:, :], rms_inv[:, :], ACT.Exp, scale=-0.5).then_inc(inv_done, 1)
                if n < 4:
                    for m in range(DK):
                        act.wait_ge(hn_done, DK * n + m + 1)
                        act.activation(h_hi[:, m, :], hn[:, m % 2, :], ACT.Copy).then_inc(hh_done, 1)

            def residual(name, n):
                for i, j in units(act, DK):
                    for q in range(INFO[name][1]):
                        next_high(name, i, j, q)
                    act.wait_ge(x_done, lin(DK * (n - 1) + j + 1, 2, i))
                    wait(act, sum_done, lin(DK * n + j - 1, 2, i))
                    act.activation(sq_ring[:, j, :], X[:, lin(j, 2, i), :], ACT.Square).then_inc(sq_done, 1)

            def merge(name, b, sg, mt, mix_hi):
                for i, j in units(act, DK):
                    m = lin(j, 2, i)
                    act.wait_ge(gate_in[b][j], lin(16, 16, i))
                    act.activation(sg[:, j, :, :], sg[:, j, :, :], ACT.Sigmoid).then_inc(gate_sig[b], 1)
                    next_high(name, i, j)
                    act.wait_ge(mixed[b], lin(j + 1, 2, i))
                    act.activation(mix_hi[:, m, :], mt[:, 2, :], ACT.Copy).then_inc(mix_hh[b], 1)

            def ffn(name, b, steps):
                for i, j in units(act, FK):
                    next_high(name, i, j, 0)
                    act.wait_ge(conv_done[b], lin(steps * j + 3, 2 * steps, i))
                    act.activation(t_gate[:, j, :], t_gate[:, j, :], ACT.Silu).then_inc(silu_done[b], 1)
                    next_high(name, i, j, 1)
                    act.wait_ge(gated[b], lin(j + 1, 2, i))
                    act.activation(act_hi[:, lin(j, 2, i), :], t_gate[:, j, :], ACT.Copy).then_inc(act_hh[b], 1)

            def inverse_roots(tiles, sq, rt, s_sq, s_ms, s_ln, s_inv, s_used, scale, serve=None):
                logs_and_exps()

                def square(n):
                    wait(act, s_ms, n - 1)
                    act.activation(sq[:, n % 2, :], tiles[n], ACT.Square).then_inc(s_sq, 1)
                square(0)
                square(1)
                for n in range(len(tiles)):
                    act.wait_ge(s_ms, n + 1)
                    wait(act, s_used, n - 1)
                    act.activation(rt[:, n % 2, :], bank(BS + n % 2), ACT.Ln, bias=EPS, scale=scale)\
                        .then_inc(s_ln, 1)
                    act.wait_ge(s_ln, n + 1)
                    act.activation(rt[:, n % 2, :], rt[:, n % 2, :], ACT.Exp, scale=-0.5).then_inc(s_inv, 1)
                    if serve:
                        serve("norm", n)
                    if n + 2 < len(tiles):
                        square(n + 2)

            def attention(a, serve=None):
                n = len(a.units)
                for s in range(n + 5):
                    if s < n:
                        w = (a.units[s][1] + 1) * P
                        act.wait_ge(a.shifted, s + 1)
                        wait(act, a.flipped, s - 2)
                        act.activation(a.p[:, s % 3, 0:w], a.sm[:, s % 2, 0:w], ACT.Exp,
                                       bias=a.nbias[:, s % 4:s % 4 + 1], scale=DH ** -0.5,
                                       accum_out=a.sums[:, s % 4:s % 4 + 1]).then_inc(a.exped, 1)
                    u = s - 2
                    if 0 <= u < n:
                        w = (a.units[u][1] + 1) * P
                        act.wait_ge(a.flipped, u + 1)
                        wait(act, a.summed, u - 1)
                        act.activation(a.pt[:, u % 2, 0:w], banks[:, BT + u % 2, 0:w], ACT.Copy)\
                            .then_inc(a.fetched, 1)
                    if serve and s < n:
                        serve("unit", s)
                    u = s - 4
                    if 0 <= u < n and u % a.per_tile == a.per_tile - 1:
                        j = u // a.per_tile
                        act.wait_ge(a.summed, u + 1)
                        act.activation(a.o_hi[:, j, :], bank(BO + j % 2), ACT.Copy).then_inc(a.high, 1)

            def fetch(n, first):
                act.dma_start(p2b[:, first:first + 4, :].rearrange("p (n a) t -> p n a t", a=2),
                              late2[first // 2:first // 2 + 2].rearrange("n a p t -> p n a t"))\
                    .then_inc(qkv_in[n], 16)

            act.dma_start(consts[:, :], t_in["consts"]).then_inc(consts_in, 16)
            act.dma_start(params[:, :], t_in["params"]).then_inc(consts_in, 16)
            act.dma_start(pos_i[:, :], t_in["positions"].partition_broadcast(P)).then_inc(pos_in, 16)
            act.dma_start(rel_row[:, :], t_in["rel"]).then_inc(rel_in, 16)
            act.dma_start(cmp_w2[:, :, :], t_in["cmp_w2"]).then_inc(cmp_in, 16)
            act.dma_start(pool_w[:, :, :], t_in["pool_w"]).then_inc(cmp_in, 16)
            for half in range(2):
                act.dma_start(cmp_w1[rows(half), :, :], t_in["cmp_w1"]).then_inc(cmp_in, 16)
            act.wait_ge(start_step, 9)
            act.activation(rope[:, 1, :], angle[:, 1, :], ACT.Sin).then_inc(sin_done, 1)
            act.activation(rope[:, 0, :], angle[:, 2, :], ACT.Sin).then_inc(sin_done, 1)
            act.wait_ge(start_step, 11)
            act.dma_start(rel_dram, rel_ext[:, :]).then_inc(rel_stored, 16)
            for m in range(DK):
                act.wait_ge(x_in[m // 2], 16)
                wait(act, sum_done, m - 1)
                act.activation(sq_ring[:, m % 2, :], X[:, m, :], ACT.Square).then_inc(sq_done, 1)
            high(Chunk(0, 0, 0, None, False), DK)
            high(Chunk(1, 0, 0, None, False), DK)
            norm(0)
            plain("in1")

            act.wait_ge(copied["in1"], 15)
            act.activation(p1[0:24, GT, :], p1[0:24, GT, :], ACT.Sigmoid).then_inc(gates_ready, 1)
            serve = late("fill1", 0, FILL1, FILLED1, stage1)
            inverse_roots([p1[:, t, :] for t in (4, 5, 6, 7, KS, KW)], nr_sq, nr_r, n_sq, n_ms, n_ln, n_inv,
                          n_gain, 1.0 / DH, serve)
            for v in range(2):
                serve("turn", v)
                act.wait_ge(turned[0], v + 1)
                act.activation(v1_nat[:, v, :, :], bank(BO + v, NT), ACT.Copy).then_inc(v_copied[0], 1)
            act.wait_ge(turned[0], 3)
            act.activation(gate_t[:, :, :], banks[:, BT, 0:NT * 24].rearrange("p (a b) -> p a b", a=NT),
                           ACT.Copy).then_inc(v_copied[0], 1)
            serve("turn", 2)
            for c in range(2):
                act.wait_ge(c_pe, c + 1)
                act.activation(hid[:, c, :], banks[0:2 * NCMP, BS + c, 0:P], ACT.Silu).then_inc(c_act, 1)
            serve("compress", 0)
            for c in range(2):
                act.wait_ge(c_pe, c + 3)
                act.activation(hid_t[:, c, :], banks[:, BT + c, 0:2 * NCMP], ACT.Copy).then_inc(c_act, 1)
            serve("compress", 1)
            act.wait_ge(c_pe, 5)
            act.activation(kc_tmp[:, 0, :], banks[:, BO, 0:NCMP], ACT.Square).then_inc(c_act, 1)
            act.wait_ge(c_pe, 6)
            act.activation(vc_nat[:, :, :], banks[0:NCMP, BO + 1, 0:2 * DH].rearrange("p (a b) -> p a b", a=2),
                           ACT.Copy).then_inc(c_act, 1)
            serve("compress", 2)
            logs_and_exps()
            act.wait_ge(c_pe, 7)
            act.activation(kc_tmp[:, 1, :], banks[:, BS, 0:NCMP], ACT.Ln, bias=EPS, scale=1.0 / DH)\
                .then_inc(c_act, 1)
            act.wait_ge(c_act, 7)
            act.activation(kc_tmp[:, 1, :], kc_tmp[:, 1, :], ACT.Exp, scale=-0.5).then_inc(c_act, 1)
            serve("compress", 3)
            for gi in range(4):
                act.wait_ge(pool_mul, gi + 1)
                act.activation(yp_hi[:, gi, :], bank(POOLED[gi % 2]), ACT.Copy, scale=param("pool_scale", gi, 1))\
                    .then_inc(yp_h, 1)
            serve("compress", 4)
            act.wait_ge(s_dve, 4)
            act.activation(cmp_s[:, :, :, :, :], cmp_s[:, :, :, :, :], ACT.Exp, scale=DH ** -0.5).then_inc(s_act, 1)
            serve("scores", 0)
            serve("scores", 1)
            for r in range(8):
                act.wait_ge(s_pe, 3 + r)
                act.activation(pc_t[:, 4 * r:4 * r + 4, :], banks[0:NCMP, BT + r % 2, :].rearrange(
                    "p (a b) -> p a b", a=4), ACT.Copy).then_inc(s_act, 1)
            attention(att1, serve)
            serve()
            merge("mix1", 0, sg1, mt1, mix1_hi)
            residual("out1", 1)
            norm(1)
            ffn("up1", 0, 3)
            residual("down1", 2)

            norm(2)
            for i, j in units(act, 12):
                next_high("in2c", i, j)
                act.wait_ge(cv_done, lin(4 * j + 4, 8, i))
                act.activation(p2a[:, lin(j, 2, i), :], cv[:, j, :], ACT.Silu).then_inc(cv_silu, 1)
            plain("in2z")
            serve = late("fill2", 1, FILL2, FILLED2, stage2)
            inverse_roots([p2a[:, t, :] for t in range(8)], l2_sq, l2_r, l_sq, l_ms, l_ln, l_inv, l_out, 1.0, serve)
            g = slice(32, 32 + GH)
            act.wait_ge(g_dve, 2)
            act.activation(gz2[g, :], gz2[g, :], ACT.Exp, scale=-1.0).then_inc(g_act, 1)
            act.wait_ge(g_act, 1)
            act.activation(gz2[g, :], gz2[g, :], ACT.Ln, bias=1.0).then_inc(g_act, 1)
            act.activation(ea[g, 0:1], params[g, PARAM["a_log"][0]:PARAM["a_log"][0] + 1], ACT.Exp)\
                .then_inc(g_act, 1)
            act.wait_ge(blk_zero, 2)
            act.activation(gb_rows[0:GH, :], p2a[0:GH, 16, :], ACT.Sigmoid).then_inc(g_act, 1)
            serve("gates", 0)
            act.wait_ge(g_pe, 1)
            act.activation(gd_cols[:, :, :], banks[:, BO, 0:NT * 64].rearrange("p (a b) -> p a b", a=NT),
                           ACT.Copy).then_inc(g_act, 1)
            act.wait_ge(g_act, 5)
            act.activation(gd_bg[:, :, :], gd_cols[:, :, 32:32 + GH], ACT.Exp).then_inc(g_act, 1)
            serve("gates", 1)
            act.wait_ge(g_dve, 7)
            for h in range(GH):
                act.wait_ge(d_pe, 6 * h + 1)
                wait(act, d_dve, 11 * (h - 1) + 5 if h else 0)
                wait(act, d_act, 7 * h)
                act.activation(gam_row[:, :], bank(BS), ACT.Exp).then_inc(d_act, 1)
                act.wait_ge(d_dve, 11 * h + 1)
                for p in range(NT):
                    act.activation(dec[:, p, :], dec[:, p, :], ACT.Exp, bias=gd_neg[:, p, h:h + 1])\
                        .then_inc(d_act, 1)
                act.wait_ge(d_dve, 11 * h + 3)
                act.activation(gd_kd[:, h, :], gd_kd[:, h, :], ACT.Exp).then_inc(d_act, 1)
                act.wait_ge(d_act, 7 * h + 1)
                act.activation(gd_last[:, h, :], gam_row[:, CH - 1:T:CH], ACT.Copy).then_inc(d_act, 1)
                serve("rows", h)
            for h in range(GH):
                serve("first", h)
            for k in range(5 * GH):
                act.wait_ge(i_bx, GH + k + 1)
                wait(act, i_pe, 2 * (k - 1))
                act.activation(bx[:, k % 2, :, :], bank(BT + k % 2, NT), ACT.Copy).then_inc(i_cp, 1)
                serve("level", k)
            for h in range(GH):
                act.wait_ge(r_w, 2 * h + 1)
                act.activation(w_t[:, h, :, :], bank(BT + h % 2, NT), ACT.Copy).then_inc(r_cp, 1)
                act.wait_ge(r_w, 2 * h + 2)
                act.activation(uv[:, h, :, :], bank(BO + h % 2, NT), ACT.Copy).then_inc(r_cp, 1)
            act.activation(p2a[:, 12:16, :], p2a[:, 12:16, :], ACT.Silu).then_inc(f_act, 1)
            for p in range(NT):
                serve("chunk", 2 * p)
                serve("chunk", 2 * p + 1)
                act.wait_ge(r_o, 2 * p + 2)
                act.activation(o_nat[:, p, :, :], bank(BO + p % 2, GH), ACT.Copy).then_inc(r_ocp, 1)
            logs_and_exps()
            act.wait_ge(r_ocp, NT)
            act.activation(o_sq, o_nat, ACT.Square).then_inc(f_act, 1)
            act.wait_ge(late_stored[1][0], 16 * 6)
            act.wait_ge(late_stored[1][1], 16 * 6)
            fetch("q", 0)
            act.wait_ge(f_dve, 1)
            fetch("v", 8)
            act.activation(o_red[:, :], o_red[:, :], ACT.Ln, bias=EPS, scale=1.0 / P).then_inc(f_act, 1)
            act.wait_ge(f_act, 3)
            act.activation(o_red[:, :], o_red[:, :], ACT.Exp, scale=-0.5).then_inc(f_act, 1)
            serve("out", 0)
            for h in range(GH):
                act.wait_ge(f_dve, 3 + h)
                act.activation(oa_hi[:, h, :], oa[:, h % 2, :], ACT.Copy).then_inc(oa_h, 1)
            fetch("k", 4)
            act.wait_ge(rel_stored, 16)
            act.wait_ge(oa_l, GH)
            for h in range(NH):
                act.dma_start(rel[:, h, :], diagonals(rel_dram, h)).then_inc(rel_loaded, 16)
            serve("out", 1)
            for v in range(4):
                serve("turn", v)
                act.wait_ge(turned[1], v + 1)
                act.activation(v2_nat[:, :, v * P:(v + 1) * P], bank(BO + v % 2, NT), ACT.Copy)\
                    .then_inc(v_copied[1], 1)
            attention(att2, serve)
            serve()
            merge("mix2", 1, sg2, mt2, mix2_hi)
            residual("out2", 3)
            norm(3)
            ffn("up2", 1, 6)
            residual("down2", 4)
            norm(4)

        @block.vector
        def _(dve):
            def sub(out_, a, b):
                return dve.tensor_tensor(out_, a, b, ALU.subtract)

            def norm(n):
                dve.wait_ge(inv_done, n + 1)

                def low(m):
                    dve.wait_ge(hh_done, DK * n + m + 1)
                    sub(h_lo[:, m, :], hn[:, m % 2, :], h_hi[:, m, :]).then_inc(hl_done, 1)

                for m in range(DK):
                    if n < 4:
                        wait(dve, hl_done, DK * n + m - 1)
                    elif m >= 2:
                        dve.wait_ge(out_stored[m % 2], 16 * (m // 2))
                    dve.scalar_tensor_tensor(hn[:, m % 2, :], X[:, m, :], param("gain", DK * n + m, 1),
                                             rms_inv[:, :], ALU.mult, ALU.mult).then_inc(hn_done, 1)
                    if n < 4 and m:
                        low(m - 1)
                if n < 4:
                    low(DK - 1)

            def add_square(n, m, first):
                dve.wait_ge(sq_done, lin(DK * n + 1, 1, m) if isinstance(m, int) else m + (DK * n + 1))
                if first:
                    dve.tensor_copy(sq_sum[:, :], sq_ring[:, 0, :]).then_inc(sum_done, 1)

            def residual(name, n):
                per = INFO[name][1]
                for i, j in units(dve, DK):
                    m = lin(j, 2, i)
                    dve.wait_ge(chunk_done, chunk(name, i, j, per - 1).count(1))
                    dve.tensor_tensor(X[:, m, :], X[:, m, :], bank(ACC + j), ALU.add).then_inc(x_done, 1)
                    dve.wait_ge(sq_done, lin(DK * n + j + 1, 2, i))
                    if isinstance(i, int) and m == 0:
                        dve.tensor_copy(sq_sum[:, :], sq_ring[:, j, :]).then_inc(sum_done, 1)
                    else:
                        dve.wait_ge(sum_done, lin(DK * n + j, 2, i))
                        dve.tensor_tensor(sq_sum[:, :], sq_sum[:, :], sq_ring[:, j, :], ALU.add)\
                            .then_inc(sum_done, 1)

            def copy_tiles(name, dst):
                for i, j in units(dve, INFO[name][0]):
                    dve.wait_ge(chunk_done, chunk(name, i, j).count(1))
                    dve.tensor_copy(dst[:, lin(j, 2, i), :], bank(ACC + j)).then_inc(copied[name], 1)

            def merge(name, b, sg, mt, mix_hi, mix_lo):
                for i, j in units(dve, DK):
                    m = lin(j, 2, i)
                    dve.wait_ge(gate_sig[b], lin(j + 1, 2, i))
                    dve.wait_ge(first_half[b], lin(j + 1, 2, i))
                    wait(dve, mixed[b], m)
                    dve.tensor_tensor(mt[:, 0, :], bank(BS), sg[:, j, 0, :], ALU.mult).then_inc(y_pool_done[b], 1)
                    dve.wait_ge(chunk_done, chunk(name, i, j).count(1))
                    dve.tensor_tensor(mt[:, 1, :], bank(BS + 1), sg[:, j, 1, :], ALU.mult).then_inc(y_nsa_done[b], 1)
                    dve.wait_ge(y_pool_done[b], lin(j + 1, 2, i))
                    dve.wait_ge(y_nsa_done[b], lin(j + 1, 2, i))
                    wait(dve, mix_hl[b], m)
                    dve.tensor_tensor(mt[:, 2, :], mt[:, 0, :], mt[:, 1, :], ALU.add).then_inc(mixed[b], 1)
                    dve.wait_ge(mix_hh[b], lin(j + 1, 2, i))
                    sub(mix_lo[:, m, :], mt[:, 2, :], mix_hi[:, m, :]).then_inc(mix_hl[b], 1)

            def ffn(name, b, steps):
                prm = param("conv1" if b == 0 else "conv2").rearrange("p (f w) -> p f w", w=4)

                def conv(dst, src, f, done, i):
                    def w(k):
                        return prm[:, f, k:k + 1]
                    dve.tensor_scalar(dst, src, w(2), w(3), ALU.mult, ALU.add).then_inc(conv_done[b], 1)
                    dve.wait_ge(conv_done[b], lin(done + 1, 2 * steps, i))
                    dve.scalar_tensor_tensor(dst[:, 1:], src[:, 0:T - 1], w(1), dst[:, 1:], ALU.mult, ALU.add)\
                        .then_inc(conv_done[b], 1)
                    dve.wait_ge(conv_done[b], lin(done + 2, 2 * steps, i))
                    dve.scalar_tensor_tensor(dst[:, 2:], src[:, 0:T - 2], w(0), dst[:, 2:], ALU.mult, ALU.add)\
                        .then_inc(conv_done[b], 1)

                for i, j in units(dve, FK):
                    f = lin(j, 2, i)
                    dve.wait_ge(chunk_done, chunk(name, i, j, 0).count(1))
                    wait(dve, act_hl[b], lin(j - 1, 2, i))
                    conv(t_gate[:, j, :], bank(ACC), f, steps * j, i)
                    dve.wait_ge(chunk_done, chunk(name, i, j, 1).count(1))
                    if b == 0:
                        val = bank(ACC + 1)
                    else:
                        val = t_val[:, j, :]
                        conv(val, bank(ACC + 1), lin(FK + j, 2, i), steps * j + 3, i)
                        dve.wait_ge(conv_done[b], lin(steps * j + 6, 2 * steps, i))
                    dve.wait_ge(silu_done[b], lin(j + 1, 2, i))
                    dve.tensor_tensor(t_gate[:, j, :], t_gate[:, j, :], val, ALU.mult).then_inc(gated[b], 1)
                    dve.wait_ge(act_hh[b], lin(j + 1, 2, i))
                    sub(act_lo[:, f, :], t_gate[:, j, :], act_hi[:, f, :]).then_inc(act_hl[b], 1)

            def attention(a, mask):
                n = len(a.units)
                for s in range(n + 5):
                    if s < n:
                        w = (a.units[s][1] + 1) * P
                        dve.wait_ge(a.scored, s + 1)
                        wait(dve, a.exped, s - 1)
                        col = slice(s % 4, s % 4 + 1)
                        dve.tensor_tensor_reduce(a.sm[:, s % 2, 0:w], banks[:, BS + s % 2, 0:w],
                                                 mask(a.units[s], w), 1.0, NEG, ALU.add, ALU.max,
                                                 a.nbias[:, col]).then_inc(a.masked, 1)
                        dve.wait_ge(a.masked, s + 1)
                        dve.tensor_scalar(a.nbias[:, col], a.nbias[:, col], -DH ** -0.5, None, ALU.mult)\
                            .then_inc(a.shifted, 1)
                    u = s - 1
                    if 0 <= u < n:
                        col = slice(u % 4, u % 4 + 1)
                        dve.wait_ge(a.exped, u + 1)
                        wait(dve, a.weighted, u - 3)
                        dve.reciprocal(a.inv[:, col], a.sums[:, col]).then_inc(a.inverted, 1)
                    u = s - 4
                    if 0 <= u < n and u % a.per_tile == a.per_tile - 1:
                        j = u // a.per_tile
                        dve.wait_ge(a.high, j + 1)
                        sub(a.o_lo[:, j, :], bank(BO + j % 2), a.o_hi[:, j, :]).then_inc(a.low, 1)

            step = [0]

            def start(ins):
                step[0] += 1
                ins.then_inc(start_step, 1)
                dve.wait_ge(start_step, step[0])

            TURN = (6.28125, 0.0019350051879882812, 3.019915981956753e-07)
            MAGIC = 12582912.0
            ang, turns, tmp = angle[:, 1, :], angle[:, 0, :], angle[:, 2, :]
            dve.wait_ge(consts_in, 32)
            dve.wait_ge(pos_in, 16)
            start(dve.tensor_copy(tmp, pos_i[:, :]))
            start(dve.tensor_scalar(ang, tmp, const("inv"), None, ALU.mult))
            start(dve.tensor_scalar(tmp, ang, 1.0 / (2.0 * np.pi), MAGIC, ALU.mult, ALU.add))
            start(dve.tensor_scalar(turns, tmp, MAGIC, None, ALU.subtract))
            for part in TURN:
                start(dve.scalar_tensor_tensor(ang, turns, -part, ang, ALU.mult, ALU.add))
            start(dve.scalar_tensor_tensor(tmp, ang, -1.0, ang, ALU.mult, ALU.max))
            start(dve.tensor_scalar(tmp, tmp, -1.0, float(np.pi / 2), ALU.mult, ALU.add))
            dve.wait_ge(rel_in, 16)
            start(dve.tensor_scalar(rel_ext[:, 0:256], rel_row[:, 1:257], DH ** 0.5, None, ALU.mult))
            start(dve.tensor_scalar(rel_ext[:, 256:640], rel_row[:, 256:257].to_broadcast([NH, 384]), DH ** 0.5,
                                    None, ALU.mult))
            for m in range(DK):
                dve.wait_ge(sq_done, m + 1)
                if m == 0:
                    dve.tensor_copy(sq_sum[:, :], sq_ring[:, 0, :]).then_inc(sum_done, 1)
                else:
                    dve.wait_ge(sum_done, m)
                    dve.tensor_tensor(sq_sum[:, :], sq_sum[:, :], sq_ring[:, m % 2, :], ALU.add)\
                        .then_inc(sum_done, 1)
            norm(0)
            copy_tiles("in1", p1)

            tiles = [(t, param("q_gain")) for t in (4, 5, 6, 7)] + [(KS, param("k_gain", 1, 1)),
                                                                   (KW, param("k_gain", 2, 1))]
            dve.wait_ge(sin_done, 2)
            dve.wait_ge(rel_stored, 16)

            def rotate(n):
                x = p1[:, tiles[n][0], :]
                dve.wait_ge(n_gain, n + 1)
                wait(dve, n_sum, n - 1)
                dve.tensor_tensor(nr_c[:, n % 2, :], x, rope[:, 0, :], ALU.mult).then_inc(n_cos, 1)
                dve.wait_ge(n_rot, n + 1)
                dve.tensor_tensor(nr_s[:, n % 2, :], bank(BT + n % 2), rope[:, 1, :], ALU.mult).then_inc(n_sin, 1)
                dve.wait_ge(n_cos, n + 1)
                dve.wait_ge(n_sin, n + 1)
                dve.tensor_tensor(x, nr_c[:, n % 2, :], nr_s[:, n % 2, :], ALU.add).then_inc(n_sum, 1)

            for n, (t, gain) in enumerate(tiles):
                dve.wait_ge(n_inv, n + 1)
                dve.scalar_tensor_tensor(p1[:, t, :], p1[:, t, :], gain, nr_r[:, n % 2, :], ALU.mult, ALU.mult)\
                    .then_inc(n_gain, 1)
                if n:
                    rotate(n - 1)
            rotate(5)
            dve.wait_ge(blk_zero, 1)
            pe_ = param("pe").rearrange("p (c l) -> p c l", c=2)
            for c in range(2):
                for g in range(2):
                    src = p1[rows(g), KC + c, :].rearrange("p (a b) -> p b a", b=16)
                    for l2 in range(2):
                        dve.tensor_tensor(cmp_blk[rows(g), c, 16 * l2:16 * l2 + 16, g, :], src[:, :, l2:l2 + NCMP],
                                          pe_[rows(g), c, 16 * l2:16 * l2 + 16].unsqueeze(2).to_broadcast(
                                              [DH, 16, NCMP]), ALU.add).then_inc(blk_done, 1)
            dve.wait_ge(c_act, 8)
            dve.scalar_tensor_tensor(kc_t[:, :], banks[:, BO, 0:NCMP], param("k_gain", 0, 1), kc_tmp[:, 1, :],
                                     ALU.mult, ALU.mult).then_inc(c_dve, 1)
            dve.wait_ge(c_dve, 1)
            dve.tensor_tensor(kc_tmp[:, 2, :], kc_t[:, :], rope[:, 0, 31:T:16], ALU.mult).then_inc(c_dve, 1)
            dve.wait_ge(c_pe, 8)
            dve.tensor_tensor(kc_tmp[:, 3, :], banks[:, BT, 0:NCMP], rope[:, 1, 31:T:16], ALU.mult)\
                .then_inc(c_dve, 1)
            dve.wait_ge(c_dve, 3)
            dve.tensor_tensor(kc_t[:, :], kc_tmp[:, 2, :], kc_tmp[:, 3, :], ALU.add).then_inc(c_dve, 1)
            for gi in range(4):
                dve.wait_ge(yp_h, gi + 1)
                dve.scalar_tensor_tensor(yp_lo[:, gi, :], bank(POOLED[gi % 2]), param("pool_scale", gi, 1),
                                         yp_hi[:, gi, :], ALU.mult, ALU.subtract).then_inc(yp_l, 1)
            flat = cmp_s[:, :, :, :, :].rearrange("p a b c n -> p (a b c) n")
            wide = [P, 32, NCMP]
            for half in range(2):
                dve.wait_ge(s_pe, half + 1)
                dve.tensor_tensor(cmp_s[:, half, :, :, :],
                                  banks[:, BS + half, 0:16 * NCMP].rearrange("p (a b n) -> p a b n", a=4, b=4),
                                  const("cmp", NT, NCMP).unsqueeze(2).to_broadcast([P, NT, 4, NCMP]), ALU.add)\
                    .then_inc(s_dve, 1)
            dve.wait_ge(s_dve, 2)
            dve.tensor_reduce(cmp_red[:, 0, :], flat, AXX, ALU.max).then_inc(s_dve, 1)
            dve.wait_ge(s_dve, 3)
            sub(flat, flat, cmp_red[:, 0, :].unsqueeze(2).to_broadcast(wide)).then_inc(s_dve, 1)
            dve.wait_ge(s_act, 1)
            dve.tensor_reduce(cmp_red[:, 1, :], flat, AXX, ALU.add).then_inc(s_dve, 1)
            dve.wait_ge(s_dve, 5)
            dve.reciprocal(cmp_red[:, 2, :], cmp_red[:, 1, :]).then_inc(s_dve, 1)
            dve.wait_ge(v_copied[0], 3)
            dve.wait_ge(s_dve, 6)
            fac = cmp_red[:, 2, :].rearrange("p (h a b) -> p h a b", h=2, a=NT)
            gts = gate_t[:, :, :].rearrange("p a (h n) -> p a h n", n=3)
            for half in range(2):
                dve.tensor_tensor(fac[:, half, :, :], fac[:, half, :, :], gts[:, :, 4 * half:4 * half + 4, 0],
                                  ALU.mult).then_inc(s_dve, 1)
            dve.wait_ge(s_dve, 8)
            dve.tensor_scalar(fac[:, :, 0, :], fac[:, :, 0, :], const("cmp_any"), None, ALU.mult).then_inc(s_dve, 1)
            dve.wait_ge(s_dve, 9)
            dve.tensor_tensor(flat, flat, cmp_red[:, 2, :].unsqueeze(2).to_broadcast(wide), ALU.mult)\
                .then_inc(s_dve, 1)
            attention(att1, lambda u, w: const("causal")[:, T - w:T])
            merge("mix1", 0, sg1, mt1, mix1_hi, mix1_lo)
            residual("out1", 1)
            norm(1)
            ffn("up1", 0, 3)
            residual("down1", 2)

            norm(2)
            taps = param("conv_qkv").rearrange("p (f w) -> p f w", w=4)
            for i, j in units(dve, 12):
                t = lin(j, 2, i)
                src, dst = bank(ACC + j), cv[:, j, :]
                dve.wait_ge(chunk_done, chunk("in2c", i, j).count(1))
                wait(dve, cv_silu, lin(j - 1, 2, i))
                dve.tensor_scalar(dst, src, taps[:, t, 3:4], None, ALU.mult).then_inc(cv_done, 1)
                for k in range(1, 4):
                    dve.wait_ge(cv_done, lin(4 * j + k, 8, i))
                    dve.scalar_tensor_tensor(dst[:, k:], src[:, 0:T - k], taps[:, t, 3 - k:4 - k], dst[:, k:],
                                             ALU.mult, ALU.add).then_inc(cv_done, 1)
            copy_tiles("in2z", p2a[:, 12:17, :])
            g = slice(32, 32 + GH)
            col = {n: params[g, PARAM[n][0]:PARAM[n][0] + 1] for n in ("a_log", "dt_bias")}
            dve.wait_ge(copied["in2z"], 5)
            dve.tensor_scalar(gz[g, :], p2a[g, 16, :], col["dt_bias"], None, ALU.add).then_inc(g_dve, 1)
            dve.wait_ge(g_dve, 1)
            dve.scalar_tensor_tensor(gz2[g, :], gz[g, :], -1.0, gz[g, :], ALU.mult, ALU.max).then_inc(g_dve, 1)
            for n in range(8):
                dve.wait_ge(l_inv, n + 1)
                dve.scalar_tensor_tensor(p2a[:, n, :], p2a[:, n, :], float(P) ** -0.5 if n < GH else 1.0,
                                         l2_r[:, n % 2, :], ALU.mult, ALU.mult).then_inc(l_out, 1)
            dve.wait_ge(g_act, 3)
            dve.scalar_tensor_tensor(gz[g, :], gz[g, :], 0.0, gz2[g, :], ALU.max, ALU.add).then_inc(g_dve, 1)
            dve.tensor_scalar(ea[g, 1:2], ea[g, 0:1], -1.0, None, ALU.mult).then_inc(g_dve, 1)
            dve.wait_ge(g_dve, 4)
            dve.tensor_scalar(gz2[g, :], gz[g, :], ea[g, 1:2], None, ALU.mult).then_inc(g_dve, 1)
            dve.wait_ge(g_dve, 5)
            dve.wait_ge(blk_zero, 2)
            dve.tensor_tensor_scan(gb_rows[g, :], const("reset")[g, :], gz2[g, :], 0.0, ALU.mult, ALU.add)\
                .then_inc(g_dve, 1)
            dve.wait_ge(g_act, 6)
            dve.tensor_scalar(gd_neg[:, :, :], gd_cols[:, :, 32:32 + GH], -1.0, None, ALU.mult).then_inc(g_dve, 1)
            dve.tensor_tensor(gd_bg[:, :, :], gd_bg[:, :, :], gd_cols[:, :, 0:GH], ALU.mult).then_inc(g_dve, 1)
            dve.wait_ge(g_dve, 8)
            sq3 = [P, NT, P]

            def every(mask):
                return mask.unsqueeze(1).to_broadcast(sq3)

            def per_token(c_):
                return c_.unsqueeze(2).to_broadcast(sq3)

            dve.wait_ge(l_out, 8)
            for h in range(GH):
                b = 11 * h
                dve.wait_ge(d_pe, 6 * h + 1)
                dve.wait_ge(d_act, 7 * h + 1)
                wait(dve, d_dve, b)
                dve.tensor_tensor(dec[:, :, :], bank(BS, NT), every(const("decay")), ALU.add).then_inc(d_dve, 1)
                for half in range(2):
                    e = CH - 1 if half == 0 else P - 1
                    sub(gd_kd[rows(half), h, :], banks[rows(half), BS, e:T:P],
                        gd_cols[rows(half), :, 32 + h]).then_inc(d_dve, 1)
                dve.wait_ge(d_pe, 6 * h + 2)
                dve.tensor_tensor(beta_strict[:, :, :], bank(BS + 1, NT), every(const("strict")), ALU.mult)\
                    .then_inc(d_dve, 1)
                dve.wait_ge(d_pe, 6 * h + 4)
                dve.wait_ge(d_act, 7 * h + 1)
                dve.tensor_tensor(p2a[:, h, :], p2a[:, h, :], gam_row[:, :], ALU.mult).then_inc(d_dve, 1)
                dve.wait_ge(d_act, 7 * h + 5)
                dve.tensor_tensor(p_t[:, h, :, :], bank(BT + 1, NT), dec[:, :, :], ALU.mult).then_inc(d_dve, 1)
                dve.wait_ge(d_dve, b + 6)
                dve.tensor_tensor(dec[:, :, :], bank(BT, NT), dec[:, :, :], ALU.mult).then_inc(d_dve, 1)
                dve.wait_ge(d_dve, b + 7)
                dve.tensor_tensor(a_t[:, h, :, :], dec[:, :, :], beta_strict[:, :, :], ALU.mult).then_inc(d_dve, 1)
                dve.wait_ge(d_pe, 6 * h + 5)
                dve.tensor_tensor(k_bg[:, h, :, :], bank(BO, NT), per_token(gd_bg[:, :, h]), ALU.mult)\
                    .then_inc(d_dve, 1)
                dve.wait_ge(d_act, 7 * h + 6)
                dve.tensor_tensor(k_dec[:, h, :, :], bank(BO, NT), per_token(gd_kd[:, h, :]), ALU.mult)\
                    .then_inc(d_dve, 1)
                dve.wait_ge(d_pe, 6 * h + 6)
                dve.tensor_tensor(v_b[:, h, :, :], bank(BO + 1, NT), per_token(gd_cols[:, :, h]), ALU.mult)\
                    .then_inc(d_dve, 1)
            dve.wait_ge(d_dve, 11 * GH)
            for h in range(GH):
                dve.wait_ge(i_mask, h + 1)
                sub(y_inv[:, h, :, :], every(ident), b_t[:, h % 2, :, :]).then_inc(i_y, 1)
                dve.wait_ge(i_bx, h + 1)
                sub(x_inv[:, h, :, :], every(ident), bank(BT + h % 2, NT)).then_inc(i_x, 1)

            def update(k):
                h = k % GH
                dve.wait_ge(i_pe, 2 * k + 1)
                sub(x_inv[:, h, :, :], x_inv[:, h, :, :], bank(BS + k % 2, NT)).then_inc(i_x, 1)
                dve.wait_ge(i_pe, 2 * k + 2)
                sub(y_inv[:, h, :, :], y_inv[:, h, :, :], bank(BO + k % 2, NT)).then_inc(i_y, 1)

            for k in range(5 * GH):
                update(k)
            for c in range(NCH):
                p, half, slot = c // 2, c % 2, c // 2 % 2
                rs = rows(half)
                if c == 0:
                    dve.wait_ge(r_cp, 2 * GH)
                    dve.tensor_copy(u_new[rs, slot, :, :], uv[rs, :, p, :]).then_inc(r_u, 1)
                else:
                    dve.wait_ge(r_ws, c)
                    sub(u_new[rs, slot, :, :], uv[rs, :, p, :], bank(BS + c % 2, GH)[rs]).then_inc(r_u, 1)
                if c == NCH - 1:
                    break
                dve.wait_ge(r_ds, c + 1)
                wait(dve, r_o, c)
                wait(dve, r_s, GH * c)
                for h in range(GH):
                    new = bank(BT + c % 2, GH)[:, h, :]
                    if c == 0:
                        dve.tensor_copy(state[:, 0, h, :], new).then_inc(r_s, 1)
                    else:
                        dve.scalar_tensor_tensor(state[:, c % 2, h, :], state[:, (c - 1) % 2, h, :],
                                                 gd_last[:, h, c:c + 1], new, ALU.mult, ALU.add).then_inc(r_s, 1)
            dve.wait_ge(f_act, 2)
            dve.tensor_reduce(o_red[:, :], o_sq.rearrange("p c h d -> p (c h) d"), AXX, ALU.add).then_inc(f_dve, 1)
            dve.wait_ge(f_act, 4)
            on = o_nat.rearrange("p c h d -> p (c h) d")
            dve.tensor_tensor(on, on, o_red[:, :].unsqueeze(2).to_broadcast([P, NT * GH, P]), ALU.mult)\
                .then_inc(f_dve, 1)
            for h in range(GH):
                dve.wait_ge(f_pe, h + 1)
                wait(dve, oa_l, h - 1)
                dve.scalar_tensor_tensor(oa[:, h % 2, :], bank(BT + h % 2), param("gdn_gain"), p2a[:, 12 + h, :],
                                         ALU.mult, ALU.mult).then_inc(f_dve, 1)
                dve.wait_ge(oa_h, h + 1)
                sub(oa_lo[:, h, :], oa[:, h % 2, :], oa_hi[:, h, :]).then_inc(oa_l, 1)
            dve.wait_ge(blk_zero, 3)
            attention(att2, lambda u, w: rel[:, 2 * u[0] + u[3], w - 1::-1])
            merge("mix2", 1, sg2, mt2, mix2_hi, mix2_lo)
            residual("out2", 3)
            norm(3)
            ffn("up2", 1, 6)
            residual("down2", 4)
            norm(4)

        @block.tensor
        def _(pe):
            def product(c, dst, hi, lo, ks, first, last, done, ready=None):
                for n, (ks_, kr) in enumerate(ks):
                    w_h = w_hi[:, c.slot, ks_ * P:(ks_ + 1) * P]
                    w_l = w_lo[:, c.slot, ks_ * P:(ks_ + 1) * P]
                    if ready:
                        pe.wait_ge(ready[0], ready[1] + kr + 1)
                    pe.matmul(dst, w_h, hi[:, kr, :], start=first and n == 0, stop=False)
                    pe.matmul(dst, w_h, lo[:, kr, :], start=False, stop=False)
                    mm = pe.matmul(dst, w_l, hi[:, kr, :], start=False, stop=last and n == len(ks) - 1)
                if done:
                    mm.then_inc(done, 1)

            def late(name, b, plan, total, before):
                state = [0]

                def fill(*at):
                    upto = plan[at][1] if at else total
                    while state[0] < upto:
                        n, r = state[0] // PIECES, state[0] % PIECES
                        c = chunk(name, n // 2, n % 2)
                        if r == 0:
                            pe.wait_ge(lo_ready, c.count(1))
                            if n < 2:
                                pe.wait_ge(before[0], before[1] - 1 + n)
                            wait(pe, filled[b], n - 1)
                        ks = [(k, k) for k in range(2 * r, 2 * r + 2)]
                        product(c, bank(ACC + (n + LATE_BANK[b]) % 2), h_hi, h_lo, ks, r == 0, r == PIECES - 1,
                                chunk_done if r == PIECES - 1 else None)
                        state[0] += 1
                return fill

            def whole(n, off=0):
                return [(k, off + k) for k in range(n)]

            def norm(n):
                pe.wait_ge(sum_done, DK * (n + 1))
                pe.matmul(bank(BS), ones, sq_sum[:, :], start=True, stop=True).then_inc(mean_done, 1)

            def linear(name, n, used, per=1):
                for i, j in units(pe, INFO[name][0]):
                    c = chunk(name, i, j)
                    pe.wait_ge(lo_ready, c.count(1))
                    wait(pe, used, lin(per * (j - 1), 2 * per, i))
                    first = isinstance(i, int) and i == 0 and j == 0
                    product(c, bank(ACC + j), h_hi, h_lo, whole(DK), True, True, chunk_done,
                            (hl_done, DK * n) if first else None)

            def residual(name, n, hi, lo, split_):
                nchunk, kt = INFO[name][1], INFO[name][2]
                for i, j in units(pe, DK):
                    wait(pe, x_done, lin(DK * (n - 1) + j - 1, 2, i) if not (isinstance(i, int) and i == 0) else 0)
                    for q in range(nchunk):
                        c = chunk(name, i, j, q)
                        pe.wait_ge(lo_ready, c.count(1))
                        first = isinstance(i, int) and i == 0 and j == 0
                        product(c, bank(ACC + j), hi, lo, whole(kt, kt * q), q == 0, q == nchunk - 1, chunk_done,
                                (split_, 0) if first else None)

            def merge(name, b, y1, y2, nlate):
                for i, j in units(pe, DK):
                    m = lin(j, 2, i)
                    c = chunk(name, i, j)
                    pe.wait_ge(lo_ready, c.count(1))
                    wait(pe, y_pool_done[b], m)
                    product(c, bank(BS), *y1, [(k, k) for k in range(4)], True, True, first_half[b])
                    wait(pe, y_nsa_done[b], m)
                    product(c, bank(BS + 1), *y2, [(4 + k, k) for k in range(4)], True, True, chunk_done)
                pe.wait_ge(filled[b], nlate)

            def ffn(name, b, n, steps):
                for i, j in units(pe, FK):
                    first = isinstance(i, int) and i == 0 and j == 0
                    for q in range(2):
                        c = chunk(name, i, j, q)
                        pe.wait_ge(lo_ready, c.count(1))
                        if q == 0 and not first:
                            pe.wait_ge(conv_done[b], lin(steps * (j - 1) + 3, 2 * steps, i))
                        elif q == 1 and b == 0:
                            wait(pe, gated[b], lin(j, 2, i))
                        elif q == 1:
                            wait(pe, conv_done[b], lin(steps * j, 2 * steps, i))
                        product(c, bank(ACC + q), h_hi, h_lo, whole(DK), True, True, chunk_done,
                                (hl_done, DK * n) if first and q == 0 else None)
                pe.wait_ge(conv_done[b], steps * (FK - 1) + 3)

            def turn(dst, src, n=P, last=None):
                return pe.transpose(dst, src, ident[0:n, 0:n])

            def attention(a, q_tile, k_tile, v_tile, first_values=None, fill=None):
                n = len(a.units)
                for s in range(n + 3):
                    if s < n:
                        j, i, b, half = a.units[s]
                        wait(pe, a.masked, s - 1)
                        pe.matmul(banks[:, BS + half, 0:(i + 1) * P], q_tile(j)[rows(half), i * P:(i + 1) * P],
                                  k_tile(j, b)[rows(half), 0:(i + 1) * P], start=True, stop=True)\
                            .then_inc(a.scored, 1)
                        if fill:
                            fill("unit", s)
                    u = s - 2
                    if 0 <= u < n:
                        j, i, b, half = a.units[u]
                        pe.wait_ge(a.weighted, u + 1)
                        wait(pe, a.fetched, u - 1)
                        for k in range(i + 1):
                            mm = turn(banks[:, BT + u % 2, k * P:(k + 1) * P], a.p[:, u % 3, k * P:(k + 1) * P])
                        mm.then_inc(a.flipped, 1)
                    u = s - 3
                    if 0 <= u < n:
                        j, i, b, half = a.units[u]
                        pe.wait_ge(a.fetched, u + 1)
                        if u % a.per_tile == 0:
                            wait(pe, a.low, j - 1)
                        dst = banks[rows(half), BO + j % 2, i * P:(i + 1) * P]
                        begin = b == 0
                        if begin and first_values:
                            pe.matmul(dst, *first_values(j, i, half), start=True, stop=False)
                            begin = False
                        end = b == max(x[2] for x in a.units)
                        for k in range(i + 1):
                            mm = pe.matmul(dst, v_tile(j, b, half, k), a.pt[:, u % 2, k * P:(k + 1) * P],
                                           start=begin and k == 0, stop=end and k == i)
                        mm.then_inc(a.summed, 1)

            pe.wait_ge(consts_in, 32)
            norm(0)
            linear("in1", 0, copied["in1"])

            pe.wait_ge(copied["in1"], 15)
            tiles = (4, 5, 6, 7, KS, KW)

            def rotate(n):
                pe.wait_ge(n_gain, n + 1)
                wait(pe, n_sin, n - 1)
                pe.matmul(bank(BT + n % 2), const("rot"), p1[:, tiles[n], :], start=True, stop=True)\
                    .then_inc(n_rot, 1)

            fill = late("fill1", 0, FILL1, FILLED1, (copied["in1"], 15))
            for n in range(6):
                pe.wait_ge(n_sq, n + 1)
                wait(pe, n_ln, n - 1)
                pe.matmul(bank(BS + n % 2), halves, nr_sq[:, n % 2, :], start=True, stop=True).then_inc(n_ms, 1)
                if n:
                    rotate(n - 1)
                fill("norm", n)
            rotate(5)
            for v in range(2):
                for k in range(NT):
                    mm = turn(banks[:, BO + v, k * P:(k + 1) * P], p1[:, VS + v, k * P:(k + 1) * P])
                mm.then_inc(turned[0], 1)
                fill("turn", v)
            pe.wait_ge(gates_ready, 1)
            pe.wait_ge(n_sin, 5)
            for k in range(NT):
                mm = turn(banks[:, BT, 24 * k:24 * k + 24], p1[0:24, GT, k * P:(k + 1) * P], 24)
            mm.then_inc(turned[0], 1)
            fill("turn", 2)
            pe.wait_ge(blk_done, 8)
            pe.wait_ge(cmp_in, 64)
            pe.wait_ge(n_ln, 6)
            pe.wait_ge(n_sin, 6)
            for c in range(2):
                for l in range(32):
                    mm = pe.matmul(banks[0:2 * NCMP, BS + c, 0:P],
                                   cmp_blk[:, c, l, :, :].rearrange("p a b -> p (a b)"),
                                   cmp_w1[:, c, l * P:(l + 1) * P], start=l == 0, stop=l == 31)
                mm.then_inc(c_pe, 1)
            fill("compress", 0)
            pe.wait_ge(v_copied[0], 3)
            for c in range(2):
                pe.wait_ge(c_act, c + 1)
                turn(banks[:, BT + c, 0:2 * NCMP], hid[:, c, :], 2 * NCMP).then_inc(c_pe, 1)
            fill("compress", 1)
            pe.wait_ge(c_act, 3)
            for g in range(2):
                mm = pe.matmul(banks[rows(g), BO, 0:NCMP], cmp_w2[:, 0, :], hid_t[:, 0, g * NCMP:(g + 1) * NCMP],
                               start=True, stop=True)
            mm.then_inc(c_pe, 1)
            pe.wait_ge(c_act, 4)
            for g in range(2):
                mm = pe.matmul(banks[0:NCMP, BO + 1, g * DH:(g + 1) * DH], hid_t[:, 1, g * NCMP:(g + 1) * NCMP],
                               cmp_w2[:, 1, :], start=True, stop=True)
            mm.then_inc(c_pe, 1)
            fill("compress", 2)
            pe.wait_ge(c_act, 5)
            pe.matmul(banks[:, BS, 0:NCMP], halves, kc_tmp[:, 0, :], start=True, stop=True).then_inc(c_pe, 1)
            for gi in range(2):
                pe.wait_ge(pooled, sum(1 + g_ + 1 + 3 for g_ in range(gi + 1)))
                pe.matmul(bank(POOLED[gi % 2]), pool_w[:, gi, :], p1[:, gi, :], start=True, stop=True)\
                    .then_inc(pool_mul, 1)
            fill("compress", 3)
            pe.wait_ge(c_dve, 1)
            pe.matmul(banks[:, BT, 0:NCMP], const("rot"), kc_t[:, :], start=True, stop=True).then_inc(c_pe, 1)
            for gi in range(2, 4):
                pe.wait_ge(pooled, sum(1 + g_ + 1 + 3 for g_ in range(gi + 1)))
                pe.wait_ge(yp_l, gi - 1)
                pe.matmul(bank(POOLED[gi % 2]), pool_w[:, gi, :], p1[:, gi, :], start=True, stop=True)\
                    .then_inc(pool_mul, 1)
            fill("compress", 4)
            pe.wait_ge(c_dve, 4)
            pe.wait_ge(n_sum, 6)
            pe.wait_ge(yp_l, 3)
            for half in range(2):
                for i in range(NT):
                    for j in range(4):
                        at_ = (4 * i + j) * NCMP
                        mm = pe.matmul(banks[:, BS + half, at_:at_ + NCMP],
                                       p1[rows(half), 4 + j, i * P:(i + 1) * P], kc_t[rows(half), :],
                                       start=True, stop=True)
                mm.then_inc(s_pe, 1)
            fill("scores", 0)
            fill("scores", 1)
            pe.wait_ge(s_dve, 10)
            pe.wait_ge(yp_l, 4)
            for r in range(8):
                wait(pe, s_act, r)
                for k in range(4):
                    half, i, j = r // 4, r % 4, k
                    mm = turn(banks[0:NCMP, BT + r % 2, k * P:(k + 1) * P], cmp_s[:, half, i, j, :])
                mm.then_inc(s_pe, 1)
            pe.wait_ge(s_act, 9)
            attention(att1, lambda j: p1[:, 4 + j, :], lambda j, b: p1[:, KS + b, :],
                      lambda j, b, half, k: v1_nat[:, b, k, rows(half)],
                      lambda j, i, half: (vc_nat[:, half, :], pc_t[:, 16 * half + 4 * i + j, :]), fill)
            pe.wait_ge(yp_l, 4)
            pe.wait_ge(att1.low, 4)
            merge("mix1", 0, (yp_hi, yp_lo), (o1_hi, o1_lo), INFO["fill1"][0])
            residual("out1", 1, mix1_hi, mix1_lo, mix_hl[0])
            norm(1)
            ffn("up1", 0, 1, 3)
            residual("down1", 2, act_hi, act_lo, act_hl[0])

            norm(2)
            linear("in2c", 2, cv_done, 4)
            pe.wait_ge(cv_done, 48)
            linear("in2z", 2, copied["in2z"])
            fill = late("fill2", 1, FILL2, FILLED2, (copied["in2z"], 5))
            for n in range(8):
                pe.wait_ge(l_sq, n + 1)
                wait(pe, l_ln, n - 1)
                pe.matmul(bank(BS + n % 2), ones, l2_sq[:, n % 2, :], start=True, stop=True).then_inc(l_ms, 1)
                fill("norm", n)
            fill("gates", 0)
            pe.wait_ge(g_dve, 6)
            pe.wait_ge(g_act, 4)
            for p in range(NT):
                mm = turn(banks[:, BO, 64 * p:64 * p + 64], gb_rows[:, p * P:(p + 1) * P], 64)
            mm.then_inc(g_pe, 1)
            fill("gates", 1)
            pe.wait_ge(g_act, 5)
            pe.wait_ge(l_out, 8)
            pick = const("pick", 2 * GH, P)
            for h in range(GH):
                q_, k_, v_ = p2a[:, h, :], p2a[:, GH + h, :], p2a[:, 2 * GH + h, :]
                b = 11 * (h - 1)

                def free(n):
                    if h:
                        pe.wait_ge(d_dve, b + n)

                free(3)
                if h:
                    pe.wait_ge(d_act, 7 * (h - 1) + 1)
                pe.matmul(bank(BS), pick[0:64, GH + h, :], gb_rows[:, :], start=True, stop=True).then_inc(d_pe, 1)
                free(4)
                pe.matmul(bank(BS + 1), pick[0:64, h, :], gb_rows[:, :], start=True, stop=True).then_inc(d_pe, 1)
                fill("rows", h)
                for n, (dst, lhs, rhs) in enumerate(((BT, k_, k_), (BT + 1, k_, q_), (BO, k_, None), (BO + 1, v_, None))):
                    free((7, 6, 10, 11)[n])
                    for p in range(NT):
                        cols = slice(p * P, (p + 1) * P)
                        if rhs is None:
                            mm = turn(banks[:, dst, cols], lhs[:, cols])
                        else:
                            mm = pe.matmul(banks[:, dst, cols], lhs[:, cols], rhs[:, cols], start=True, stop=True)
                    mm.then_inc(d_pe, 1)
            pe.wait_ge(d_dve, 11 * GH)
            for h in range(GH):
                pe.wait_ge(i_mask, h + 1)
                wait(pe, i_x, h - 1)
                for p in range(NT):
                    mm = turn(banks[:, BT + h % 2, p * P:(p + 1) * P], b_t[:, h % 2, p, :])
                mm.then_inc(i_bx, 1)
                fill("first", h)
            pe.wait_ge(i_x, GH)

            def corrections(k):
                h, r = k % GH, k % 2
                pe.wait_ge(i_cp, k + 1)
                wait(pe, i_x, GH + k - 1)
                for p in range(NT):
                    mm = pe.matmul(banks[:, BS + r, p * P:(p + 1) * P], y_inv[:, h, p, :], bx[:, r, p, :],
                                   start=True, stop=True)
                mm.then_inc(i_pe, 1)
                wait(pe, i_y, GH + k - 1)
                for p in range(NT):
                    mm = pe.matmul(banks[:, BO + r, p * P:(p + 1) * P], bx[:, r, p, :], y_inv[:, h, p, :],
                                   start=True, stop=True)
                mm.then_inc(i_pe, 1)

            for k in range(5 * GH):
                h, r = k % GH, k % 2
                pe.wait_ge(i_mask, GH + k + 1)
                pe.wait_ge(i_x, k + 1)
                pe.wait_ge(i_y, k + 1)
                wait(pe, i_cp, k - 1)
                for p in range(NT):
                    mm = pe.matmul(banks[:, BT + r, p * P:(p + 1) * P], b_t[:, r, p, :], x_inv[:, h, p, :],
                                   start=True, stop=True)
                mm.then_inc(i_bx, 1)
                fill("level", k)
                if k:
                    corrections(k - 1)
            corrections(5 * GH - 1)
            pe.wait_ge(i_y, 6 * GH)
            pe.wait_ge(i_x, 6 * GH)
            for h in range(GH):
                for m, dst in ((0, BT), (1, BO)):
                    wait(pe, r_cp, 2 * (h - 2) + 1 + m)
                    for p in range(NT):
                        lhs, rhs = (k_bg[:, h, p, :], y_inv[:, h, p, :]) if m == 0 else \
                            (y_inv[:, h, p, :], v_b[:, h, p, :])
                        mm = pe.matmul(banks[:, dst + h % 2, p * P:(p + 1) * P], lhs, rhs, start=True, stop=True)
                    mm.then_inc(r_w, 1)
            pe.wait_ge(r_cp, 2 * GH)
            for c in range(NCH):
                p, half, slot = c // 2, c % 2, c // 2 % 2
                rs, tok = rows(half), slice(c * CH, (c + 1) * CH)
                if c:
                    pe.wait_ge(r_s, GH * c)
                    for h in range(GH):
                        w = w_t[:, h, :, :].rearrange("p a b -> p (a b)")
                        mm = pe.matmul(banks[rs, BS + c % 2, h * P:(h + 1) * P], w[:, tok],
                                       state[:, (c - 1) % 2, h, :], start=True, stop=True)
                    mm.then_inc(r_ws, 1)
                fill("chunk", c)
                pe.wait_ge(r_u, c + 1)
                if c < NCH - 1:
                    for h in range(GH):
                        mm = pe.matmul(banks[:, BT + c % 2, h * P:(h + 1) * P], k_dec[rs, h, p, :],
                                       u_new[rs, slot, h, :], start=True, stop=True)
                    mm.then_inc(r_ds, 1)
                if half == 0:
                    wait(pe, r_ocp, p - 1)
                for h in range(GH):
                    dst = banks[rs, BO + p % 2, h * P:(h + 1) * P]
                    if c:
                        pe.matmul(dst, p2a[:, h, tok], state[:, (c - 1) % 2, h, :], start=True, stop=False)
                    mm = pe.matmul(dst, p_t[rs, h, p, rs], u_new[rs, slot, h, :], start=c == 0, stop=True)
                mm.then_inc(r_o, 1)
            fill("out", 0)
            pe.wait_ge(f_dve, 2)
            for h in range(GH):
                wait(pe, f_dve, h + 1 if h >= 2 else 0)
                for p in range(NT):
                    mm = turn(banks[:, BT + h % 2, p * P:(p + 1) * P], o_nat[:, p, h, :])
                mm.then_inc(f_pe, 1)
            fill("out", 1)
            for v in range(4):
                fill("turn", v)
                pe.wait_ge(qkv_in["v"], 16)
                wait(pe, v_copied[1], v - 1)
                for k in range(NT):
                    mm = turn(banks[:, BO + v % 2, k * P:(k + 1) * P], p2b[:, 8 + v, k * P:(k + 1) * P])
                mm.then_inc(turned[1], 1)
            pe.wait_ge(v_copied[1], 4)
            pe.wait_ge(qkv_in["q"], 16)
            pe.wait_ge(qkv_in["k"], 16)
            attention(att2, lambda j: p2b[:, j, :], lambda j, b: p2b[:, 4 + j, :],
                      lambda j, b, half, k: v2_nat[:, k, j * P + half * DH:j * P + (half + 1) * DH], fill=fill)
            pe.wait_ge(att2.low, 4)
            pe.wait_ge(oa_l, 4)
            merge("mix2", 1, (oa_hi, oa_lo), (ob_hi, ob_lo), INFO["fill2"][0])
            residual("out2", 3, mix2_hi, mix2_lo, mix_hl[1])
            norm(3)
            ffn("up2", 1, 3, 6)
            residual("down2", 4, act_hi, act_lo, act_hl[1])
            norm(4)


def diagonals(rows_dram, h):
    view = rows_dram[h:h + 1, 0:T]
    return bass.AP(tensor=view.tensor, offset=view.offset, ap=[[1, P], [1, T]])


def by_tiles(w, columns=None):
    k, m = w.shape
    if columns is None:
        t = w.reshape(k // P, P, m // P, P)
    else:
        t = np.zeros((k, len(columns), P), w.dtype)
        for n, cols in enumerate(columns):
            for at, a, b in cols:
                t[:, n, at:at + b - a] = w[:, a:b]
        t = t.reshape(k // P, P, len(columns), P)
    return np.ascontiguousarray(t.transpose(2, 1, 0, 3)).reshape(t.shape[2], P, -1)


def by_columns(v):
    return v.reshape(-1, P).T


def kernel(**inputs):
    from concourse import bacc
    from concourse.bass_utils import run_bass_kernel_spmd

    a = {k: np.asarray(v) for k, v in inputs.items()}
    a = {k: v[0] if k not in ("norm_final_w_2",) else v for k, v in a.items()}

    def straight(first, n):
        return [[(0, first + P * t, first + P * (t + 1))] for t in range(n)]

    def gate_pairs(first):
        return [[(0, at, at + P)] for m in range(DK) for at in (first + P * m, first + D + P * m)]

    q_pairs = [[(0, 512 + DH * j, 512 + DH * (j + 1)), (DH, 512 + DH * (j + 4), 512 + DH * (j + 5))]
               for j in range(4)]
    kv = 1024
    in1 = straight(0, 4) + q_pairs + straight(kv, 2) + straight(kv + 3 * P, 1) + straight(kv + 5 * P, 1) + \
        straight(kv + 2 * P, 1) + straight(kv + 4 * P, 1) + [[(0, 1792, 1816)]]
    branch = np.concatenate([a["w_pool_out"]] + [a["w_nsa_out"][DH * h:DH * (h + 1)] for h in
                                                 (0, 4, 1, 5, 2, 6, 3, 7)])

    def gate_and_value(w):
        t = by_tiles(w)
        return np.stack([t[:FK], t[FK:]], 1).reshape(2 * FK, P, -1)

    def in_halves(w):
        t = by_tiles(w)
        return np.ascontiguousarray(t.reshape(DK, P, 2, -1).transpose(0, 2, 1, 3)).reshape(2 * DK, P, -1)

    w2 = a["w_in_2"]
    small = [[(0, 2048, 2052), (32, 2052, 2056)]]
    feeds = {
        "w_in1": by_tiles(a["w_in"], in1),
        "w_fill1": by_tiles(a["w_in"], gate_pairs(1816)),
        "w_mix1": by_tiles(branch),
        "w_out1": by_tiles(a["w_out"]),
        "w_up1": gate_and_value(a["w_up"]),
        "w_down1": in_halves(a["w_down"]),
        "w_in2c": by_tiles(w2, straight(0, 12)),
        "w_in2z": by_tiles(w2, straight(1536, 4) + small),
        "w_fill2": by_tiles(w2, straight(2056, 12) + gate_pairs(2056 + 1536)),
        "w_mix2": by_tiles(np.concatenate([a["w_branch_a_2"], a["w_branch_b_2"]])),
        "w_out2": by_tiles(a["w_out_2"]),
        "w_up2": gate_and_value(a["w_up_2"]),
        "w_down2": in_halves(a["w_down_2"]),
        "x": np.ascontiguousarray(a["x"].T.reshape(DK, P, T).transpose(1, 0, 2)),
        "positions": a["positions"][None, :],
        "rel": a["rel_bias_2"],
        "cmp_w1": np.ascontiguousarray(a["cmp_w1"].transpose(2, 0, 1, 3)).reshape(DH, 2, 32 * P),
        "cmp_w2": np.ascontiguousarray(a["cmp_w2"].transpose(1, 0, 2)),
        "pool_w": np.ascontiguousarray(a["pool_w"].transpose(1, 0, 2)),
        "consts": constants(),
    }
    prm = np.zeros((P, N_PARAM), np.float32)

    def put(name, value, rows_=slice(0, P)):
        at, n = PARAM[name]
        prm[rows_, at:at + n] = value

    put("gain", np.concatenate([by_columns(a[n]) for n in (
        "mix_norm_g", "ffn_norm_g", "norm_mix_w_2", "norm_ffn_w_2", "norm_final_w_2")], 1))
    twice = (slice(0, DH), slice(DH, P))
    for r in twice:
        put("q_gain", a["q_norm_g"][:, None], r)
        put("k_gain", a["k_norm_g"].T, r)
        put("pe", a["cmp_pe"].transpose(2, 0, 1).reshape(DH, 64), r)
    put("pool_scale", by_columns(a["pool_scale"]))

    def taps(w, b=None):
        rows_ = [by_columns(x) for x in w] + ([by_columns(b)] if b is not None else [])
        return np.stack(rows_, 2).reshape(P, -1)

    put("conv1", taps(a["conv_w"], a["conv_b"]))
    put("conv2", taps(a["conv_ffn_w_2"], a["conv_ffn_b_2"]))
    put("conv_qkv", taps(a["conv_qkv_w_2"]))
    put("gdn_gain", a["gdn_norm_w_2"][:, None])
    put("a_log", a["a_log_2"][:, None], slice(32, 32 + GH))
    put("dt_bias", a["dt_bias_2"][:, None], slice(32, 32 + GH))
    feeds["params"] = prm

    nc = bacc.Bacc("TRN2", target_bir_lowering=False, num_devices=1)
    t_in = {name: nc.dram_tensor("in_" + name, v.shape, mybir.dt.from_np(v.dtype), kind="ExternalInput").ap()
            for name, v in feeds.items()}
    out = nc.dram_tensor("out_t", (P, DK, T), F32, kind="ExternalOutput").ap()
    two_blocks(nc, t_in, out)
    r = run_bass_kernel_spmd(nc, [{"in_" + k: v for k, v in feeds.items()}], core_ids=[0])
    got = np.asarray(r.results[0]["out_t"]).reshape(P, DK, T)
    return got.transpose(2, 1, 0).reshape(1, T, D)
```

```python
from contextlib import ExitStack

import numpy as np

import concourse.bass as bass
from concourse import mybir

F32 = mybir.dt.float32
F32R = mybir.dt.float32r
I32 = mybir.dt.int32
ALU = mybir.AluOpType
ACT = mybir.ActivationFunctionType
AXX = mybir.AxisListType.X

P = 128
T = 512
D = 1024
DK = D // P
FF = 2816
FK = FF // P
NT = T // P
NH = 8
DH = 64
GH = 4
CH = 64
NCH = T // CH
NCMP = (T - 32) // 16 + 1
NEG = -1.0e30
EPS = 1e-6
CMP_PIECES = 8
SLOT = 11 * P

STAGES = [
    ("in1", 15, 1, DK), ("fill1", 2 * DK, 1, DK), ("mix1", DK, 1, DK), ("out1", DK, 1, DK), ("up1", FK, 2, DK), ("down1", DK, 2, FK // 2),
    ("in2c", 12, 1, DK), ("in2z", 5, 1, DK), ("fill2", 12 + 2 * DK, 1, DK), ("mix2", DK, 1, DK), ("out2", DK, 1, DK), ("up2", FK, 2, DK),
    ("down2", DK, 2, FK // 2),
]

PIECES = 4


def fill_plan(steps):
    plan, total = {}, 0
    for name, n, num, den in steps:
        start = total
        for i in range(n):
            behind = start + num * (i + 1) // den
            plan[name, i] = (total, behind)
            total = behind
    return plan, total


FILL2, FILLED2 = fill_plan([("start", 1, 3, 1), ("norm", 8, 2, 1), ("gates", 2, 3, 1), ("rows", 4, 2, 1), ("ready", 1, 3, 1), ("first", 4, 1, 1),
                            ("level", 20, 9, 10), ("chunk", 8, 3, 2), ("out", 4, 3, 1), ("turn", 4, 2, 1),
                            ("unit", 32, 22, 32)])
FILL1, FILLED1 = fill_plan([("start", 1, 3, 1), ("norm", 6, 2, 1), ("turn", 3, 3, 1), ("compress", 5, 1, 1), ("scores", 2, 3, 1),
                            ("unit", 64, 29, 64)])
assert FILLED1 == PIECES * 2 * DK
assert FILLED2 == PIECES * (12 + 2 * DK)

CONST = {}
_at = 0
for _name, _n in (("ident", P), ("ones", P), ("halves", P), ("rot", P), ("causal", T), ("level", 6 * P),
                  ("decay", P), ("strict", P), ("pick", 2 * GH * P), ("cmp", NT * NCMP), ("reset", T),
                  ("count", 4 * 16), ("cmp_any", 1), ("inv", 1)):
    CONST[_name] = (_at, _n)
    _at += _n
N_CONST = _at

PARAM = {}
_at = 0
for _name, _n in (("gain", 5 * DK), ("q_gain", 1), ("k_gain", 3), ("pe", 2 * 32), ("pool_scale", 4),
                  ("conv1", FK * 4), ("conv2", 2 * FK * 4), ("conv_qkv", 12 * 4), ("gdn_gain", 1),
                  ("a_log", 1), ("dt_bias", 1)):
    PARAM[_name] = (_at, _n)
    _at += _n
N_PARAM = _at


def constants():
    c = np.zeros((P, N_CONST), np.float32)
    p = np.arange(P)[:, None]
    m = np.arange(P)[None, :]

    def put(name, value):
        at, n = CONST[name]
        c[:, at:at + n] = value

    put("ident", p == m)
    put("ones", 1.0)
    put("halves", p // DH == m // DH)
    rot = np.zeros((P, P), np.float32)
    for half in (0, DH):
        for d in range(8):
            rot[half + d + 8, half + d] = -1.0
            rot[half + d, half + d + 8] = 1.0
    put("rot", rot)
    put("causal", np.where(np.arange(T)[None, :] - (T - P) <= p, 0.0, NEG))
    lev = np.zeros((P, 6, P), np.float32)
    for s in range(6):
        w = 2 ** s
        lev[:, s] = (p // (2 * w) == m // (2 * w)) & (p // w % 2 == 0) & (m // w % 2 == 1)
    put("level", lev.reshape(P, -1))
    put("decay", np.where((p // CH == m // CH) & (m >= p), 0.0, NEG))
    put("strict", m > p)
    pick = np.zeros((P, 2 * GH, P), np.float32)
    for h in range(GH):
        pick[h, h] = 1.0
        pick[32 + h, GH + h] = 1.0
    put("pick", pick.reshape(P, -1))
    tok = (np.arange(NT)[None, :, None] * P + np.arange(P)[:, None, None])
    put("cmp", np.where(np.arange(NCMP)[None, None, :] * 16 + 31 <= tok, 0.0, NEG).reshape(P, -1))
    put("reset", np.arange(T)[None, :] % CH != 0)
    t = np.arange(16)
    put("count", np.stack([1.0 / np.minimum(t + 1, w) for w in (2, 4, 8, 16)]).reshape(1, -1))
    put("cmp_any", p >= 31)
    inv = np.zeros((P, 1), np.float32)
    freq = np.float32(500000.0) ** (-(np.arange(8, dtype=np.float32) * np.float32(2.0) / np.float32(16)))
    for half in (0, DH):
        inv[half:half + 8, 0] = freq
        inv[half + 8:half + 16, 0] = freq
    put("inv", inv)
    return c


def lin(a, b, i):
    return a + b * i if isinstance(i, int) else i * b + a


class Chunk:

    def __init__(self, first, half, i, index, loop):
        self.first, self.half, self.i, self.index, self.loop = first, half, i, index, loop
        self.slot = first % 2

    def count(self, more=0):
        return lin(self.first + more, 2 * self.half, self.i)

    def loads(self):
        return lin(16 * (self.first // 2 + 1), 16 * self.half, self.i)


def units(eng, n):
    full = n // 2
    for j in range(2):
        yield 0, j
    if full > 2:
        with eng.Fori(1, full - 1) as i:
            for j in range(2):
                yield i, j
    for u in range(2 * (full - 1), n):
        yield u // 2, u % 2


def chunk_table():
    base, at, sizes = {}, 0, []
    for name, n, per, kt in STAGES:
        base[name] = at
        sizes += [kt] * (n * per)
        at += n * per
    return base, sizes


def two_blocks(nc, t_in, out):
    BASE, SIZES = chunk_table()
    INFO = {name: (n, per, kt) for name, n, per, kt in STAGES}
    NCHUNK = len(SIZES)

    def chunk(name, i, j, q=0):
        n, per, kt = INFO[name]
        local = per * j + q
        return Chunk(BASE[name] + local, per, i, lin(local, 2 * per, i), not isinstance(i, int))

    ctx = ExitStack()
    with ctx:
        kb = 1024
        base = -(-nc.sbuf_base // 64) * 64

        def sb(name, shape, dt, at):
            return nc.alloc_sbuf_tensor_at(name, shape, dt, offset=base + int(at))

        def sem(name):
            return ctx.enter_context(nc.semaphore(name))

        at = 0
        w_raw = sb("w_raw", [P, 2, SLOT], F32, at); at += 2 * SLOT * 4
        w_hi = sb("w_hi", [P, 2, SLOT], F32R, at); at += 2 * SLOT * 4
        w_lo = sb("w_lo", [P, 2, SLOT], F32R, at); at += 2 * SLOT * 4
        X = sb("X", [P, DK, T], F32, at); at += DK * T * 4
        h_hi = sb("h_hi", [P, DK, T], F32R, at); at += DK * T * 4
        h_lo = sb("h_lo", [P, DK, T], F32R, at); at += DK * T * 4
        y_out = sb("y_out", [P, DK, T], F32, at - 2 * DK * T * 4)
        consts = sb("consts", [P, N_CONST], F32, at); at += -(-N_CONST * 4 // 64) * 64
        params = sb("params", [P, N_PARAM], F32, at); at += -(-N_PARAM * 4 // 64) * 64
        sq_sum = sb("sq_sum", [P, T], F32, at); at += T * 4
        rms_inv = sb("rms_inv", [P, T], F32, at); at += T * 4
        arena = at
        arena_size = (nc.sbuf_usable_end - base - arena) // 64 * 64

        def area(name, shape, dt, at_kb):
            n = 4 * int(np.prod(shape[1:]))
            assert at_kb * kb + n <= arena_size, (name, at_kb, n, arena_size)
            return sb(name, shape, dt, arena + at_kb * kb)

        def const(name, *shape):
            a, n = CONST[name]
            v = consts[:, a:a + n]
            if len(shape) == 2:
                v = v.rearrange("p (a b) -> p a b", a=shape[0])
            return v

        def param(name, a=0, n=None):
            at, size = PARAM[name]
            return params[:, at + a:at + a + (size - a if n is None else n)]

        gains = param("gain").rearrange("p (a b) -> p a b", b=1)
        ident, ones, halves = const("ident"), const("ones"), const("halves")

        sq_ring = area("sq_ring", [P, 2, T], F32, 97)
        rope = area("rope", [P, 2, T], F32, 84)
        angle = area("angle", [P, 3, T], F32, 62)
        pos_i = area("pos_i", [P, T], I32, 68)
        rel_row = area("rel_row", [NH, 257], F32, 70)
        rel_ext = area("rel_ext", [NH, 640], F32, 72)
        p1 = area("p1", [P, 15, T], F32, 0)
        KC, VC, VS, VW, KS, KW, GT = range(8, 15)
        cmp_w1 = area("cmp_w1", [P, 2, 32 * P], F32, 30)
        cmp_blk = area("cmp_blk", [P, 2, 32, 2, NCMP], F32, 62)
        nr_sq = area("nr_sq", [P, 2, T], F32, 62)
        nr_r = area("nr_r", [P, 2, T], F32, 66)
        nr_c = area("nr_c", [P, 2, T], F32, 70)
        nr_s = area("nr_s", [P, 2, T], F32, 74)
        v1_nat = area("v1_nat", [P, 2, NT, P], F32, 78)
        pool_w = area("pool_w", [P, 4, P], F32, 82)
        pool_pad = area("pool_pad", [P, 2, 16 + T], F32, 88)
        cmp_w2 = area("cmp_w2", [P, 2, DH], F32, 92.25)
        gate_t = area("gate_t", [P, NT, 24], F32, 92.75)
        hid = area("hid", [2 * NCMP, 2, P], F32, 93.25)
        hid_t = area("hid_t", [P, 2, 2 * NCMP], F32, 94.25)
        kc_t = area("kc_t", [P, NCMP], F32, 94.75)
        vc_nat = area("vc_nat", [NCMP, 2, DH], F32, 95)
        cmp_red = area("cmp_red", [P, 3, 4 * NT * 2], F32, 95.5)
        cmp_s = area("cmp_s", [P, 2, NT, 4, NCMP], F32, 96)
        kc_tmp = area("kc_tmp", [P, 4, NCMP], F32, 100)
        cols1 = area("cols1", [P, 12], F32, 100.5)
        pc_t = area("pc_t", [NCMP, NT * NH, P], F32, 30)
        at1_sm = area("at1_sm", [P, 2, T], F32, 62)
        at1_p = area("at1_p", [P, 3, T], F32, 66)
        at1_pt = area("at1_pt", [P, 2, T], F32, 72)
        o1_hi = area("o1_hi", [P, 4, T], F32R, 46)
        o1_lo = area("o1_lo", [P, 4, T], F32R, 54)
        yp_hi = area("yp_hi", [P, 4, T], F32R, 0)
        yp_lo = area("yp_lo", [P, 4, T], F32R, 16)
        sg1 = area("sg1", [P, 2, 2, T], F32, 82)
        mt1 = area("mt1", [P, 3, T], F32, 8)
        stage1 = area("stage1", [P, 2, T], F32, 101)
        mix1_hi = area("mix1_hi", [P, DK, T], F32R, 24)
        mix1_lo = area("mix1_lo", [P, DK, T], F32R, 62)
        act_hi = area("act_hi", [P, FK, T], F32R, 0)
        act_lo = area("act_lo", [P, FK, T], F32R, 44)
        t_gate = area("t_gate", [P, 2, T], F32, 88)
        t_val = area("t_val", [P, 2, T], F32, 92)
        t_raw = area("t_raw", [P, 2, T], F32, 96)
        p2a = area("p2a", [P, 17, T], F32, 0)
        cv = area("cv", [P, 2, T], F32, 74)
        cv_raw = area("cv_raw", [P, 2, T], F32, 86)
        l2_sq = area("l2_sq", [P, 2, T], F32, 78)
        l2_r = area("l2_r", [P, 2, T], F32, 82)
        a_t = area("a_t", [P, GH, NT, P], F32, 34)
        x_inv = area("x_inv", [P, GH, NT, P], F32, 42)
        y_inv = area("y_inv", [P, GH, NT, P], F32, 50)
        p_t = area("p_t", [P, GH, NT, P], F32, 58)
        k_dec = area("k_dec", [P, GH, NT, P], F32, 66)
        gam_row = area("gam_row", [P, T], F32, 74)
        dec = area("dec", [P, NT, P], F32, 76)
        beta_strict = area("beta_strict", [P, NT, P], F32, 78)
        b_t = area("b_t", [P, GH, NT, P], F32, 76)
        bx = area("bx", [P, 2, NT, P], F32, 84)
        state = area("state", [P, 2, GH, P], F32, 88)
        u_new = area("u_new", [P, 2, GH, P], F32, 92)
        gd_cols = area("gd_cols", [P, NT, 64], F32, 96)
        gd_neg = area("gd_neg", [P, NT, GH], F32, 97)
        gd_bg = area("gd_bg", [P, NT, GH], F32, 97.25)
        gd_kd = area("gd_kd", [P, GH, NT], F32, 97.5)
        gd_last = area("gd_last", [P, GH, NCH], F32, 97.75)
        o_red = area("o_red", [P, NT * GH], F32, 98)
        gb_rows = area("gb_rows", [64, T], F32, 99)
        gz = area("gz", [64, T], F32, 42)
        gz2 = area("gz2", [64, T], F32, 44)
        stage2 = area("stage2", [P, 2, T], F32, 101)
        ea = area("ea", [64, 2], F32, 105)
        k_bg = p2a[:, 4:8, :].rearrange("p h (c d) -> p h c d", c=NT)
        v_b = p2a[:, 8:12, :].rearrange("p h (c d) -> p h c d", c=NT)
        w_t, uv = x_inv, a_t
        o_nat = p2a[:, 4:8, :].rearrange("p c (h d) -> p c h d", h=GH)
        o_sq = p2a[:, 8:12, :].rearrange("p c (h d) -> p c h d", h=GH)
        oa = area("oa", [P, 2, T], F32, 34)
        oa_hi = area("oa_hi", [P, 4, T], F32R, 58)
        oa_lo = area("oa_lo", [P, 4, T], F32R, 66)
        p2b = area("p2b", [P, 12, T], F32, 0)
        rel = area("rel", [P, NH, T], F32, 24)
        v2_nat = area("v2_nat", [P, NT, T], F32, 40)
        at2_sm = area("at2_sm", [P, 2, T], F32, 74)
        at2_p = area("at2_p", [P, 3, T], F32, 78)
        at2_pt = area("at2_pt", [P, 2, T], F32, 84)
        cols2 = area("cols2", [P, 12], F32, 56)
        ob_hi = area("ob_hi", [P, 4, T], F32R, 48)
        ob_lo = area("ob_lo", [P, 4, T], F32R, 88)
        sg2 = area("sg2", [P, 2, 2, T], F32, 16)
        mt2 = area("mt2", [P, 3, T], F32, 40)
        mix2_hi = area("mix2_hi", [P, DK, T], F32R, 0)
        mix2_lo = area("mix2_lo", [P, DK, T], F32R, 24)

        banks = ctx.enter_context(nc.psum_tensor("banks", [P, 8, T], F32))
        ACC, BS, BT, BO = 0, 2, 4, 6
        POOLED = (BS + 1, BT + 1)

        def bank(n, shape=None):
            v = banks[:, n, :]
            return v.rearrange("p (a b) -> p a b", a=shape) if shape else v

        late1 = nc.dram_tensor("late1_scratch", (DK, 2, P, T), F32, kind="Internal").ap()
        late2 = nc.dram_tensor("late2_scratch", (6 + DK, 2, P, T), F32, kind="Internal").ap()
        rel_dram = nc.dram_tensor("rel_scratch", (NH, 640), F32, kind="Internal").ap()

        w_loaded = [sem(f"w_loaded{s}") for s in range(2)]
        hi_ready = sem("hi_ready")
        lo_ready = sem("lo_ready")
        chunk_done = sem("chunk_done")
        first_half = [sem(f"first_half{b}") for b in (1, 2)]
        consts_in, params_in = sem("consts_in"), sem("params_in")
        x_in = [sem(f"x_in{q}") for q in range(4)]
        pos_in, rel_in, cmp_in = sem("pos_in"), sem("rel_in"), sem("cmp_in")
        rel_stored, rel_loaded = sem("rel_stored"), sem("rel_loaded")
        start_step = sem("start_step")
        sin_done = sem("sin_done")
        copied = {n: sem("copied_" + n) for n in ("in1", "in2z")}
        filled = [sem("filled1"), sem("filled2")]
        late_stored = [[sem(f"late_stored{b}{s}") for s in range(2)] for b in (1, 2)]
        gate_in = [[sem(f"gate_in{b}{s}") for s in range(2)] for b in (1, 2)]
        qkv_in = {n: sem(n + "2_in") for n in "qkv"}
        x_done = sem("x_done")
        sq_done = sem("sq_done")
        sum_done = sem("sum_done")
        mean_done = sem("mean_done")
        ln_done = sem("ln_done")
        inv_done = sem("inv_done")
        y_done = sem("y_done")
        hh_done = sem("hh_done")
        hl_done = sem("hl_done")
        out_stored = sem("out_stored")
        gate_sig = [sem(f"gate_sig{b}") for b in (1, 2)]
        y_pool_done = [sem(f"y_first{b}") for b in (1, 2)]
        y_nsa_done = [sem(f"y_second{b}") for b in (1, 2)]
        mixed = [sem(f"mixed{b}") for b in (1, 2)]
        mix_hh = [sem(f"mix_hh{b}") for b in (1, 2)]
        mix_hl = [sem(f"mix_hl{b}") for b in (1, 2)]
        conv_done = [sem(f"conv_done{b}") for b in (1, 2)]
        silu_done = [sem(f"silu_done{b}") for b in (1, 2)]
        gated = [sem(f"gated{b}") for b in (1, 2)]
        act_hh = [sem(f"act_hh{b}") for b in (1, 2)]
        act_hl = [sem(f"act_hl{b}") for b in (1, 2)]
        cv_done, cv_silu = sem("cv_done"), sem("cv_silu")
        n_sq, n_ms, n_ln, n_inv, n_gain = (sem("n_" + x) for x in ("sq", "ms", "ln", "inv", "gain"))
        n_rot, n_cos, n_sin, n_sum = (sem("n_" + x) for x in ("rot", "cos", "sin", "sum"))
        l_sq, l_ms, l_ln, l_inv, l_out = (sem("l_" + x) for x in ("sq", "ms", "ln", "inv", "out"))
        turned = [sem(f"turned{b}") for b in (1, 2)]
        v_copied = [sem(f"v_copied{b}") for b in (1, 2)]
        gates_ready = sem("gates_ready")
        pad_zero, blk_zero = sem("pad_zero"), sem("blk_zero")
        pooled = sem("pooled")
        pool_mul = sem("pool_mul")
        yp_h, yp_l = sem("yp_h"), sem("yp_l")
        blk_done = sem("blk_done")
        c_pe, c_act, c_dve = sem("c_pe"), sem("c_act"), sem("c_dve")
        s_pe, s_act, s_dve = sem("s_pe"), sem("s_act"), sem("s_dve")

        class Attention:

            def __init__(self, b, units_, per_tile, sm, p, pt, cols, o_hi, o_lo):
                self.units, self.per_tile = units_, per_tile
                self.sm, self.p, self.pt, self.o_hi, self.o_lo = sm, p, pt, o_hi, o_lo
                self.nbias, self.sums, self.inv = cols[:, 0:4], cols[:, 4:8], cols[:, 8:12]
                self.scored = sem(f"scored{b}")
                self.masked = sem(f"masked{b}")
                self.shifted = sem(f"shifted{b}")
                self.exped = sem(f"exped{b}")
                self.inverted = sem(f"inverted{b}")
                self.weighted = sem(f"weighted{b}")
                self.flipped = sem(f"flipped{b}")
                self.fetched = sem(f"fetched{b}")
                self.summed = sem(f"summed{b}")
                self.high = sem(f"o_high{b}")
                self.low = sem(f"o_low{b}")

        att1 = Attention(1, [(j, i, b, half) for j in range(4) for i in range(NT) for b in range(2)
                             for half in range(2)], 4 * NT, at1_sm, at1_p, at1_pt, cols1, o1_hi, o1_lo)
        att2 = Attention(2, [(j, i, 0, half) for j in range(4) for i in range(NT) for half in range(2)],
                         2 * NT, at2_sm, at2_p, at2_pt, cols2, ob_hi, ob_lo)
        d_pe, d_dve, d_act = sem("d_pe"), sem("d_dve"), sem("d_act")
        g_pe, g_dve, g_act = sem("g_pe"), sem("g_dve"), sem("g_act")
        i_mask, i_bx, i_cp, i_pe, i_x, i_y = (sem("i_" + x) for x in ("mask", "bx", "cp", "pe", "x", "y"))
        r_w, r_cp, r_ws, r_u, r_ds, r_s, r_o, r_ocp = (
            sem("r_" + x) for x in ("w", "cp", "ws", "u", "ds", "s", "o", "ocp"))
        f_dve, f_act, f_pe = sem("f_dve"), sem("f_act"), sem("f_pe")
        oa_h, oa_l = sem("oa_h"), sem("oa_l")

        LATE_BANK = (1, 1)

        block = ctx.enter_context(nc.Block())

        WITH_X = 4 * GH

        def corrected(k):
            return 2 * min(k + 1, WITH_X) + max(k + 1 - WITH_X, 0)

        def level(n):
            return const("level", 6, P)[:, n, :].unsqueeze(1).to_broadcast([P, NT, P])

        def rows(half):
            return slice(half * DH, (half + 1) * DH)

        def ahead(c, q_kt):
            if c.loop:
                return Chunk(c.first + 2, c.half, c.i, None, True), q_kt
            n = c.count() + 2
            return (Chunk(n, 0, 0, None, False), SIZES[n]) if n < NCHUNK else (None, 0)

        def wait(eng, s, value):
            if not isinstance(value, int) or value > 0:
                eng.wait_ge(s, value)

        @block.sync
        def _(sp):
            def cmp_piece(e):
                sp.dma_start(cmp_w1.rearrange("p c (e n) -> p (c e) n", e=CMP_PIECES // 2)[:, e, :],
                             t_in["cmp_w1"][e]).then_inc(cmp_in, 16)

            def load(c, name, kt):
                wait(sp, lo_ready, c.count(-1))
                sp.dma_start(w_raw[:, c.slot, 0:kt * P], t_in["w_" + name][c.index]).then_inc(w_loaded[c.slot], 16)

            def store_late(b, late, stage, n):
                sp.wait_ge(filled[b], n + 1)
                sp.dma_start(late[n // 2, n % 2], stage[:, n % 2, :]).then_inc(late_stored[b][n % 2], 16)

            def late(name, b, scratch, stage):
                n = INFO[name][0]
                for c in range(n):
                    load(chunk(name, c // 2, c % 2), name, DK)
                    if c >= 3:
                        store_late(b, scratch, stage, c - 3)

            def merge(name, b, last, late_, scratch, stage, first_gate, sg):
                n = INFO[late_][0]

                def gates(m, j):
                    sp.dma_start(sg[:, j, :, :], scratch.rearrange("n a p t -> n p a t")[m + first_gate])\
                        .then_inc(gate_in[b][j], 16)

                for i, j in units(sp, DK):
                    load(chunk(name, i, j), name, DK)
                    m = lin(j, 2, i)
                    if isinstance(m, int) and m == 0:
                        store_late(b, scratch, stage, n - 3)
                        last()
                        for j_ in range(2):
                            for half in range(2):
                                sp.wait_ge(late_stored[b][half], 16 * (first_gate + j_ + 1))
                            gates(j_, j_)
                    elif isinstance(m, int) and m == 1:
                        store_late(b, scratch, stage, n - 2)
                        store_late(b, scratch, stage, n - 1)
                        sp.wait_ge(late_stored[b][0], 16 * ((n + 1) // 2))
                        sp.wait_ge(late_stored[b][1], 16 * (n // 2))
                    else:
                        sp.wait_ge(y_nsa_done[b], m - 1)
                        gates(m, j)

            for name, n, per, kt in STAGES:
                if name == "fill1":
                    late(name, 0, late1, stage1)
                elif name == "mix1":
                    merge(name, 0, lambda: sp.wait_ge(pool_mul, 4), "fill1", late1, stage1, 0, sg1)
                elif name == "in1":
                    for i, j in units(sp, n):
                        if isinstance(i, int) and i == 0:
                            for q in range(2 * j, 2 * j + 2):
                                sp.dma_start(X[:, 2 * q:2 * q + 2, :], t_in["x"][:, 2 * q:2 * q + 2, :])\
                                    .then_inc(x_in[q], 16)
                                if q == 0:
                                    load(chunk(name, i, j), name, kt)
                        if not (isinstance(i, int) and i == 0 and j == 0):
                            load(chunk(name, i, j), name, kt)
                        if isinstance(i, int) and i == 0 and j == 1:
                            sp.dma_start(consts[:, :], t_in["consts"]).then_inc(consts_in, 16)
                        if not isinstance(i, int) and j == 0:
                            cmp_piece(i + -1)
                        elif isinstance(i, int) and i > 0:
                            cmp_piece(CMP_PIECES - n + 2 * i + j)
                elif name == "fill2":
                    late(name, 1, late2, stage2)
                elif name == "mix2":
                    merge(name, 1, lambda: sp.wait_ge(turned[1], 4), "fill2", late2, stage2, 6, sg2)
                else:
                    for i, j in units(sp, n):
                        for q in range(per):
                            load(chunk(name, i, j, q), name, kt)
            for m in range(DK):
                sp.wait_ge(y_done, m + 1)
                sp.dma_start(out[:, m, :], y_out[:, m, :]).then_inc(out_stored, 16)
            sp.wait_ge(out_stored, 16 * DK)

        @block.gpsimd
        def _(pool):
            def low(c, kt):
                pool.wait_ge(hi_ready, c.count(1))
                pool.tensor_tensor(w_lo[:, c.slot, 0:kt * P], w_raw[:, c.slot, 0:kt * P],
                                   w_hi[:, c.slot, 0:kt * P], ALU.subtract).then_inc(lo_ready, 1)

            def split(name):
                n, per, kt = INFO[name]
                for i, j in units(pool, n):
                    for q in range(per):
                        c2, kt2 = ahead(chunk(name, i, j, q), kt)
                        if c2:
                            low(c2, kt2)

            step = [0]

            def pool_step(ins):
                step[0] += 1
                ins.then_inc(pooled, 1)
                pool.wait_ge(pooled, step[0])

            def pooling(gi):
                w, cur, u = 2 ** (gi + 1), 0, p1[:, gi, :]
                pool_step(pool.tensor_copy(pool_pad[:, 0, 16:], u))
                d = 1
                while d < w:
                    pool_step(pool.tensor_tensor(pool_pad[:, 1 - cur, 16:], pool_pad[:, cur, 16:],
                                                 pool_pad[:, cur, 16 - d:16 + T - d], ALU.add))
                    cur, d = 1 - cur, 2 * d
                s, m = pool_pad[:, cur, :], pool_pad[:, 1 - cur, :]
                pool_step(pool.tensor_scalar(m[:, 32:], s[:, 32:], 1.0 / w, None, ALU.mult))
                pool_step(pool.tensor_tensor(m[:, 16:32], s[:, 16:32], const("count", 4, 16)[:, gi, :], ALU.mult))
                pool_step(pool.tensor_tensor(u, m[:, 16:], u, ALU.subtract))

            def lows(name, plan, total):
                state = [0]

                def serve(*at):
                    upto = (plan[at][0] if at else total) // PIECES
                    while state[0] < upto:
                        low(*ahead(chunk(name, state[0] // 2, state[0] % 2), DK))
                        state[0] += 1
                return serve

            def weights(a, gated_, serve=None):
                for u, (j, i, b, half) in enumerate(a.units):
                    w = (i + 1) * P
                    pr = a.p[:, u % 3, 0:w]
                    pool.wait_ge(a.inverted, u + 1)
                    if gated_:
                        g = (j + 4 * half) * 3 + 1 + b
                        ins = pool.tensor_scalar(pr, pr, a.inv[:, u % 4:u % 4 + 1], gate_t[:, i, g:g + 1],
                                                 ALU.mult, ALU.mult)
                    else:
                        ins = pool.tensor_scalar(pr, pr, a.inv[:, u % 4:u % 4 + 1], None, ALU.mult)
                    ins.then_inc(a.weighted, 1)
                    if serve:
                        serve("unit", u)

            low(Chunk(0, 0, 0, None, False), DK)
            low(Chunk(1, 0, 0, None, False), DK)
            split("in1")
            pool.wait_ge(copied["in1"], 15)
            pool.wait_ge(consts_in, 16)
            pool.memset(pool_pad[:, :, 0:16], 0.0).then_inc(pad_zero, 1)
            pool.wait_ge(pad_zero, 1)
            serve = lows("fill1", FILL1, FILLED1)
            serve("norm", 2)
            pooling(0)
            serve("norm", 4)
            pooling(1)
            serve("norm", 5)
            pool.wait_ge(n_sum, 6)
            pool.memset(cmp_blk[:, :, :, :, :], 0.0).then_inc(blk_zero, 1)
            serve("turn", 2)
            pooling(2)
            pooling(3)
            serve("compress", 4)
            serve("scores", 0)
            serve("scores", 1)
            weights(att1, True, serve)
            serve()
            for name in ("mix1", "out1", "up1", "down1", "in2c", "in2z"):
                split(name)
            pool.wait_ge(copied["in2z"], 5)
            pool.memset(gb_rows[:, :], 0.0).then_inc(blk_zero, 1)
            serve = lows("fill2", FILL2, FILLED2)
            for h in range(GH):
                if h < 3:
                    serve("rows", h + 1)
                if h == 2:
                    serve("ready", 0)
                pool.wait_ge(d_dve, 11 * (h + 1) if h < 2 else 11 * GH)
                pool.tensor_tensor(b_t[:, (h + 2) % GH, :, :], a_t[:, h, :, :], level(0), ALU.mult).then_inc(i_mask, 1)
            for k in range(5 * GH):
                pool.wait_ge(i_bx, k + 1)
                pool.wait_ge(i_y, min(k + 1, GH))
                pool.tensor_tensor(b_t[:, (k + 2) % GH, :, :], a_t[:, k % GH, :, :], level(1 + k // GH), ALU.mult)\
                    .then_inc(i_mask, 1)
                serve("first", k) if k < GH else serve("level", k - GH)
            for k in range(4 * GH, 5 * GH):
                serve("level", k)
            for c in range(NCH):
                serve("chunk", c)
            for n in range(4):
                serve("out", n)
            for v in range(4):
                serve("turn", v)
            pool.wait_ge(rel_loaded, 16)
            pool.memset(rel[0:CH, :, 0:CH], NEG).then_inc(blk_zero, 1)
            weights(att2, False, serve)
            serve()
            for name in ("mix2", "out2", "up2", "down2"):
                split(name)

        @block.scalar
        def _(act):
            def high(c, kt):
                act.wait_ge(w_loaded[c.slot], c.loads())
                wait(act, chunk_done, c.count(-1))
                act.activation(w_hi[:, c.slot, 0:kt * P], w_raw[:, c.slot, 0:kt * P], ACT.Copy)\
                    .then_inc(hi_ready, 1)

            def next_high(name, i, j, q=0):
                c2, kt2 = ahead(chunk(name, i, j, q), INFO[name][2])
                if c2:
                    high(c2, kt2)

            def plain(name, behind_pair=None):
                for i, j in units(act, INFO[name][0]):
                    next_high(name, i, j)
                    if behind_pair and isinstance(i, int) and i == 0 and j == 1:
                        behind_pair()

            def late(name, plan, total):
                state = [0]

                def serve(*at):
                    upto = (plan[at][0] if at else total) // PIECES
                    while state[0] < upto:
                        next_high(name, state[0] // 2, state[0] % 2)
                        state[0] += 1
                return serve

            def logs_and_exps():
                act.preload_act_table_set("natural_log_exp_and_others")

            def norm(n):
                logs_and_exps()
                act.wait_ge(mean_done, n + 1)
                act.activation(rms_inv[:, :], bank(BS), ACT.Ln, bias=EPS, scale=1.0 / D).then_inc(ln_done, 1)
                act.wait_ge(ln_done, n + 1)
                act.activation(rms_inv[:, :], rms_inv[:, :], ACT.Exp, scale=-0.5).then_inc(inv_done, 1)

            def gained(n, m, j):
                if n < 4:
                    act.activation(h_hi[:, m, :], X[:, m, :], ACT.Copy, scale=gains[:, m + DK * n, :])\
                        .then_inc(hh_done, 1)
                wait(act, sum_done, m + (DK * n - 1))
                act.activation(sq_ring[:, j, :], X[:, m, :], ACT.Square).then_inc(sq_done, 1)

            def residual(name, n):
                for m in range(DK):
                    i, j = m // 2, m % 2
                    for q in range(INFO[name][1]):
                        next_high(name, i, j, q)
                    act.wait_ge(x_done, lin(DK * (n - 1) + j + 1, 2, i))
                    gained(n, lin(j, 2, i), j)

            def merge(name, b, sg, mt, mix_hi):
                for i, j in units(act, DK):
                    m = lin(j, 2, i)
                    act.wait_ge(gate_in[b][j], lin(16, 16, i))
                    act.activation(sg[:, j, :, :], sg[:, j, :, :], ACT.Sigmoid).then_inc(gate_sig[b], 1)
                    next_high(name, i, j)
                    act.wait_ge(mixed[b], lin(j + 1, 2, i))
                    act.activation(mix_hi[:, m, :], mt[:, 2, :], ACT.Copy).then_inc(mix_hh[b], 1)

            def ffn(name, b, steps):
                for i, j in units(act, FK):
                    next_high(name, i, j, 0)
                    act.wait_ge(conv_done[b], lin(steps * j + 4, 2 * steps, i))
                    act.activation(t_gate[:, j, :], t_gate[:, j, :], ACT.Silu).then_inc(silu_done[b], 1)
                    next_high(name, i, j, 1)
                    act.wait_ge(gated[b], lin(j + 1, 2, i))
                    act.activation(act_hi[:, lin(j, 2, i), :], t_gate[:, j, :], ACT.Copy).then_inc(act_hh[b], 1)

            def inverse_roots(tiles, sq, rt, s_sq, s_ms, s_ln, s_inv, s_used, scale, serve=None):
                def square(n):
                    wait(act, s_ms, n - 1)
                    act.activation(sq[:, n % 2, :], tiles[n], ACT.Square).then_inc(s_sq, 1)
                square(0)
                square(1)
                logs_and_exps()
                for n in range(len(tiles)):
                    act.wait_ge(s_ms, n + 1)
                    wait(act, s_used, n - 1)
                    act.activation(rt[:, n % 2, :], bank(BS + n % 2), ACT.Ln, bias=EPS, scale=scale)\
                        .then_inc(s_ln, 1)
                    act.wait_ge(s_ln, n + 1)
                    act.activation(rt[:, n % 2, :], rt[:, n % 2, :], ACT.Exp, scale=-0.5).then_inc(s_inv, 1)
                    if serve:
                        serve("norm", n)
                    if n + 2 < len(tiles):
                        square(n + 2)

            def attention(a, serve=None):
                n = len(a.units)
                for s in range(n + 5):
                    if s < n:
                        w = (a.units[s][1] + 1) * P
                        act.wait_ge(a.shifted, s + 1)
                        wait(act, a.flipped, s - 2)
                        act.activation(a.p[:, s % 3, 0:w], a.sm[:, s % 2, 0:w], ACT.Exp,
                                       bias=a.nbias[:, s % 4:s % 4 + 1], scale=DH ** -0.5,
                                       accum_out=a.sums[:, s % 4:s % 4 + 1]).then_inc(a.exped, 1)
                    u = s - 2
                    if 0 <= u < n:
                        w = (a.units[u][1] + 1) * P
                        act.wait_ge(a.flipped, u + 1)
                        wait(act, a.summed, u - 1)
                        act.activation(a.pt[:, u % 2, 0:w], banks[:, BT + u % 2, 0:w], ACT.Copy)\
                            .then_inc(a.fetched, 1)
                    if serve and s < n:
                        serve("unit", s)
                    u = s - 4
                    if 0 <= u < n and u % a.per_tile == a.per_tile - 1:
                        j = u // a.per_tile
                        act.wait_ge(a.summed, u + 1)
                        act.activation(a.o_hi[:, j, :], bank(BO + j % 2), ACT.Copy).then_inc(a.high, 1)

            def fetch(n, first):
                act.dma_start(p2b[:, first:first + 4, :].rearrange("p (n a) t -> p n a t", a=2),
                              late2[first // 2:first // 2 + 2].rearrange("n a p t -> p n a t"))\
                    .then_inc(qkv_in[n], 16)

            act.dma_start(params[:, :], t_in["params"]).then_inc(params_in, 16)
            act.dma_start(pos_i[:, :], t_in["positions"].partition_broadcast(P)).then_inc(pos_in, 16)
            act.dma_start(rel_row[:, :], t_in["rel"]).then_inc(rel_in, 16)
            act.wait_ge(params_in, 16)
            for m in range(DK):
                act.wait_ge(x_in[m // 2], 16)
                gained(0, m, m % 2)
                if m % 4 == 1:
                    high(Chunk(m // 4, 0, 0, None, False), DK)
            norm(0)

            def tables():
                act.wait_ge(start_step, 9)
                act.activation(rope[:, 1, :], angle[:, 1, :], ACT.Sin).then_inc(sin_done, 1)
                act.activation(rope[:, 0, :], angle[:, 2, :], ACT.Sin).then_inc(sin_done, 1)
                act.wait_ge(start_step, 11)
                act.dma_start(rel_dram, rel_ext[:, :]).then_inc(rel_stored, 16)
                act.dma_start(cmp_w2[:, :, :], t_in["cmp_w2"]).then_inc(cmp_in, 16)
                act.dma_start(pool_w[:, :, :], t_in["pool_w"]).then_inc(cmp_in, 16)

            plain("in1", tables)

            act.wait_ge(copied["in1"], GT)
            serve = late("fill1", FILL1, FILLED1)
            inverse_roots([p1[:, t, :] for t in (4, 5, 6, 7, KS, KW)], nr_sq, nr_r, n_sq, n_ms, n_ln, n_inv,
                          n_gain, 1.0 / DH, serve)
            act.wait_ge(copied["in1"], 15)
            act.activation(p1[0:24, GT, :], p1[0:24, GT, :], ACT.Sigmoid).then_inc(gates_ready, 1)
            for v in range(2):
                serve("turn", v)
                act.wait_ge(turned[0], v + 1)
                act.activation(v1_nat[:, v, :, :], bank(BO + v, NT), ACT.Copy).then_inc(v_copied[0], 1)
            act.wait_ge(turned[0], 3)
            act.activation(gate_t[:, :, :], banks[:, BT, 0:NT * 24].rearrange("p (a b) -> p a b", a=NT),
                           ACT.Copy).then_inc(v_copied[0], 1)
            serve("turn", 2)
            for c in range(2):
                act.wait_ge(c_pe, c + 1)
                act.activation(hid[:, c, :], banks[0:2 * NCMP, BS + c, 0:P], ACT.Silu).then_inc(c_act, 1)
            serve("compress", 0)
            for c in range(2):
                act.wait_ge(c_pe, c + 3)
                act.activation(hid_t[:, c, :], banks[:, BT + c, 0:2 * NCMP], ACT.Copy).then_inc(c_act, 1)
            serve("compress", 1)
            act.wait_ge(c_pe, 5)
            act.activation(kc_tmp[:, 0, :], banks[:, BO, 0:NCMP], ACT.Square).then_inc(c_act, 1)
            act.wait_ge(c_pe, 6)
            act.activation(vc_nat[:, :, :], banks[0:NCMP, BO + 1, 0:2 * DH].rearrange("p (a b) -> p a b", a=2),
                           ACT.Copy).then_inc(c_act, 1)
            serve("compress", 2)
            logs_and_exps()
            act.wait_ge(c_pe, 7)
            act.activation(kc_tmp[:, 1, :], banks[:, BS, 0:NCMP], ACT.Ln, bias=EPS, scale=1.0 / DH)\
                .then_inc(c_act, 1)
            act.wait_ge(c_act, 7)
            act.activation(kc_tmp[:, 1, :], kc_tmp[:, 1, :], ACT.Exp, scale=-0.5).then_inc(c_act, 1)
            serve("compress", 3)
            for gi in range(4):
                act.wait_ge(pool_mul, gi + 1)
                act.activation(yp_hi[:, gi, :], bank(POOLED[gi % 2]), ACT.Copy, scale=param("pool_scale", gi, 1))\
                    .then_inc(yp_h, 1)
            serve("compress", 4)
            act.wait_ge(s_dve, 4)
            act.activation(cmp_s[:, :, :, :, :], cmp_s[:, :, :, :, :], ACT.Exp, scale=DH ** -0.5).then_inc(s_act, 1)
            serve("scores", 0)
            serve("scores", 1)
            for r in range(8):
                act.wait_ge(s_pe, 3 + r)
                act.activation(pc_t[:, 4 * r:4 * r + 4, :], banks[0:NCMP, BT + r % 2, :].rearrange(
                    "p (a b) -> p a b", a=4), ACT.Copy).then_inc(s_act, 1)
            attention(att1, serve)
            serve()
            merge("mix1", 0, sg1, mt1, mix1_hi)
            residual("out1", 1)
            norm(1)
            ffn("up1", 0, 5)
            residual("down1", 2)

            norm(2)
            for i, j in units(act, 12):
                next_high("in2c", i, j)
                act.wait_ge(cv_done, lin(5 * j + 5, 10, i))
                act.activation(p2a[:, lin(j, 2, i), :], cv[:, j, :], ACT.Silu).then_inc(cv_silu, 1)
            plain("in2z")
            serve = late("fill2", FILL2, FILLED2)
            inverse_roots([p2a[:, t, :] for t in range(8)], l2_sq, l2_r, l_sq, l_ms, l_ln, l_inv, l_out, 1.0, serve)
            g = slice(32, 32 + GH)
            act.wait_ge(g_dve, 2)
            act.activation(gz2[g, :], gz2[g, :], ACT.Exp, scale=-1.0).then_inc(g_act, 1)
            act.wait_ge(g_act, 1)
            act.activation(gz2[g, :], gz2[g, :], ACT.Ln, bias=1.0).then_inc(g_act, 1)
            act.activation(ea[g, 0:1], params[g, PARAM["a_log"][0]:PARAM["a_log"][0] + 1], ACT.Exp)\
                .then_inc(g_act, 1)
            act.wait_ge(blk_zero, 2)
            act.activation(gb_rows[0:GH, :], p2a[0:GH, 16, :], ACT.Sigmoid).then_inc(g_act, 1)
            logs_and_exps()
            serve("gates", 0)
            act.wait_ge(g_pe, 1)
            act.activation(gd_cols[:, :, :], banks[:, BO, 0:NT * 64].rearrange("p (a b) -> p a b", a=NT),
                           ACT.Copy).then_inc(g_act, 1)
            act.wait_ge(g_act, 5)
            act.activation(gd_bg[:, :, :], gd_cols[:, :, 32:32 + GH], ACT.Exp).then_inc(g_act, 1)
            serve("gates", 1)
            act.wait_ge(g_dve, 7)
            for h in range(GH):
                act.wait_ge(d_pe, 6 * h + 1)
                wait(act, d_dve, 11 * (h - 1) + 5 if h else 0)
                wait(act, d_act, 7 * h)
                act.activation(gam_row[:, :], bank(BS), ACT.Exp).then_inc(d_act, 1)
                act.wait_ge(d_dve, 11 * h + 1)
                for p in range(NT):
                    act.activation(dec[:, p, :], dec[:, p, :], ACT.Exp, bias=gd_neg[:, p, h:h + 1])\
                        .then_inc(d_act, 1)
                act.wait_ge(d_dve, 11 * h + 3)
                act.activation(gd_kd[:, h, :], gd_kd[:, h, :], ACT.Exp).then_inc(d_act, 1)
                act.wait_ge(d_act, 7 * h + 1)
                act.activation(gd_last[:, h, :], gam_row[:, CH - 1:T:CH], ACT.Copy).then_inc(d_act, 1)
                serve("rows", h)
            serve("ready", 0)
            for h in range(GH):
                serve("first", h)
            for k in range(5 * GH):
                act.wait_ge(i_bx, GH + k + 1)
                wait(act, i_pe, corrected(k - 2) if k >= 2 else 0)
                act.activation(bx[:, k % 2, :, :], bank(BT + k % 2, NT), ACT.Copy).then_inc(i_cp, 1)
                serve("level", k)
            for h in range(GH):
                act.wait_ge(r_w, 2 * h + 1)
                act.activation(w_t[:, h, :, :], bank(BT + h % 2, NT), ACT.Copy).then_inc(r_cp, 1)
                act.wait_ge(r_w, 2 * h + 2)
                act.activation(uv[:, h, :, :], bank(BO + h % 2, NT), ACT.Copy).then_inc(r_cp, 1)
            act.activation(p2a[:, 12:16, :], p2a[:, 12:16, :], ACT.Silu).then_inc(f_act, 1)
            logs_and_exps()
            for p in range(NT):
                serve("chunk", 2 * p)
                serve("chunk", 2 * p + 1)
                act.wait_ge(r_o, 2 * p + 2)
                act.activation(o_nat[:, p, :, :], bank(BO + p % 2, GH), ACT.Copy).then_inc(r_ocp, 1)
            act.wait_ge(r_ocp, NT)
            act.activation(o_sq, o_nat, ACT.Square).then_inc(f_act, 1)
            serve("out", 0)
            act.wait_ge(late_stored[1][0], 16 * 6)
            act.wait_ge(late_stored[1][1], 16 * 6)
            fetch("q", 0)
            act.wait_ge(f_dve, 1)
            fetch("v", 8)
            act.activation(o_red[:, :], o_red[:, :], ACT.Ln, bias=EPS, scale=1.0 / P).then_inc(f_act, 1)
            act.wait_ge(f_act, 3)
            act.activation(o_red[:, :], o_red[:, :], ACT.Exp, scale=-0.5).then_inc(f_act, 1)
            serve("out", 1)
            for h in range(GH):
                act.wait_ge(f_dve, 3 + h)
                act.activation(oa_hi[:, h, :], oa[:, h % 2, :], ACT.Copy).then_inc(oa_h, 1)
                if h == 1:
                    serve("out", 2)
            fetch("k", 4)
            act.wait_ge(rel_stored, 16)
            act.wait_ge(oa_l, GH)
            act.dma_start(rel[:, :, :], diagonals(rel_dram)).then_inc(rel_loaded, 16)
            serve("out", 3)
            for v in range(4):
                serve("turn", v)
                act.wait_ge(turned[1], v + 1)
                act.activation(v2_nat[:, :, v * P:(v + 1) * P], bank(BO + v % 2, NT), ACT.Copy)\
                    .then_inc(v_copied[1], 1)
            attention(att2, serve)
            serve()
            merge("mix2", 1, sg2, mt2, mix2_hi)
            residual("out2", 3)
            norm(3)
            ffn("up2", 1, 8)
            residual("down2", 4)
            norm(4)

        @block.vector
        def _(dve):
            def sub(out_, a, b):
                return dve.tensor_tensor(out_, a, b, ALU.subtract)

            def gained(n, m, j, first):
                if n < 4:
                    dve.wait_ge(hh_done, m + (DK * n + 1))
                    dve.scalar_tensor_tensor(h_lo[:, m, :], X[:, m, :], gains[:, m + DK * n, :], h_hi[:, m, :],
                                             ALU.mult, ALU.subtract).then_inc(hl_done, 1)
                dve.wait_ge(sq_done, m + (DK * n + 1))
                if first:
                    dve.tensor_copy(sq_sum[:, :], sq_ring[:, j, :]).then_inc(sum_done, 1)
                else:
                    dve.wait_ge(sum_done, m + DK * n)
                    dve.tensor_tensor(sq_sum[:, :], sq_sum[:, :], sq_ring[:, j, :], ALU.add).then_inc(sum_done, 1)

            def scaled(dst, src):
                return dve.tensor_tensor(dst, src, rms_inv[:, :], ALU.mult)

            def late(name, b, plan, total, stage):
                state = [0]

                def serve(*at):
                    upto = (plan[at][0] if at else total) // PIECES
                    while state[0] < upto:
                        n = state[0]
                        dve.wait_ge(chunk_done, chunk(name, n // 2, n % 2).count(1))
                        wait(dve, late_stored[b][n % 2], 16 * (n // 2))
                        scaled(stage[:, n % 2, :], bank(ACC + (n + LATE_BANK[b]) % 2)).then_inc(filled[b], 1)
                        state[0] += 1
                return serve

            def residual(name, n):
                per = INFO[name][1]
                for i, j in units(dve, DK):
                    m = lin(j, 2, i)
                    dve.wait_ge(chunk_done, chunk(name, i, j, per - 1).count(1))
                    dve.tensor_tensor(X[:, m, :], X[:, m, :], bank(ACC + j), ALU.add).then_inc(x_done, 1)
                    gained(n, m, j, isinstance(i, int) and m == 0)

            def copy_tiles(name, dst):
                for i, j in units(dve, INFO[name][0]):
                    dve.wait_ge(chunk_done, chunk(name, i, j).count(1))
                    scaled(dst[:, lin(j, 2, i), :], bank(ACC + j)).then_inc(copied[name], 1)

            def merge(name, b, sg, mt, mix_hi, mix_lo):
                for i, j in units(dve, DK):
                    m = lin(j, 2, i)
                    dve.wait_ge(gate_sig[b], lin(j + 1, 2, i))
                    dve.wait_ge(first_half[b], lin(j + 1, 2, i))
                    wait(dve, mixed[b], m)
                    dve.tensor_tensor(mt[:, 0, :], bank(BS), sg[:, j, 0, :], ALU.mult).then_inc(y_pool_done[b], 1)
                    dve.wait_ge(chunk_done, chunk(name, i, j).count(1))
                    dve.tensor_tensor(mt[:, 1, :], bank(BS + 1), sg[:, j, 1, :], ALU.mult).then_inc(y_nsa_done[b], 1)
                    dve.wait_ge(y_pool_done[b], lin(j + 1, 2, i))
                    dve.wait_ge(y_nsa_done[b], lin(j + 1, 2, i))
                    wait(dve, mix_hl[b], m)
                    dve.tensor_tensor(mt[:, 2, :], mt[:, 0, :], mt[:, 1, :], ALU.add).then_inc(mixed[b], 1)
                    dve.wait_ge(mix_hh[b], lin(j + 1, 2, i))
                    sub(mix_lo[:, m, :], mt[:, 2, :], mix_hi[:, m, :]).then_inc(mix_hl[b], 1)

            def ffn(name, b, steps):
                prm = param("conv1" if b == 0 else "conv2").rearrange("p (f w) -> p f w", w=4)

                def conv(dst, src, raw, f, done, i, j):
                    def w(k):
                        return prm[:, f, k:k + 1]
                    wait(dve, conv_done[b], lin(done + 4 - steps, 2 * steps, i))
                    scaled(raw, src).then_inc(conv_done[b], 1)
                    dve.wait_ge(conv_done[b], lin(done + 1, 2 * steps, i))
                    wait(dve, act_hl[b], lin(j - 1, 2, i))
                    dve.tensor_scalar(dst, raw, w(2), w(3), ALU.mult, ALU.add).then_inc(conv_done[b], 1)
                    dve.wait_ge(conv_done[b], lin(done + 2, 2 * steps, i))
                    dve.scalar_tensor_tensor(dst[:, 1:], raw[:, 0:T - 1], w(1), dst[:, 1:], ALU.mult, ALU.add)\
                        .then_inc(conv_done[b], 1)
                    dve.wait_ge(conv_done[b], lin(done + 3, 2 * steps, i))
                    dve.scalar_tensor_tensor(dst[:, 2:], raw[:, 0:T - 2], w(0), dst[:, 2:], ALU.mult, ALU.add)\
                        .then_inc(conv_done[b], 1)

                for i, j in units(dve, FK):
                    f = lin(j, 2, i)
                    val = t_val[:, j, :]
                    dve.wait_ge(chunk_done, chunk(name, i, j, 0).count(1))
                    conv(t_gate[:, j, :], bank(ACC), t_raw[:, 0, :], f, steps * j, i, j)
                    dve.wait_ge(chunk_done, chunk(name, i, j, 1).count(1))
                    if b == 0:
                        wait(dve, gated[b], lin(j - 1, 2, i))
                        scaled(val, bank(ACC + 1)).then_inc(conv_done[b], 1)
                    else:
                        conv(val, bank(ACC + 1), t_raw[:, 1, :], lin(FK + j, 2, i), steps * j + 4, i, j)
                    dve.wait_ge(conv_done[b], lin(steps * j + steps, 2 * steps, i))
                    dve.wait_ge(silu_done[b], lin(j + 1, 2, i))
                    dve.tensor_tensor(t_gate[:, j, :], t_gate[:, j, :], val, ALU.mult).then_inc(gated[b], 1)
                    dve.wait_ge(act_hh[b], lin(j + 1, 2, i))
                    sub(act_lo[:, f, :], t_gate[:, j, :], act_hi[:, f, :]).then_inc(act_hl[b], 1)

            def attention(a, mask, serve):
                n = len(a.units)
                for s in range(n + 5):
                    if s < n:
                        w = (a.units[s][1] + 1) * P
                        dve.wait_ge(a.scored, s + 1)
                        wait(dve, a.exped, s - 1)
                        col = slice(s % 4, s % 4 + 1)
                        dve.tensor_tensor_reduce(a.sm[:, s % 2, 0:w], banks[:, BS + s % 2, 0:w],
                                                 mask(a.units[s], w), 1.0, NEG, ALU.add, ALU.max,
                                                 a.nbias[:, col]).then_inc(a.masked, 1)
                        dve.wait_ge(a.masked, s + 1)
                        dve.tensor_scalar(a.nbias[:, col], a.nbias[:, col], -DH ** -0.5, None, ALU.mult)\
                            .then_inc(a.shifted, 1)
                    u = s - 1
                    if 0 <= u < n:
                        col = slice(u % 4, u % 4 + 1)
                        dve.wait_ge(a.exped, u + 1)
                        wait(dve, a.weighted, u - 3)
                        dve.reciprocal(a.inv[:, col], a.sums[:, col]).then_inc(a.inverted, 1)
                    u = s - 4
                    if 0 <= u < n and u % a.per_tile == a.per_tile - 1:
                        j = u // a.per_tile
                        dve.wait_ge(a.high, j + 1)
                        sub(a.o_lo[:, j, :], bank(BO + j % 2), a.o_hi[:, j, :]).then_inc(a.low, 1)
                    if s < n:
                        serve("unit", s)
                serve()

            step = [0]

            def start(ins):
                step[0] += 1
                ins.then_inc(start_step, 1)
                dve.wait_ge(start_step, step[0])

            dve.wait_ge(params_in, 16)
            for m in range(DK):
                gained(0, m, m % 2, m == 0)
            TURN = (6.28125, 0.0019350051879882812, 3.019915981956753e-07)
            MAGIC = 12582912.0
            ang, turns, tmp = angle[:, 1, :], angle[:, 0, :], angle[:, 2, :]
            dve.wait_ge(consts_in, 16)
            dve.wait_ge(pos_in, 16)
            start(dve.tensor_copy(tmp, pos_i[:, :]))
            start(dve.tensor_scalar(ang, tmp, const("inv"), None, ALU.mult))
            start(dve.tensor_scalar(tmp, ang, 1.0 / (2.0 * np.pi), MAGIC, ALU.mult, ALU.add))
            start(dve.tensor_scalar(turns, tmp, MAGIC, None, ALU.subtract))
            for part in TURN:
                start(dve.scalar_tensor_tensor(ang, turns, -part, ang, ALU.mult, ALU.add))
            start(dve.scalar_tensor_tensor(tmp, ang, -1.0, ang, ALU.mult, ALU.max))
            start(dve.tensor_scalar(tmp, tmp, -1.0, float(np.pi / 2), ALU.mult, ALU.add))
            dve.wait_ge(rel_in, 16)
            start(dve.tensor_scalar(rel_ext[:, 0:256], rel_row[:, 1:257], DH ** 0.5, None, ALU.mult))
            start(dve.tensor_scalar(rel_ext[:, 256:640], rel_row[:, 256:257].to_broadcast([NH, 384]), DH ** 0.5,
                                    None, ALU.mult))
            dve.wait_ge(inv_done, 1)
            copy_tiles("in1", p1)

            tiles = [(t, param("q_gain")) for t in (4, 5, 6, 7)] + [(KS, param("k_gain", 1, 1)),
                                                                   (KW, param("k_gain", 2, 1))]
            dve.wait_ge(sin_done, 2)
            dve.wait_ge(rel_stored, 16)

            def rotate(n):
                x = p1[:, tiles[n][0], :]
                dve.wait_ge(n_gain, n + 1)
                wait(dve, n_sum, n - 1)
                dve.tensor_tensor(nr_c[:, n % 2, :], x, rope[:, 0, :], ALU.mult).then_inc(n_cos, 1)
                dve.wait_ge(n_rot, n + 1)
                dve.tensor_tensor(nr_s[:, n % 2, :], bank(BT + n % 2), rope[:, 1, :], ALU.mult).then_inc(n_sin, 1)
                dve.wait_ge(n_cos, n + 1)
                dve.wait_ge(n_sin, n + 1)
                dve.tensor_tensor(x, nr_c[:, n % 2, :], nr_s[:, n % 2, :], ALU.add).then_inc(n_sum, 1)

            serve = late("fill1", 0, FILL1, FILLED1, stage1)
            for n, (t, gain) in enumerate(tiles):
                dve.wait_ge(n_inv, n + 1)
                dve.scalar_tensor_tensor(p1[:, t, :], p1[:, t, :], gain, nr_r[:, n % 2, :], ALU.mult, ALU.mult)\
                    .then_inc(n_gain, 1)
                if n:
                    rotate(n - 1)
                serve("norm", n)
            rotate(5)
            serve("turn", 0)
            dve.wait_ge(blk_zero, 1)
            pe_ = param("pe").rearrange("p (c l) -> p c l", c=2)
            for c in range(2):
                for g in range(2):
                    src = p1[rows(g), KC + c, :].rearrange("p (a b) -> p b a", b=16)
                    for l2 in range(2):
                        dve.tensor_tensor(cmp_blk[rows(g), c, 16 * l2:16 * l2 + 16, g, :], src[:, :, l2:l2 + NCMP],
                                          pe_[rows(g), c, 16 * l2:16 * l2 + 16].unsqueeze(2).to_broadcast(
                                              [DH, 16, NCMP]), ALU.add).then_inc(blk_done, 1)
            for n in (1, 2):
                serve("turn", n)
            for n in range(3):
                serve("compress", n)
            dve.wait_ge(c_act, 8)
            dve.scalar_tensor_tensor(kc_t[:, :], banks[:, BO, 0:NCMP], param("k_gain", 0, 1), kc_tmp[:, 1, :],
                                     ALU.mult, ALU.mult).then_inc(c_dve, 1)
            dve.wait_ge(c_dve, 1)
            dve.tensor_tensor(kc_tmp[:, 2, :], kc_t[:, :], rope[:, 0, 31:T:16], ALU.mult).then_inc(c_dve, 1)
            serve("compress", 3)
            dve.wait_ge(c_pe, 8)
            dve.tensor_tensor(kc_tmp[:, 3, :], banks[:, BT, 0:NCMP], rope[:, 1, 31:T:16], ALU.mult)\
                .then_inc(c_dve, 1)
            dve.wait_ge(c_dve, 3)
            dve.tensor_tensor(kc_t[:, :], kc_tmp[:, 2, :], kc_tmp[:, 3, :], ALU.add).then_inc(c_dve, 1)
            for gi in range(4):
                dve.wait_ge(yp_h, gi + 1)
                dve.scalar_tensor_tensor(yp_lo[:, gi, :], bank(POOLED[gi % 2]), param("pool_scale", gi, 1),
                                         yp_hi[:, gi, :], ALU.mult, ALU.subtract).then_inc(yp_l, 1)
            serve("compress", 4)
            flat = cmp_s[:, :, :, :, :].rearrange("p a b c n -> p (a b c) n")
            wide = [P, 32, NCMP]
            for half in range(2):
                dve.wait_ge(s_pe, half + 1)
                dve.tensor_tensor(cmp_s[:, half, :, :, :],
                                  banks[:, BS + half, 0:16 * NCMP].rearrange("p (a b n) -> p a b n", a=4, b=4),
                                  const("cmp", NT, NCMP).unsqueeze(2).to_broadcast([P, NT, 4, NCMP]), ALU.add)\
                    .then_inc(s_dve, 1)
            dve.wait_ge(s_dve, 2)
            dve.tensor_reduce(cmp_red[:, 0, :], flat, AXX, ALU.max).then_inc(s_dve, 1)
            dve.wait_ge(s_dve, 3)
            sub(flat, flat, cmp_red[:, 0, :].unsqueeze(2).to_broadcast(wide)).then_inc(s_dve, 1)
            serve("scores", 0)
            dve.wait_ge(s_act, 1)
            dve.tensor_reduce(cmp_red[:, 1, :], flat, AXX, ALU.add).then_inc(s_dve, 1)
            serve("scores", 1)
            dve.wait_ge(s_dve, 5)
            dve.reciprocal(cmp_red[:, 2, :], cmp_red[:, 1, :]).then_inc(s_dve, 1)
            dve.wait_ge(v_copied[0], 3)
            dve.wait_ge(s_dve, 6)
            fac = cmp_red[:, 2, :].rearrange("p (h a b) -> p h a b", h=2, a=NT)
            gts = gate_t[:, :, :].rearrange("p a (h n) -> p a h n", n=3)
            for half in range(2):
                dve.tensor_tensor(fac[:, half, :, :], fac[:, half, :, :], gts[:, :, 4 * half:4 * half + 4, 0],
                                  ALU.mult).then_inc(s_dve, 1)
            dve.wait_ge(s_dve, 8)
            dve.tensor_scalar(fac[:, :, 0, :], fac[:, :, 0, :], const("cmp_any"), None, ALU.mult).then_inc(s_dve, 1)
            dve.wait_ge(s_dve, 9)
            dve.tensor_tensor(flat, flat, cmp_red[:, 2, :].unsqueeze(2).to_broadcast(wide), ALU.mult)\
                .then_inc(s_dve, 1)
            attention(att1, lambda u, w: const("causal")[:, T - w:T], serve)
            merge("mix1", 0, sg1, mt1, mix1_hi, mix1_lo)
            residual("out1", 1)
            dve.wait_ge(inv_done, 2)
            ffn("up1", 0, 5)
            residual("down1", 2)

            dve.wait_ge(inv_done, 3)
            taps = param("conv_qkv").rearrange("p (f w) -> p f w", w=4)
            for i, j in units(dve, 12):
                t = lin(j, 2, i)
                src, raw, dst = bank(ACC + j), cv_raw[:, j, :], cv[:, j, :]
                dve.wait_ge(chunk_done, chunk("in2c", i, j).count(1))
                wait(dve, cv_done, lin(5 * j - 5, 10, i))
                scaled(raw, src).then_inc(cv_done, 1)
                dve.wait_ge(cv_done, lin(5 * j + 1, 10, i))
                wait(dve, cv_silu, lin(j - 1, 2, i))
                dve.tensor_scalar(dst, raw, taps[:, t, 3:4], None, ALU.mult).then_inc(cv_done, 1)
                for k in range(1, 4):
                    dve.wait_ge(cv_done, lin(5 * j + k + 1, 10, i))
                    dve.scalar_tensor_tensor(dst[:, k:], raw[:, 0:T - k], taps[:, t, 3 - k:4 - k], dst[:, k:],
                                             ALU.mult, ALU.add).then_inc(cv_done, 1)
            copy_tiles("in2z", p2a[:, 12:17, :])
            g = slice(32, 32 + GH)
            col = {n: params[g, PARAM[n][0]:PARAM[n][0] + 1] for n in ("a_log", "dt_bias")}
            dve.wait_ge(copied["in2z"], 5)
            dve.tensor_scalar(gz[g, :], p2a[g, 16, :], col["dt_bias"], None, ALU.add).then_inc(g_dve, 1)
            dve.wait_ge(g_dve, 1)
            dve.scalar_tensor_tensor(gz2[g, :], gz[g, :], -1.0, gz[g, :], ALU.mult, ALU.max).then_inc(g_dve, 1)
            serve = late("fill2", 1, FILL2, FILLED2, stage2)
            for n in range(8):
                dve.wait_ge(l_inv, n + 1)
                dve.scalar_tensor_tensor(p2a[:, n, :], p2a[:, n, :], float(P) ** -0.5 if n < GH else 1.0,
                                         l2_r[:, n % 2, :], ALU.mult, ALU.mult).then_inc(l_out, 1)
                serve("norm", n)
            dve.wait_ge(g_act, 3)
            dve.scalar_tensor_tensor(gz[g, :], gz[g, :], 0.0, gz2[g, :], ALU.max, ALU.add).then_inc(g_dve, 1)
            dve.tensor_scalar(ea[g, 1:2], ea[g, 0:1], -1.0, None, ALU.mult).then_inc(g_dve, 1)
            dve.wait_ge(g_dve, 4)
            dve.tensor_scalar(gz2[g, :], gz[g, :], ea[g, 1:2], None, ALU.mult).then_inc(g_dve, 1)
            dve.wait_ge(g_dve, 5)
            dve.wait_ge(blk_zero, 2)
            dve.tensor_tensor_scan(gb_rows[g, :], const("reset")[g, :], gz2[g, :], 0.0, ALU.mult, ALU.add)\
                .then_inc(g_dve, 1)
            serve("gates", 0)
            dve.wait_ge(g_act, 6)
            dve.tensor_scalar(gd_neg[:, :, :], gd_cols[:, :, 32:32 + GH], -1.0, None, ALU.mult).then_inc(g_dve, 1)
            dve.tensor_tensor(gd_bg[:, :, :], gd_bg[:, :, :], gd_cols[:, :, 0:GH], ALU.mult).then_inc(g_dve, 1)
            serve("gates", 1)
            dve.wait_ge(g_dve, 8)
            sq3 = [P, NT, P]

            def every(mask):
                return mask.unsqueeze(1).to_broadcast(sq3)

            def per_token(c_):
                return c_.unsqueeze(2).to_broadcast(sq3)

            dve.wait_ge(l_out, 8)
            for h in range(GH):
                b = 11 * h
                dve.wait_ge(d_pe, 6 * h + 1)
                dve.wait_ge(d_act, 7 * h + 1)
                wait(dve, d_dve, b)
                dve.tensor_tensor(dec[:, :, :], bank(BS, NT), every(const("decay")), ALU.add).then_inc(d_dve, 1)
                for half in range(2):
                    e = CH - 1 if half == 0 else P - 1
                    sub(gd_kd[rows(half), h, :], banks[rows(half), BS, e:T:P],
                        gd_cols[rows(half), :, 32 + h]).then_inc(d_dve, 1)
                dve.wait_ge(d_pe, 6 * h + 2)
                dve.tensor_tensor(beta_strict[:, :, :], bank(BS + 1, NT), every(const("strict")), ALU.mult)\
                    .then_inc(d_dve, 1)
                serve("rows", h)
                dve.wait_ge(d_pe, 6 * h + 4)
                dve.wait_ge(d_act, 7 * h + 1)
                dve.tensor_tensor(p2a[:, h, :], p2a[:, h, :], gam_row[:, :], ALU.mult).then_inc(d_dve, 1)
                dve.wait_ge(d_act, 7 * h + 5)
                dve.tensor_tensor(p_t[:, h, :, :], bank(BT + 1, NT), dec[:, :, :], ALU.mult).then_inc(d_dve, 1)
                dve.wait_ge(d_dve, b + 6)
                dve.tensor_tensor(dec[:, :, :], bank(BT, NT), dec[:, :, :], ALU.mult).then_inc(d_dve, 1)
                dve.wait_ge(d_dve, b + 7)
                dve.tensor_tensor(a_t[:, h, :, :], dec[:, :, :], beta_strict[:, :, :], ALU.mult).then_inc(d_dve, 1)
                dve.wait_ge(d_pe, 6 * h + 5)
                dve.tensor_tensor(k_bg[:, h, :, :], bank(BO, NT), per_token(gd_bg[:, :, h]), ALU.mult)\
                    .then_inc(d_dve, 1)
                dve.wait_ge(d_act, 7 * h + 6)
                dve.tensor_tensor(k_dec[:, h, :, :], bank(BO, NT), per_token(gd_kd[:, h, :]), ALU.mult)\
                    .then_inc(d_dve, 1)
                dve.wait_ge(d_pe, 6 * h + 6)
                dve.tensor_tensor(v_b[:, h, :, :], bank(BO + 1, NT), per_token(gd_cols[:, :, h]), ALU.mult)\
                    .then_inc(d_dve, 1)
            serve("ready", 0)
            dve.wait_ge(d_dve, 11 * GH)
            for h in range(GH):
                dve.wait_ge(i_mask, h + 1)
                sub(y_inv[:, h, :, :], every(ident), b_t[:, (h + 2) % GH, :, :]).then_inc(i_y, 1)
                dve.wait_ge(i_bx, h + 1)
                sub(x_inv[:, h, :, :], every(ident), bank(BT + h % 2, NT)).then_inc(i_x, 1)
                serve("first", h)

            def update(k):
                h = k % GH
                if k < WITH_X:
                    dve.wait_ge(i_pe, corrected(k) - 1)
                    sub(x_inv[:, h, :, :], x_inv[:, h, :, :], bank(BS + k % 2, NT)).then_inc(i_x, 1)
                dve.wait_ge(i_pe, corrected(k))
                sub(y_inv[:, h, :, :], y_inv[:, h, :, :], bank(BO + k % 2, NT)).then_inc(i_y, 1)

            for k in range(5 * GH):
                serve("level", k)
                update(k)
            for c in range(NCH):
                p, half, slot = c // 2, c % 2, c // 2 % 2
                rs = rows(half)
                if c == 0:
                    dve.wait_ge(r_cp, 2 * GH)
                    dve.tensor_copy(u_new[rs, slot, :, :], uv[rs, :, p, :]).then_inc(r_u, 1)
                else:
                    dve.wait_ge(r_ws, c)
                    sub(u_new[rs, slot, :, :], uv[rs, :, p, :], bank(BS + c % 2, GH)[rs]).then_inc(r_u, 1)
                if c == NCH - 1:
                    serve("chunk", c)
                    break
                dve.wait_ge(r_ds, c + 1)
                wait(dve, r_o, c)
                wait(dve, r_s, GH * c)
                for h in range(GH):
                    new = bank(BT + c % 2, GH)[:, h, :]
                    if c == 0:
                        dve.tensor_copy(state[:, 0, h, :], new).then_inc(r_s, 1)
                    else:
                        dve.scalar_tensor_tensor(state[:, c % 2, h, :], state[:, (c - 1) % 2, h, :],
                                                 gd_last[:, h, c:c + 1], new, ALU.mult, ALU.add).then_inc(r_s, 1)
                serve("chunk", c)
            dve.wait_ge(f_act, 2)
            dve.tensor_reduce(o_red[:, :], o_sq.rearrange("p c h d -> p (c h) d"), AXX, ALU.add).then_inc(f_dve, 1)
            dve.wait_ge(f_act, 4)
            on = o_nat.rearrange("p c h d -> p (c h) d")
            dve.tensor_tensor(on, on, o_red[:, :].unsqueeze(2).to_broadcast([P, NT * GH, P]), ALU.mult)\
                .then_inc(f_dve, 1)
            serve("out", 0)
            serve("out", 1)
            for h in range(GH):
                dve.wait_ge(f_pe, h + 1)
                wait(dve, oa_l, h - 1)
                dve.scalar_tensor_tensor(oa[:, h % 2, :], bank(BT + h % 2), param("gdn_gain"), p2a[:, 12 + h, :],
                                         ALU.mult, ALU.mult).then_inc(f_dve, 1)
                dve.wait_ge(oa_h, h + 1)
                sub(oa_lo[:, h, :], oa[:, h % 2, :], oa_hi[:, h, :]).then_inc(oa_l, 1)
                if h == 1:
                    serve("out", 2)
            serve("out", 3)
            for v in range(4):
                serve("turn", v)
            dve.wait_ge(blk_zero, 3)
            attention(att2, lambda u, w: rel[:, 2 * u[0] + u[3], w - 1::-1], serve)
            merge("mix2", 1, sg2, mt2, mix2_hi, mix2_lo)
            residual("out2", 3)
            dve.wait_ge(inv_done, 4)
            ffn("up2", 1, 8)
            residual("down2", 4)
            dve.wait_ge(inv_done, 5)
            for m in range(DK):
                dve.scalar_tensor_tensor(y_out[:, m, :], X[:, m, :], gains[:, 4 * DK + m, :], rms_inv[:, :],
                                         ALU.mult, ALU.mult).then_inc(y_done, 1)

        @block.tensor
        def _(pe):
            def product(c, dst, hi, lo, ks, first, last, done, ready=None):
                for n, (ks_, kr) in enumerate(ks):
                    w_h = w_hi[:, c.slot, ks_ * P:(ks_ + 1) * P]
                    w_l = w_lo[:, c.slot, ks_ * P:(ks_ + 1) * P]
                    if ready:
                        pe.wait_ge(ready[0], ready[1] + kr + 1)
                    pe.matmul(dst, w_h, hi[:, kr, :], start=first and n == 0, stop=False)
                    pe.matmul(dst, w_h, lo[:, kr, :], start=False, stop=False)
                    mm = pe.matmul(dst, w_l, hi[:, kr, :], start=False, stop=last and n == len(ks) - 1)
                if done:
                    mm.then_inc(done, 1)

            def late(name, b, plan, total, before):
                state = [0]

                def fill(*at):
                    upto = plan[at][1] if at else total
                    while state[0] < upto:
                        n, r = state[0] // PIECES, state[0] % PIECES
                        c = chunk(name, n // 2, n % 2)
                        if r == 0:
                            pe.wait_ge(lo_ready, c.count(1))
                            if n < 2:
                                pe.wait_ge(before[0], before[1] - 1 + n)
                            wait(pe, filled[b], n - 1)
                        ks = [(k, k) for k in range(2 * r, 2 * r + 2)]
                        product(c, bank(ACC + (n + LATE_BANK[b]) % 2), h_hi, h_lo, ks, r == 0, r == PIECES - 1,
                                chunk_done if r == PIECES - 1 else None)
                        state[0] += 1
                return fill

            def whole(n, off=0):
                return [(k, off + k) for k in range(n)]

            def norm(n):
                if n == 0:
                    pe.wait_ge(consts_in, 16)
                pe.wait_ge(sum_done, DK * (n + 1))
                pe.matmul(bank(BS), ones, sq_sum[:, :], start=True, stop=True).then_inc(mean_done, 1)

            def linear(name, n, used, per=1, mean=True):
                for i, j in units(pe, INFO[name][0]):
                    c = chunk(name, i, j)
                    pe.wait_ge(lo_ready, c.count(1))
                    wait(pe, used, lin(per * (j - 2) + 1, 2 * per, i))
                    first = isinstance(i, int) and i == 0 and j == 0
                    if first and mean and n:
                        pe.wait_ge(x_done, DK * n - 1)
                    product(c, bank(ACC + j), h_hi, h_lo, whole(DK), True, True, chunk_done,
                            (hl_done, DK * n) if first and mean else None)
                    if first and mean:
                        norm(n)

            def residual(name, n, hi, lo, split_):
                nchunk, kt = INFO[name][1], INFO[name][2]
                for i, j in units(pe, DK):
                    wait(pe, x_done, lin(DK * (n - 1) + j - 1, 2, i) if not (isinstance(i, int) and i == 0) else 0)
                    for q in range(nchunk):
                        c = chunk(name, i, j, q)
                        pe.wait_ge(lo_ready, c.count(1))
                        first = isinstance(i, int) and i == 0 and j == 0
                        product(c, bank(ACC + j), hi, lo, whole(kt, kt * q), q == 0, q == nchunk - 1, chunk_done,
                                (split_, 0) if first else None)

            def merge(name, b, y1, y2, nlate):
                for i, j in units(pe, DK):
                    m = lin(j, 2, i)
                    c = chunk(name, i, j)
                    pe.wait_ge(lo_ready, c.count(1))
                    wait(pe, y_pool_done[b], m)
                    product(c, bank(BS), *y1, [(k, k) for k in range(4)], True, True, first_half[b])
                    wait(pe, y_nsa_done[b], m)
                    product(c, bank(BS + 1), *y2, [(4 + k, k) for k in range(4)], True, True, chunk_done)
                pe.wait_ge(filled[b], nlate)

            def ffn(name, b, n, steps):
                for i, j in units(pe, FK):
                    first = isinstance(i, int) and i == 0 and j == 0
                    for q in range(2):
                        c = chunk(name, i, j, q)
                        pe.wait_ge(lo_ready, c.count(1))
                        if q == 0 and not first:
                            pe.wait_ge(conv_done[b], lin(steps * (j - 1) + 1, 2 * steps, i))
                        elif q == 0:
                            pe.wait_ge(x_done, DK * n - 1)
                        else:
                            wait(pe, conv_done[b], lin(steps * (j - 1) + 5, 2 * steps, i))
                        product(c, bank(ACC + q), h_hi, h_lo, whole(DK), True, True, chunk_done,
                                (hl_done, DK * n) if first and q == 0 else None)
                        if first and q == 0:
                            norm(n)
                pe.wait_ge(conv_done[b], steps * (FK - 1) + 5)

            def turn(dst, src, n=P, last=None):
                return pe.transpose(dst, src, ident[0:n, 0:n])

            def attention(a, q_tile, k_tile, v_tile, first_values=None, fill=None):
                n = len(a.units)
                for s in range(n + 3):
                    if s < n:
                        j, i, b, half = a.units[s]
                        wait(pe, a.masked, s - 1)
                        pe.matmul(banks[:, BS + half, 0:(i + 1) * P], q_tile(j)[rows(half), i * P:(i + 1) * P],
                                  k_tile(j, b)[rows(half), 0:(i + 1) * P], start=True, stop=True)\
                            .then_inc(a.scored, 1)
                        if fill:
                            fill("unit", s)
                    u = s - 2
                    if 0 <= u < n:
                        j, i, b, half = a.units[u]
                        pe.wait_ge(a.weighted, u + 1)
                        wait(pe, a.fetched, u - 1)
                        for k in range(i + 1):
                            mm = turn(banks[:, BT + u % 2, k * P:(k + 1) * P], a.p[:, u % 3, k * P:(k + 1) * P])
                        mm.then_inc(a.flipped, 1)
                    u = s - 3
                    if 0 <= u < n:
                        j, i, b, half = a.units[u]
                        pe.wait_ge(a.fetched, u + 1)
                        if u % a.per_tile == 0:
                            wait(pe, a.low, j - 1)
                        dst = banks[rows(half), BO + j % 2, i * P:(i + 1) * P]
                        begin = b == 0
                        if begin and first_values:
                            pe.matmul(dst, *first_values(j, i, half), start=True, stop=False)
                            begin = False
                        end = b == max(x[2] for x in a.units)
                        for k in range(i + 1):
                            mm = pe.matmul(dst, v_tile(j, b, half, k), a.pt[:, u % 2, k * P:(k + 1) * P],
                                           start=begin and k == 0, stop=end and k == i)
                        mm.then_inc(a.summed, 1)

            linear("in1", 0, copied["in1"])

            tiles = (4, 5, 6, 7, KS, KW)

            def rotate(n):
                pe.wait_ge(n_gain, n + 1)
                wait(pe, n_sin, n - 1)
                pe.matmul(bank(BT + n % 2), const("rot"), p1[:, tiles[n], :], start=True, stop=True)\
                    .then_inc(n_rot, 1)

            fill = late("fill1", 0, FILL1, FILLED1, (copied["in1"], 15))
            fill("start", 0)
            pe.wait_ge(copied["in1"], 15)
            for n in range(6):
                pe.wait_ge(n_sq, n + 1)
                wait(pe, n_ln, n - 1)
                pe.matmul(bank(BS + n % 2), halves, nr_sq[:, n % 2, :], start=True, stop=True).then_inc(n_ms, 1)
                if n:
                    rotate(n - 1)
                fill("norm", n)
            rotate(5)
            for v in range(2):
                for k in range(NT):
                    mm = turn(banks[:, BO + v, k * P:(k + 1) * P], p1[:, VS + v, k * P:(k + 1) * P])
                mm.then_inc(turned[0], 1)
                fill("turn", v)
            pe.wait_ge(gates_ready, 1)
            pe.wait_ge(n_sin, 5)
            for k in range(NT):
                mm = turn(banks[:, BT, 24 * k:24 * k + 24], p1[0:24, GT, k * P:(k + 1) * P], 24)
            mm.then_inc(turned[0], 1)
            fill("turn", 2)
            pe.wait_ge(blk_done, 8)
            pe.wait_ge(cmp_in, 16 * (2 + CMP_PIECES))
            pe.wait_ge(n_ln, 6)
            pe.wait_ge(n_sin, 6)
            for c in range(2):
                for l in range(32):
                    mm = pe.matmul(banks[0:2 * NCMP, BS + c, 0:P],
                                   cmp_blk[:, c, l, :, :].rearrange("p a b -> p (a b)"),
                                   cmp_w1[:, c, l * P:(l + 1) * P], start=l == 0, stop=l == 31)
                mm.then_inc(c_pe, 1)
            fill("compress", 0)
            pe.wait_ge(v_copied[0], 3)
            for c in range(2):
                pe.wait_ge(c_act, c + 1)
                turn(banks[:, BT + c, 0:2 * NCMP], hid[:, c, :], 2 * NCMP).then_inc(c_pe, 1)
            fill("compress", 1)
            pe.wait_ge(c_act, 3)
            for g in range(2):
                mm = pe.matmul(banks[rows(g), BO, 0:NCMP], cmp_w2[:, 0, :], hid_t[:, 0, g * NCMP:(g + 1) * NCMP],
                               start=True, stop=True)
            mm.then_inc(c_pe, 1)
            pe.wait_ge(c_act, 4)
            for g in range(2):
                mm = pe.matmul(banks[0:NCMP, BO + 1, g * DH:(g + 1) * DH], hid_t[:, 1, g * NCMP:(g + 1) * NCMP],
                               cmp_w2[:, 1, :], start=True, stop=True)
            mm.then_inc(c_pe, 1)
            fill("compress", 2)
            pe.wait_ge(c_act, 5)
            pe.matmul(banks[:, BS, 0:NCMP], halves, kc_tmp[:, 0, :], start=True, stop=True).then_inc(c_pe, 1)
            for gi in range(2):
                pe.wait_ge(pooled, sum(1 + g_ + 1 + 3 for g_ in range(gi + 1)))
                pe.matmul(bank(POOLED[gi % 2]), pool_w[:, gi, :], p1[:, gi, :], start=True, stop=True)\
                    .then_inc(pool_mul, 1)
            fill("compress", 3)
            pe.wait_ge(c_dve, 1)
            pe.matmul(banks[:, BT, 0:NCMP], const("rot"), kc_t[:, :], start=True, stop=True).then_inc(c_pe, 1)
            for gi in range(2, 4):
                pe.wait_ge(pooled, sum(1 + g_ + 1 + 3 for g_ in range(gi + 1)))
                pe.wait_ge(yp_l, gi - 1)
                pe.matmul(bank(POOLED[gi % 2]), pool_w[:, gi, :], p1[:, gi, :], start=True, stop=True)\
                    .then_inc(pool_mul, 1)
            fill("compress", 4)
            pe.wait_ge(c_dve, 4)
            pe.wait_ge(n_sum, 6)
            pe.wait_ge(yp_l, 3)
            for half in range(2):
                for i in range(NT):
                    for j in range(4):
                        at_ = (4 * i + j) * NCMP
                        mm = pe.matmul(banks[:, BS + half, at_:at_ + NCMP],
                                       p1[rows(half), 4 + j, i * P:(i + 1) * P], kc_t[rows(half), :],
                                       start=True, stop=True)
                mm.then_inc(s_pe, 1)
            fill("scores", 0)
            fill("scores", 1)
            pe.wait_ge(s_dve, 10)
            pe.wait_ge(yp_l, 4)
            for r in range(8):
                wait(pe, s_act, r)
                for k in range(4):
                    half, i, j = r // 4, r % 4, k
                    mm = turn(banks[0:NCMP, BT + r % 2, k * P:(k + 1) * P], cmp_s[:, half, i, j, :])
                mm.then_inc(s_pe, 1)
            pe.wait_ge(s_act, 9)
            attention(att1, lambda j: p1[:, 4 + j, :], lambda j, b: p1[:, KS + b, :],
                      lambda j, b, half, k: v1_nat[:, b, k, rows(half)],
                      lambda j, i, half: (vc_nat[:, half, :], pc_t[:, 16 * half + 4 * i + j, :]), fill)
            pe.wait_ge(yp_l, 4)
            pe.wait_ge(att1.low, 4)
            merge("mix1", 0, (yp_hi, yp_lo), (o1_hi, o1_lo), INFO["fill1"][0])
            residual("out1", 1, mix1_hi, mix1_lo, mix_hl[0])
            ffn("up1", 0, 1, 5)
            residual("down1", 2, act_hi, act_lo, act_hl[0])

            linear("in2c", 2, cv_done, 5)
            pe.wait_ge(cv_done, 5 * 11 + 1)
            linear("in2z", 2, copied["in2z"], mean=False)
            fill = late("fill2", 1, FILL2, FILLED2, (copied["in2z"], 5))
            fill("start", 0)
            for n in range(8):
                pe.wait_ge(l_sq, n + 1)
                wait(pe, l_ln, n - 1)
                pe.matmul(bank(BS + n % 2), ones, l2_sq[:, n % 2, :], start=True, stop=True).then_inc(l_ms, 1)
                fill("norm", n)
            fill("gates", 0)
            pe.wait_ge(g_dve, 6)
            pe.wait_ge(g_act, 4)
            for p in range(NT):
                mm = turn(banks[:, BO, 64 * p:64 * p + 64], gb_rows[:, p * P:(p + 1) * P], 64)
            mm.then_inc(g_pe, 1)
            fill("gates", 1)
            pe.wait_ge(g_act, 5)
            pe.wait_ge(l_out, 8)
            pick = const("pick", 2 * GH, P)
            for h in range(GH):
                q_, k_, v_ = p2a[:, h, :], p2a[:, GH + h, :], p2a[:, 2 * GH + h, :]
                b = 11 * (h - 1)

                def free(n):
                    if h:
                        pe.wait_ge(d_dve, b + n)

                free(3)
                if h:
                    pe.wait_ge(d_act, 7 * (h - 1) + 1)
                pe.matmul(bank(BS), pick[0:64, GH + h, :], gb_rows[:, :], start=True, stop=True).then_inc(d_pe, 1)
                free(4)
                pe.matmul(bank(BS + 1), pick[0:64, h, :], gb_rows[:, :], start=True, stop=True).then_inc(d_pe, 1)
                fill("rows", h)
                for n, (dst, lhs, rhs) in enumerate(((BT, k_, k_), (BT + 1, k_, q_), (BO, k_, None), (BO + 1, v_, None))):
                    free((7, 6, 10, 11)[n])
                    for p in range(NT):
                        cols = slice(p * P, (p + 1) * P)
                        if rhs is None:
                            mm = turn(banks[:, dst, cols], lhs[:, cols])
                        else:
                            mm = pe.matmul(banks[:, dst, cols], lhs[:, cols], rhs[:, cols], start=True, stop=True)
                    mm.then_inc(d_pe, 1)
            fill("ready", 0)
            pe.wait_ge(d_dve, 11 * GH)
            for h in range(GH):
                pe.wait_ge(i_mask, h + 1)
                wait(pe, i_x, h - 1)
                for p in range(NT):
                    mm = turn(banks[:, BT + h % 2, p * P:(p + 1) * P], b_t[:, (h + 2) % GH, p, :])
                mm.then_inc(i_bx, 1)
                fill("first", h)
            pe.wait_ge(i_x, GH)

            def corrections(k):
                h, r = k % GH, k % 2
                pe.wait_ge(i_cp, k + 1)
                if k < WITH_X:
                    wait(pe, i_x, GH + k - 1)
                    for p in range(NT):
                        mm = pe.matmul(banks[:, BS + r, p * P:(p + 1) * P], y_inv[:, h, p, :], bx[:, r, p, :],
                                       start=True, stop=True)
                    mm.then_inc(i_pe, 1)
                wait(pe, i_y, GH + k - 1)
                for p in range(NT):
                    mm = pe.matmul(banks[:, BO + r, p * P:(p + 1) * P], bx[:, r, p, :], y_inv[:, h, p, :],
                                   start=True, stop=True)
                mm.then_inc(i_pe, 1)

            for k in range(5 * GH):
                h, r = k % GH, k % 2
                pe.wait_ge(i_mask, GH + k + 1)
                pe.wait_ge(i_x, k + 1)
                pe.wait_ge(i_y, k + 1)
                wait(pe, i_cp, k - 1)
                for p in range(NT):
                    mm = pe.matmul(banks[:, BT + r, p * P:(p + 1) * P], b_t[:, (h + 2) % GH, p, :], x_inv[:, h, p, :],
                                   start=True, stop=True)
                mm.then_inc(i_bx, 1)
                fill("level", k)
                if k:
                    corrections(k - 1)
            corrections(5 * GH - 1)
            pe.wait_ge(i_y, 6 * GH)
            pe.wait_ge(i_x, 5 * GH)
            for h in range(GH):
                for m, dst in ((0, BT), (1, BO)):
                    wait(pe, r_cp, 2 * (h - 2) + 1 + m)
                    for p in range(NT):
                        lhs, rhs = (k_bg[:, h, p, :], y_inv[:, h, p, :]) if m == 0 else \
                            (y_inv[:, h, p, :], v_b[:, h, p, :])
                        mm = pe.matmul(banks[:, dst + h % 2, p * P:(p + 1) * P], lhs, rhs, start=True, stop=True)
                    mm.then_inc(r_w, 1)
            pe.wait_ge(r_cp, 2 * GH)
            for c in range(NCH):
                p, half, slot = c // 2, c % 2, c // 2 % 2
                rs, tok = rows(half), slice(c * CH, (c + 1) * CH)
                if c:
                    pe.wait_ge(r_s, GH * c)
                    for h in range(GH):
                        w = w_t[:, h, :, :].rearrange("p a b -> p (a b)")
                        mm = pe.matmul(banks[rs, BS + c % 2, h * P:(h + 1) * P], w[:, tok],
                                       state[:, (c - 1) % 2, h, :], start=True, stop=True)
                    mm.then_inc(r_ws, 1)
                fill("chunk", c)
                pe.wait_ge(r_u, c + 1)
                if c < NCH - 1:
                    for h in range(GH):
                        mm = pe.matmul(banks[:, BT + c % 2, h * P:(h + 1) * P], k_dec[rs, h, p, :],
                                       u_new[rs, slot, h, :], start=True, stop=True)
                    mm.then_inc(r_ds, 1)
                if half == 0:
                    wait(pe, r_ocp, p - 1)
                for h in range(GH):
                    dst = banks[rs, BO + p % 2, h * P:(h + 1) * P]
                    if c:
                        pe.matmul(dst, p2a[:, h, tok], state[:, (c - 1) % 2, h, :], start=True, stop=False)
                    mm = pe.matmul(dst, p_t[rs, h, p, rs], u_new[rs, slot, h, :], start=c == 0, stop=True)
                mm.then_inc(r_o, 1)
            fill("out", 0)
            fill("out", 1)
            pe.wait_ge(f_dve, 2)
            for h in range(GH):
                wait(pe, f_dve, h + 1 if h >= 2 else 0)
                for p in range(NT):
                    mm = turn(banks[:, BT + h % 2, p * P:(p + 1) * P], o_nat[:, p, h, :])
                mm.then_inc(f_pe, 1)
            fill("out", 2)
            fill("out", 3)
            for v in range(4):
                fill("turn", v)
                pe.wait_ge(qkv_in["v"], 16)
                wait(pe, v_copied[1], v - 1)
                for k in range(NT):
                    mm = turn(banks[:, BO + v % 2, k * P:(k + 1) * P], p2b[:, 8 + v, k * P:(k + 1) * P])
                mm.then_inc(turned[1], 1)
            pe.wait_ge(v_copied[1], 4)
            pe.wait_ge(qkv_in["q"], 16)
            pe.wait_ge(qkv_in["k"], 16)
            attention(att2, lambda j: p2b[:, j, :], lambda j, b: p2b[:, 4 + j, :],
                      lambda j, b, half, k: v2_nat[:, k, j * P + half * DH:j * P + (half + 1) * DH], fill=fill)
            pe.wait_ge(att2.low, 4)
            pe.wait_ge(oa_l, 4)
            merge("mix2", 1, (oa_hi, oa_lo), (ob_hi, ob_lo), INFO["fill2"][0])
            residual("out2", 3, mix2_hi, mix2_lo, mix_hl[1])
            ffn("up2", 1, 3, 8)
            residual("down2", 4, act_hi, act_lo, act_hl[1])
            norm(4)


def diagonals(rows_dram):
    view = rows_dram[0:NH, 0:T]
    return bass.AP(tensor=view.tensor, offset=view.offset, ap=[[1, P], [640, NH], [1, T]])


def by_tiles(w, columns=None):
    k, m = w.shape
    if columns is None:
        t = w.reshape(k // P, P, m // P, P)
    else:
        t = np.zeros((k, len(columns), P), w.dtype)
        for n, cols in enumerate(columns):
            for at, a, b in cols:
                t[:, n, at:at + b - a] = w[:, a:b]
        t = t.reshape(k // P, P, len(columns), P)
    return np.ascontiguousarray(t.transpose(2, 1, 0, 3)).reshape(t.shape[2], P, -1)


def by_columns(v):
    return v.reshape(-1, P).T


def kernel(**inputs):
    from concourse import bacc
    from concourse.bass_utils import run_bass_kernel_spmd

    a = {k: np.asarray(v) for k, v in inputs.items()}
    a = {k: v[0] if k not in ("norm_final_w_2",) else v for k, v in a.items()}

    def straight(first, n):
        return [[(0, first + P * t, first + P * (t + 1))] for t in range(n)]

    def gate_pairs(first):
        return [[(0, at, at + P)] for m in range(DK) for at in (first + P * m, first + D + P * m)]

    q_pairs = [[(0, 512 + DH * j, 512 + DH * (j + 1)), (DH, 512 + DH * (j + 4), 512 + DH * (j + 5))]
               for j in range(4)]
    kv = 1024
    in1 = straight(0, 4) + q_pairs + straight(kv, 2) + straight(kv + 3 * P, 1) + straight(kv + 5 * P, 1) + \
        straight(kv + 2 * P, 1) + straight(kv + 4 * P, 1) + [[(0, 1792, 1816)]]
    branch = np.concatenate([a["w_pool_out"]] + [a["w_nsa_out"][DH * h:DH * (h + 1)] for h in
                                                 (0, 4, 1, 5, 2, 6, 3, 7)])

    def gate_and_value(w):
        t = by_tiles(w)
        return np.stack([t[:FK], t[FK:]], 1).reshape(2 * FK, P, -1)

    def in_halves(w):
        t = by_tiles(w)
        return np.ascontiguousarray(t.reshape(DK, P, 2, -1).transpose(0, 2, 1, 3)).reshape(2 * DK, P, -1)

    w2 = a["w_in_2"]
    small = [[(0, 2048, 2052), (32, 2052, 2056)]]
    feeds = {
        "w_in1": by_tiles(a["w_in"], in1),
        "w_fill1": by_tiles(a["w_in"], gate_pairs(1816)),
        "w_mix1": by_tiles(branch),
        "w_out1": by_tiles(a["w_out"]),
        "w_up1": gate_and_value(a["w_up"]),
        "w_down1": in_halves(a["w_down"]),
        "w_in2c": by_tiles(w2, straight(0, 12)),
        "w_in2z": by_tiles(w2, straight(1536, 4) + small),
        "w_fill2": by_tiles(w2, straight(2056, 12) + gate_pairs(2056 + 1536)),
        "w_mix2": by_tiles(np.concatenate([a["w_branch_a_2"], a["w_branch_b_2"]])),
        "w_out2": by_tiles(a["w_out_2"]),
        "w_up2": gate_and_value(a["w_up_2"]),
        "w_down2": in_halves(a["w_down_2"]),
        "x": np.ascontiguousarray(a["x"].T.reshape(DK, P, T).transpose(1, 0, 2)),
        "positions": a["positions"][None, :],
        "rel": a["rel_bias_2"],
        "cmp_w1": np.ascontiguousarray(np.concatenate([a["cmp_w1"].transpose(2, 0, 1, 3).reshape(
            DH, CMP_PIECES, -1)] * 2).transpose(1, 0, 2)),
        "cmp_w2": np.ascontiguousarray(a["cmp_w2"].transpose(1, 0, 2)),
        "pool_w": np.ascontiguousarray(a["pool_w"].transpose(1, 0, 2)),
        "consts": constants(),
    }
    prm = np.zeros((P, N_PARAM), np.float32)

    def put(name, value, rows_=slice(0, P)):
        at, n = PARAM[name]
        prm[rows_, at:at + n] = value

    put("gain", np.concatenate([by_columns(a[n]) for n in (
        "mix_norm_g", "ffn_norm_g", "norm_mix_w_2", "norm_ffn_w_2", "norm_final_w_2")], 1))
    twice = (slice(0, DH), slice(DH, P))
    for r in twice:
        put("q_gain", a["q_norm_g"][:, None], r)
        put("k_gain", a["k_norm_g"].T, r)
        put("pe", a["cmp_pe"].transpose(2, 0, 1).reshape(DH, 64), r)
    put("pool_scale", by_columns(a["pool_scale"]))

    def taps(w, b=None):
        rows_ = [by_columns(x) for x in w] + ([by_columns(b)] if b is not None else [])
        return np.stack(rows_, 2).reshape(P, -1)

    put("conv1", taps(a["conv_w"], a["conv_b"]))
    put("conv2", taps(a["conv_ffn_w_2"], a["conv_ffn_b_2"]))
    put("conv_qkv", taps(a["conv_qkv_w_2"]))
    put("gdn_gain", a["gdn_norm_w_2"][:, None])
    put("a_log", a["a_log_2"][:, None], slice(32, 32 + GH))
    put("dt_bias", a["dt_bias_2"][:, None], slice(32, 32 + GH))
    feeds["params"] = prm

    nc = bacc.Bacc("TRN2", target_bir_lowering=False, num_devices=1)
    t_in = {name: nc.dram_tensor("in_" + name, v.shape, mybir.dt.from_np(v.dtype), kind="ExternalInput").ap()
            for name, v in feeds.items()}
    out = nc.dram_tensor("out_t", (P, DK, T), F32, kind="ExternalOutput").ap()
    two_blocks(nc, t_in, out)
    r = run_bass_kernel_spmd(nc, [{"in_" + k: v for k, v in feeds.items()}], core_ids=[0])
    got = np.asarray(r.results[0]["out_t"]).reshape(P, DK, T)
    return got.transpose(2, 1, 0).reshape(1, T, D)
```
